# Optimizing a Trainium2 kernel written in Bass

```python
import math
import jax, jax.numpy as jnp
from jax import lax
import numpy as np

D_MODEL = 2048
BATCH = 1
SEQ = 256
DEPTH = 1

MEM_LEN = 256
EPS = 1e-6
SGU_HEADS = 8
SGU_DIM = 128
SGU_CHUNK = 128
SGU_WIDTH = SGU_HEADS * SGU_DIM
DIFF_HEADS = 8
DIFF_QK_DIM = 64
DIFF_V_DIM = 128
DIFF_WIDTH = DIFF_HEADS * DIFF_V_DIM
DIFF_QK_WIDTH = DIFF_HEADS * 2 * DIFF_QK_DIM
Q_BLOCK = 128
MIX_WIDTH = SGU_WIDTH + DIFF_WIDTH
IN_WIDTH = 2 * SGU_WIDTH + 2 * DIFF_QK_WIDTH + DIFF_WIDTH
REL_BUCKETS = 32
REL_MAX_DIST = 128
CROSS_HEADS = 4
CROSS_HEAD_DIM = D_MODEL // CROSS_HEADS
PEER_HEADS = 8
PEER_NKEYS = 128
PEER_N_EXPERTS = PEER_NKEYS * PEER_NKEYS
PEER_QDIM = 256
PEER_HALF = PEER_QDIM // 2
PEER_TOPK = 16
PEER_CHUNK = 128

kernel_name = "hybrid_sgu_diffattn_peer_layer"

def rmsnorm(x, g):
    xf = x.astype(jnp.float32)
    y = xf * lax.rsqrt(jnp.mean(xf * xf, axis=-1, keepdims=True) + EPS)
    return (y * g.astype(jnp.float32)).astype(x.dtype)

def t5_bucket(n):
    max_exact = REL_BUCKETS // 2
    nf = jnp.maximum(n, 1).astype(jnp.float32)
    large = max_exact + (jnp.log(nf / max_exact) / math.log(REL_MAX_DIST / max_exact)
                         * (REL_BUCKETS - max_exact)).astype(jnp.int32)
    large = jnp.minimum(large, REL_BUCKETS - 1)
    return jnp.where(n < max_exact, n, large)

def spatial_gating(u, v, norm_g, w_s, b_s):
    B, S = u.shape[0], u.shape[1]
    vn = rmsnorm(v, norm_g)
    vc = vn.reshape(B, S // SGU_CHUNK, SGU_CHUNK, SGU_HEADS, SGU_DIM)
    mask = jnp.tril(jnp.ones((SGU_CHUNK, SGU_CHUNK), w_s.dtype))
    mixed = jnp.einsum('hpq,bnqhc->bnphc', w_s * mask, vc) + b_s.T[None, None, :, :, None]
    return u * mixed.reshape(B, S, SGU_HEADS, SGU_DIM)

def diff_attention(q, k, v, lam, rel_bias):
    B, S = q.shape[0], q.shape[1]
    qh = q.transpose(0, 2, 3, 1, 4)
    kh = k.transpose(0, 2, 3, 1, 4)
    vh = v.transpose(0, 2, 1, 3)
    kpos = jnp.arange(S)
    scale = DIFF_QK_DIM ** -0.5

    def block(i):
        start = i * Q_BLOCK
        qb = lax.dynamic_slice_in_dim(qh, start, Q_BLOCK, axis=3)
        dist = (start + jnp.arange(Q_BLOCK))[:, None] - kpos[None, :]
        bias = rel_bias[t5_bucket(jnp.maximum(dist, 0))].transpose(2, 0, 1)
        logits = (jnp.einsum('bhcqd,bhckd->bhcqk', qb, kh).astype(jnp.float32) * scale
                  + bias[None, :, None].astype(jnp.float32))
        logits = jnp.where((dist >= 0)[None, None, None], logits, -jnp.inf)
        p = jax.nn.softmax(logits, axis=-1)
        a = p[:, :, 0] - lam * p[:, :, 1]
        return jnp.einsum('bhqk,bhkd->bhqd', a.astype(vh.dtype), vh)

    out = lax.map(block, jnp.arange(S // Q_BLOCK))
    return out.transpose(1, 0, 3, 2, 4).reshape(B, S, DIFF_HEADS, DIFF_V_DIM)

def cross_attention(h, memn, w_q, w_kv, qg, kg, w_o):
    B, S = h.shape[0], h.shape[1]
    M = memn.shape[1]
    q = rmsnorm((h @ w_q).reshape(B, S, CROSS_HEADS, CROSS_HEAD_DIM), qg)
    kv = (memn @ w_kv).reshape(B, M, 2, CROSS_HEADS, CROSS_HEAD_DIM)
    k = rmsnorm(kv[:, :, 0], kg)
    v = kv[:, :, 1]
    logits = jnp.einsum('bshd,bmhd->bhsm', q, k).astype(jnp.float32) * (CROSS_HEAD_DIM ** -0.5)
    p = jax.nn.softmax(logits, axis=-1)
    o = jnp.einsum('bhsm,bmhd->bshd', p.astype(v.dtype), v)
    return o.reshape(B, S, D_MODEL) @ w_o

def peer(h, w_q, keys, U, V):
    B, S, D = h.shape
    T = B * S
    hf = h.reshape(T, D)
    q = (hf @ w_q).reshape(T, PEER_HEADS, 2, PEER_HALF)
    sub = jnp.einsum('thcd,hckd->thck', q, keys).astype(jnp.float32)
    s, i = lax.top_k(sub, PEER_TOPK)
    cand_s = (s[:, :, 0, :, None] + s[:, :, 1, None, :]).reshape(T, PEER_HEADS, PEER_TOPK * PEER_TOPK)
    cand_i = (i[:, :, 0, :, None] * PEER_NKEYS + i[:, :, 1, None, :]).reshape(T, PEER_HEADS, PEER_TOPK * PEER_TOPK)
    top_s, pos = lax.top_k(cand_s, PEER_TOPK)
    idx = jnp.take_along_axis(cand_i, pos, axis=-1)
    g = jax.nn.softmax(top_s, axis=-1)
    nc = T // PEER_CHUNK

    def chunk(args):
        xc, ic, gc = args
        u = jnp.take(U, ic, axis=0)
        a = jnp.einsum('cd,chkd->chk', xc, u)
        coeff = (gc * jax.nn.gelu(a.astype(jnp.float32), approximate=False)).astype(xc.dtype)
        vv = jnp.take(V, ic, axis=0)
        return jnp.einsum('chk,chkd->cd', coeff, vv)

    out = lax.map(chunk, (hf.reshape(nc, PEER_CHUNK, D),
                          idx.reshape(nc, PEER_CHUNK, PEER_HEADS, PEER_TOPK),
                          g.reshape(nc, PEER_CHUNK, PEER_HEADS, PEER_TOPK)))
    return out.reshape(B, S, D)

def setup_inputs(seed: int = 0) -> dict:
    key = jax.random.key(seed)
    ks = jax.random.split(key, 32)
    f32 = jnp.float32
    L = DEPTH

    def nrm(k, shape, scale):
        return jax.random.normal(k, shape, f32) * scale

    def gain(k, shape):
        return 1.0 + 0.02 * jax.random.normal(k, shape, f32)

    return {
        "x": nrm(ks[0], (BATCH, SEQ, D_MODEL), 1.0),
        "mem": nrm(ks[1], (BATCH, MEM_LEN, D_MODEL), 1.0),
        "norm_mix_g": gain(ks[2], (L, D_MODEL)),
        "w_in": nrm(ks[3], (L, D_MODEL, IN_WIDTH), D_MODEL ** -0.5),
        "sgu_norm_g": gain(ks[4], (L, SGU_HEADS, SGU_DIM)),
        "sgu_w": nrm(ks[5], (L, SGU_HEADS, SGU_CHUNK, SGU_CHUNK), SGU_CHUNK ** -0.5),
        "sgu_b": gain(ks[6], (L, SGU_HEADS, SGU_CHUNK)),
        "q_norm_g": gain(ks[7], (L, DIFF_QK_DIM)),
        "k_norm_g": gain(ks[8], (L, DIFF_QK_DIM)),
        "lambda_q1": nrm(ks[9], (L, DIFF_QK_DIM), 0.1),
        "lambda_k1": nrm(ks[10], (L, DIFF_QK_DIM), 0.1),
        "lambda_q2": nrm(ks[11], (L, DIFF_QK_DIM), 0.1),
        "lambda_k2": nrm(ks[12], (L, DIFF_QK_DIM), 0.1),
        "diff_subln_g": gain(ks[13], (L, DIFF_V_DIM)),
        "rel_bias": nrm(ks[14], (REL_BUCKETS, DIFF_HEADS), 0.5),
        "w_out": nrm(ks[15], (L, MIX_WIDTH, D_MODEL), MIX_WIDTH ** -0.5),
        "norm_cross_g": gain(ks[16], (L, D_MODEL)),
        "norm_mem_g": gain(ks[17], (L, D_MODEL)),
        "w_cq": nrm(ks[18], (L, D_MODEL, D_MODEL), D_MODEL ** -0.5),
        "w_ckv": nrm(ks[19], (L, D_MODEL, 2 * D_MODEL), D_MODEL ** -0.5),
        "cq_norm_g": gain(ks[20], (L, CROSS_HEAD_DIM)),
        "ck_norm_g": gain(ks[21], (L, CROSS_HEAD_DIM)),
        "w_co": nrm(ks[22], (L, D_MODEL, D_MODEL), D_MODEL ** -0.5),
        "norm_ffn_g": gain(ks[23], (L, D_MODEL)),
        "peer_wq": nrm(ks[24], (L, D_MODEL, PEER_HEADS * PEER_QDIM), D_MODEL ** -0.5),
        "peer_keys": nrm(ks[25], (L, PEER_HEADS, 2, PEER_NKEYS, PEER_HALF), PEER_HALF ** -0.5),
        "peer_u": nrm(ks[26], (L, PEER_N_EXPERTS, D_MODEL), D_MODEL ** -0.5),
        "peer_v": nrm(ks[27], (L, PEER_N_EXPERTS, D_MODEL), 0.5),
    }

def reference(x, mem, norm_mix_g, w_in, sgu_norm_g, sgu_w, sgu_b, q_norm_g, k_norm_g,
              lambda_q1, lambda_k1, lambda_q2, lambda_k2, diff_subln_g, rel_bias, w_out,
              norm_cross_g, norm_mem_g, w_cq, w_ckv, cq_norm_g, ck_norm_g, w_co,
              norm_ffn_g, peer_wq, peer_keys, peer_u, peer_v):
    B, S, _ = x.shape
    h = x
    a0 = 2 * SGU_WIDTH
    a1 = a0 + DIFF_QK_WIDTH
    a2 = a1 + DIFF_QK_WIDTH
    for l in range(DEPTH):
        lam_init = 0.8 - 0.6 * math.exp(-0.3 * l)
        hn = rmsnorm(h, norm_mix_g[l])
        z = hn @ w_in[l]
        zs = jax.nn.gelu(z[..., :a0].astype(jnp.float32), approximate=False).astype(z.dtype)
        u = zs[..., :SGU_WIDTH].reshape(B, S, SGU_HEADS, SGU_DIM)
        v = zs[..., SGU_WIDTH:].reshape(B, S, SGU_HEADS, SGU_DIM)
        out_sgu = spatial_gating(u, v, sgu_norm_g[l], sgu_w[l], sgu_b[l])

        q = rmsnorm(z[..., a0:a1].reshape(B, S, DIFF_HEADS, 2, DIFF_QK_DIM), q_norm_g[l])
        k = rmsnorm(z[..., a1:a2].reshape(B, S, DIFF_HEADS, 2, DIFF_QK_DIM), k_norm_g[l])
        vd = z[..., a2:].reshape(B, S, DIFF_HEADS, DIFF_V_DIM)
        lam = (jnp.exp(jnp.sum(lambda_q1[l].astype(jnp.float32) * lambda_k1[l].astype(jnp.float32)))
               - jnp.exp(jnp.sum(lambda_q2[l].astype(jnp.float32) * lambda_k2[l].astype(jnp.float32)))
               + lam_init)
        out_diff = diff_attention(q, k, vd, lam, rel_bias)
        out_diff = rmsnorm(out_diff, diff_subln_g[l]) * (1.0 - lam_init)

        mix = jnp.concatenate([out_sgu.reshape(B, S, SGU_WIDTH),
                               out_diff.reshape(B, S, DIFF_WIDTH)], axis=-1) @ w_out[l]
        h = h + mix
        h = h + cross_attention(rmsnorm(h, norm_cross_g[l]), rmsnorm(mem, norm_mem_g[l]),
                                w_cq[l], w_ckv[l], cq_norm_g[l], ck_norm_g[l], w_co[l])
        h = h + peer(rmsnorm(h, norm_ffn_g[l]), peer_wq[l], peer_keys[l], peer_u[l], peer_v[l])
    return h


_drawn_inputs = setup_inputs


def setup_inputs(seed=0):
    import zlib

    import numpy as np

    out = dict(_drawn_inputs(seed))
    spreads = {}
    factors = {'sgu_norm_g': 3.752,
     'sgu_b': 2.957,
     'k_norm_g': 2.7,
     'lambda_q1': 2.961,
     'lambda_k1': 5.596,
     'diff_subln_g': 2.708,
     'norm_cross_g': 6.816,
     'norm_mem_g': 4.691,
     'cq_norm_g': 6.706,
     'ck_norm_g': 7.06,
     'norm_ffn_g': 8.0}
    for name, (base, spread) in spreads.items():
        noise = np.random.default_rng([zlib.crc32(name.encode()), seed]).standard_normal(out[name].shape)
        drawn = base * np.exp(spread * noise) if base else spread * noise
        out[name] = __import__('jax').numpy.asarray(drawn.astype(out[name].dtype))
    for name, factor in factors.items():
        out[name] = (out[name] * factor).astype(out[name].dtype)
    return out
```

```python
from contextlib import ExitStack

import concourse.bass as bass
from concourse import mybir

ALU = mybir.AluOpType
ACT = mybir.ActivationFunctionType
AX = mybir.AxisListType
F32 = mybir.dt.float32
F32R = mybir.dt.float32r
U32 = mybir.dt.uint32
ds = bass.ds

P = 128
D = 2048
KC = D // P
TT = 2
TOK = TT * P
EPS = 1e-6
NB = 512
SUB = 512
SLOTS = 4
LEAD = 2
SGU_H, SGU_D = 8, 128
DIFF_H, DIFF_D, DIFF_V = 8, 64, 128
CROSS_H = 4
CROSS_D = D // CROSS_H
CH = CROSS_D // P
PH, NK, TOPK = 8, 128, 16
HALF = NK // 2
LAM_INIT = 0.2
NEG = -1.0e30
LOW = -3.0e38

BLK = KC
N_IN, N_CKV, N_OUT, N_CQ, N_CO, N_PQ = 10, 8, 4, 4, 4, 4
U_IN = 0
U_CKV = U_IN + N_IN * BLK
U_OUT = U_CKV + N_CKV * BLK
U_CQ = U_OUT + N_OUT * BLK
U_CO = U_CQ + N_CQ * BLK
U_PQ = U_CO + N_CO * BLK
U_U = [U_PQ + N_PQ * BLK, 0]
U_V = [U_U[0] + HALF * 4, 0]
U_U[1] = U_V[0] + HALF * 4
U_V[1] = U_U[1] + HALF * 4
U_END = U_V[1] + HALF * 4
ITS = HALF // 2
PLAIN = 16
TPI = [TOK // (ITS - PLAIN), TOK // ITS]

MT = 0
Z = 8192
ZW = 5120
ZU, ZV, ZQ, ZK, ZVD = 0, 1024, 2048, 3072, 4096
MEM = 18432
SG, WS = 22528, 23552
KV = 18432
H = 26624
BI = 30720
CQ = 8192
OC = 12288
XN = 8192
KEYS = 30720
PQ = 18432
PQT = 22528
CAND, EQ = 22528, 24576
PK = 26624
G = 0
W = 16384
R = 0
SPITCH = 384


def at_least(eng, sem, value):
    if not isinstance(value, int) or value > 0:
        eng.wait_ge(sem, value)


class Steps:

    def __init__(self, eng, sem):
        self.eng, self.sem, self.n = eng, sem, 0

    def done(self, ins):
        ins.then_inc(self.sem, 1)
        self.n = self.n + 1

    def settle(self):
        self.eng.wait_ge(self.sem, self.n)

    def run(self, ins):
        self.done(ins)
        self.settle()


def hybrid_layer(nc, x, mem, w_in, w_ckv, w_out, w_cq, w_co, peer_wq, peer_u, peer_v, peer_keys, mix_g, mem_g,
                 cross_g, ffn_g, sgu_g, sgu_w, sgu_b, q_g, k_g, lambdas, subln_g, rel_bias, bucket_of, cq_g, ck_g, out):
    ctx = ExitStack()
    with ctx:
        def sb(name, shape, dt=F32):
            return ctx.enter_context(nc.sbuf_tensor(name, shape, dt))

        def sem(name):
            return ctx.enter_context(nc.semaphore(name))

        with nc.sbuf_tensor("m_hi", [P, KC, TOK], F32R) as m_hi, nc.sbuf_tensor("m_lo", [P, KC, TOK], F32R) as m_lo:
            pass
        arena = sb("arena", [P, 32768])
        with ExitStack() as late:
            def lsb(name, shape, dt=F32):
                return late.enter_context(nc.sbuf_tensor(name, shape, dt))
            hot1 = lsb("hot1", [P, 8, NK])
            hot2 = lsb("hot2", [P, 8, HALF])
            c_hi = lsb("c_hi", [P, 2, TOK], F32R)
            c_lo = lsb("c_lo", [P, 2, TOK], F32R)
            pickT = lsb("pickT", [P, 3, TOK])
        wk = sb("wk", [P, 3328])
        raw = sb("raw", [P, SLOTS, 2, SUB])
        w_hi = sb("w_hi", [P, SLOTS, SUB], F32R)
        w_lo = sb("w_lo", [P, SLOTS, SUB], F32R)
        a_hi = sb("a_hi", [P, KC, TOK], F32R)
        a_lo = sb("a_lo", [P, KC, TOK], F32R)
        ident = sb("ident", [P, P])
        iota = sb("iota", [P, NK])
        gains = sb("gains", [P, 5, KC])
        sgb = sb("sgb", [P, SGU_H])
        qkg = sb("qkg", [P, 2])
        subg = sb("subg", [P, DIFF_V])
        eps = sb("eps", [P, 1])
        ss = sb("ss", [P, 8])
        rs = sb("rs", [P, 8])
        st = sb("st", [P, 2, 64])
        lam = sb("lam", [P, 8])
        sm = sb("sm", [P, 2, 16])

        def ar(col, *dims):
            n = 1
            for d in dims:
                n *= d
            v = arena[:, col:col + n]
            if len(dims) == 2:
                return v.rearrange("p (a b) -> p a b", b=dims[1])
            if len(dims) == 3:
                return v.rearrange("p (a b c) -> p a b c", b=dims[1], c=dims[2])
            return v

        z = ar(Z, TT, ZW)
        xh = ar(H, TT, D)
        memr = ar(MEM, TT, D)
        kv = ar(KV, TT, 2 * D)
        bias = ar(BI, DIFF_H, TOK)
        sgg, wst = ar(SG, SGU_H * SGU_D), ar(WS, SGU_H, P)
        kT, qT = ar(MT, KC, TOK), ar(MT + KC * TOK, KC, TOK)
        cq, oc, xn = ar(CQ, TT, D), ar(OC, TT, D), ar(XN, TT, D)
        keysT, pq, sc = ar(KEYS, 2 * PH, NK), ar(PQ, TT, D), ar(PQ, TT, 2 * PH, NK)
        pqT = ar(PQT, KC, TOK)
        cand, eq = ar(CAND, PH, TOPK, TOPK), ar(EQ, PH, TOPK, TOPK)
        res = ar(R, TT, D)
        pk_top, pk_idxf = ar(PK, TT, 2 * PH, TOPK), ar(PK + 1024, TT, 2 * PH, TOPK)
        pk_idx = ar(PK + 512, TT, 2 * PH, TOPK).bitcast(U32)

        def pk(col, m):
            return arena[:, PK + col + P * m:PK + col + P * (m + 1)]

        def pk_gate(m):
            return pk(3328, m)

        sq = wk[:, 0:2048]
        qk_st = wk[:, 0:512].rearrange("p (a b) -> p a b", a=4)
        logit = wk[:, 512:1536].rearrange("p (a c k) -> p a c k", a=2, c=2)
        aT = wk[:, 1536:1920].rearrange("p (a b) -> p a b", a=3)
        qz = wk[:, 2048:2560].rearrange("p (c t) -> p c t", c=2)
        kz = wk[:, 2560:2816]
        lamv = wk[:, 2816:3072].rearrange("p (a b) -> p a b", a=4)
        cp = wk[:, 0:1024].rearrange("p (b t m) -> p b t m", b=2, t=2)
        cpT = wk[:, 1024:2048].rearrange("p (b n q) -> p b n q", b=2, q=P)
        onehot = wk[0:32, 0:SPITCH]
        relb = wk[0:32, 400:408]
        toep = wk[0:8, 512:512 + SPITCH]

        ps = [ctx.enter_context(nc.psum_tensor(f"ps{i}", [P, 512], F32)) for i in range(8)]

        raw_in = [sem(f"raw_in{s}") for s in range(SLOTS)]
        hi_done = sem("hi_done")
        lo_done = sem("lo_done")
        used = sem("used")
        evac = sem("evac")
        added = sem("added")
        turned = sem("turned")
        turn_hi = sem("turn_hi")
        turn_out = sem("turn_out")
        sums = sem("sums")
        rstds = sem("rstds")
        x_in, mem_in, small_in = sem("x_in"), sem("mem_in"), sem("small_in")
        onehot_in = sem("onehot_in")
        consts = sem("consts")
        masked = sem("masked")
        toep_ps, toep_sb, toep_out, bias_in = sem("toep_ps"), sem("toep_sb"), sem("toep_out"), sem("bias_in")
        dve_step, act_step, pool_step = sem("dve_step"), sem("act_step"), sem("pool_step")
        grp_sq, grp_root = sem("grp_sq"), sem("grp_root")
        lam_sum, lam_exp = sem("lam_sum"), sem("lam_exp")
        vn_ready, sgu_ps = sem("vn_ready"), sem("sgu_ps")
        qk_scaled, qk_turned, qk_ready = sem("qk_scaled"), sem("qk_turned"), sem("qk_ready")
        score_ps, logit_ready, prob_ready = sem("score_ps"), sem("logit_ready"), sem("prob_ready")
        a_ready, aT_ps, aT_ready = sem("a_ready"), sem("aT_ps"), sem("aT_ready")
        o_ps, o_out = sem("o_ps"), sem("o_out")
        mix_ready = sem("mix_ready")
        kc_ready, qc_ready = sem("kc_ready"), sem("qc_ready")
        x_score, x_max, x_prob, x_rsum = sem("x_score"), sem("x_max"), sem("x_prob"), sem("x_rsum")
        x_pT, x_pT_out, x_o, x_o_out = sem("x_pT"), sem("x_pT_out"), sem("x_o"), sem("x_o_out")
        xn_ready = sem("xn_ready")
        keys_in, h_saved = sem("keys_in"), sem("h_saved")
        sc_ps, sc_out = sem("sc_ps"), sem("sc_out")
        gate_in, gate_exp, picks_ready = sem("gate_in"), sem("gate_exp"), sem("picks_ready")
        gelu_done = sem("gelu_done")
        hot_ready, gate_ps, gate_out = sem("hot_ready"), sem("gate_ps"), sem("gate_out")
        coef, coef_hi, coef_ready = sem("coef"), sem("coef_hi"), sem("coef_ready")
        acc_out, res_in, stored = sem("acc_out"), sem("res_in"), sem("stored")

        scratch = nc.dram_tensor("toeplitz_rows", [DIFF_H, SPITCH], F32, kind="Internal").ap()
        shifted = nc.dram_tensor("toeplitz_copies", [DIFF_H, P, SPITCH], F32, kind="Internal").ap()
        x_t = x.rearrange("(t p) d -> p t d", p=P)
        mem_t = mem.rearrange("(t p) d -> p t d", p=P)
        out_t = out.rearrange("(t p) d -> p t d", p=P)

        block = ctx.enter_context(nc.Block())

        @block.sync
        def _(sp):
            def tile(u, src, row):
                s = (u // 2) % SLOTS
                if u >= 2 * SLOTS:
                    sp.wait_ge(lo_done, u - 2 * SLOTS + 2)
                sp.dma_start(raw[:, s], src[row].rearrange("p (a n) -> p a n", a=2)).then_inc(raw_in[s], 16)

            def tiles(u0, src, row0, count):
                with sp.Fori(0, count // SLOTS) as i:
                    for s in range(SLOTS):
                        sp.wait_ge(lo_done, i * (2 * SLOTS) + (u0 + 2 * s - 2 * SLOTS + 2))
                        sp.dma_start(raw[:, s], src[ds(i * SLOTS + (row0 + s), 1)]
                                     .rearrange("o p (a n) -> p (o a) n", a=2)).then_inc(raw_in[s], 16)

            sp.dma_start(xh, x_t).then_inc(x_in, 16)
            for s in range(SLOTS):
                tile(2 * s, w_in, s)
            sp.dma_start(onehot, bucket_of).then_inc(onehot_in, 16)
            sp.dma_start(relb, rel_bias).then_inc(onehot_in, 16)
            for col, g in enumerate((mix_g, mem_g, cross_g, ffn_g)):
                sp.dma_start(gains[:, col, :], g).then_inc(small_in, 16)
            sp.dma_start(gains[:, 4, 0:4], cq_g).then_inc(small_in, 16)
            sp.dma_start(gains[:, 4, 4:8], ck_g).then_inc(small_in, 16)
            sp.dma_start(sgb[:], sgu_b).then_inc(small_in, 16)
            for c in range(2):
                sp.dma_start(qkg[64 * c:64 * c + 64, 0:1], q_g).then_inc(small_in, 16)
                sp.dma_start(qkg[64 * c:64 * c + 64, 1:2], k_g).then_inc(small_in, 16)
            sp.dma_start(subg[:], subln_g.partition_broadcast(P)).then_inc(small_in, 16)
            sp.dma_start(lamv, lambdas.partition_broadcast(P)).then_inc(small_in, 16)
            sp.dma_start(sgg, sgu_g.partition_broadcast(P)).then_inc(small_in, 16)
            sp.dma_start(wst, sgu_w).then_inc(small_in, 16)
            sp.dma_start(memr, mem_t).then_inc(mem_in, 16)
            sp.wait_ge(toep_sb, 1)
            sp.dma_start(scratch, toep).then_inc(toep_out, 16)
            sp.wait_ge(toep_out, 16)
            sp.dma_start(shifted, scratch.unsqueeze(1).to_broadcast([DIFF_H, P, SPITCH])).then_inc(toep_out, 16)
            sp.wait_ge(toep_out, 32)
            sp.dma_start(bias, bass.AP(tensor=shifted.tensor, offset=P - 1,
                                       ap=[[SPITCH - 1, P], [P * SPITCH, DIFF_H], [1, TOK]])).then_inc(bias_in, 16)
            tiles(2 * SLOTS, w_in, SLOTS, N_IN * BLK // 2 - SLOTS)
            tiles(U_CKV, w_ckv, 0, N_CKV * BLK // 2)
            tiles(U_OUT, w_out, 0, N_OUT * BLK // 2)
            sp.wait_ge(logit_ready, 2 * DIFF_H)
            sp.dma_start(keysT, peer_keys).then_inc(keys_in, 16)
            tiles(U_CQ, w_cq, 0, N_CQ * BLK // 2)
            tiles(U_CO, w_co, 0, N_CO * BLK // 2)
            tiles(U_PQ, peer_wq, 0, N_PQ * BLK // 2)
            for half in range(2):
                tiles(U_U[half], peer_u, half * HALF * 2, HALF * 2)
                tiles(U_V[half], peer_v, half * HALF * 2, HALF * 2)

        @block.gpsimd
        def _(pool):
            g = Steps(pool, pool_step)
            g.run(pool.memset(ident[:], 0.0))
            pool.affine_select(out=ident[:], in_=ident[:], compare_op=ALU.not_equal, fill=1.0, base=0,
                               pattern=[[-1, P]], channel_multiplier=1).then_inc(consts, 1)
            pool.iota(iota[:], pattern=[[1, NK]], base=0, channel_multiplier=0,
                      allow_small_or_imprecise_dtypes=True).then_inc(consts, 1)
            pool.memset(eps[:], EPS).then_inc(consts, 1)
            pool.memset(qz, 0.0).then_inc(consts, 1)
            pool.wait_ge(small_in, 16 * 15)
            pool.affine_select(out=wst, in_=wst, compare_op=ALU.is_ge, fill=0.0, base=0,
                               pattern=[[0, SGU_H], [1, P]], channel_multiplier=-1).then_inc(masked, 1)
            pool.wait_ge(bias_in, 16)
            pool.affine_select(out=bias, in_=bias, compare_op=ALU.is_ge, fill=NEG, base=P,
                               pattern=[[0, DIFF_H], [-1, TOK]], channel_multiplier=1).then_inc(masked, 1)
            pool.wait_ge(added, N_OUT + N_CO)
            pool.dma_start(out_t, xh).then_inc(h_saved, 16)
            pool.wait_ge(h_saved, 16)
            for half in range(2):
                pool.wait_ge(coef_ready, half * HALF + 16)
                pool.dma_start(res, out_t).then_inc(res_in, 16)
                for m in range(TT):
                    for s in range(4):
                        pool.wait_ge(acc_out, half * 8 + m * 4 + s + 1)
                        pool.dma_start(out_t[:, m, s * NB:(s + 1) * NB], res[:, m, s * NB:(s + 1) * NB]).then_inc(stored, 16)
                pool.wait_ge(stored, 128 * (half + 1))

        @block.scalar
        def _(act):
            st_ = Steps(act, act_step)

            def hi(u):
                act.wait_ge(raw_in[u % 8 // 2], 16 * (u // 8 + 1))
                at_least(act, used, u - 3)
                act.activation(w_hi[:, u % 4], raw[:, u % 8 // 2, u % 2], ACT.Copy).then_inc(hi_done, 1)

            def hi_loop(i, per, u0, r):
                s = (r % 8) // 2
                act.wait_ge(raw_in[s], i * (2 * per) + 16 * ((u0 + r) // 8 + 1))
                act.wait_ge(used, i * per + (u0 + r - 3))
                act.activation(w_hi[:, r % 4], raw[:, s, r % 2], ACT.Copy).then_inc(hi_done, 1)

            def copy_block(u_end, parity, dst, scale, func=ACT.Copy):
                act.wait_ge(used, u_end)
                for m in range(TT):
                    ins = act.activation(dst(m), ps[2 * parity + m][:], func, scale=scale(m))
                ins.then_inc(evac, 1)

            def turn_parts(n, gain):
                dst = m_hi if n == 1 else a_hi
                for j in range(KC // 2):
                    act.wait_ge(turned, 8 * n + j + 1)
                    for kk in range(2):
                        k = 2 * j + kk
                        src = ps[4 + j % 4][:, kk * TOK:(kk + 1) * TOK]
                        ins = act.activation(dst[:, k, :], src, ACT.Copy,
                                             scale=1.0 if gain is None else gains[:, gain, k:k + 1])
                    ins.then_inc(turn_hi, 1)

            def turn_whole(n, dst, gain):
                for j in range(KC // 2):
                    act.wait_ge(turned, 8 * n + j + 1)
                    for kk in range(2):
                        k = 2 * j + kk
                        ins = act.activation(dst[:, k, :], ps[4 + j % 4][:, kk * TOK:(kk + 1) * TOK], ACT.Copy,
                                             scale=1.0 if gain is None else gain(k))
                    ins.then_inc(turn_out, 1)

            def mean_square(n, src, junk):
                for m in range(TT):
                    st_.run(act.activation(junk, src[:, m], ACT.Square, accum_out=ss[:, 2 * n + m:2 * n + m + 1]))
                act.activation(rs[:, 2 * n:2 * n + 2], ss[:, 2 * n:2 * n + 2], ACT.Sqrt, bias=eps[:, 0:1],
                               scale=1.0 / D).then_inc(sums, 1)

            hi(0)
            hi(1)
            act.wait_ge(small_in, 16 * 15)
            act.wait_ge(consts, 4)
            turn_parts(0, 0)
            act.wait_ge(x_in, 16)
            mean_square(0, xh, z[:, 0, 0:D])
            act.wait_ge(toep_ps, 1)
            act.activation(toep, ps[3][0:8, 0:SPITCH], ACT.Copy).then_inc(toep_sb, 1)
            act.wait_ge(rstds, 1)
            for b in range(4):
                for r in range(BLK):
                    hi(U_IN + b * BLK + r + LEAD)
                copy_block(U_IN + (b + 1) * BLK, b % 2, lambda m: z[:, m, b * NB:(b + 1) * NB], lambda m: rs[:, m:m + 1], ACT.Gelu)
            with act.Fori(2, N_IN // 2) as i:
                for r in range(2 * BLK):
                    hi_loop(i, 2 * BLK, U_IN, r + LEAD)
                    if r % BLK == BLK - 1:
                        b = r // BLK
                        copy_block(i * (2 * BLK) + (U_IN + (b + 1) * BLK), b, lambda m: z[:, m, ds(i * (2 * NB) + b * NB, NB)],
                                   lambda m: rs[:, m:m + 1])
            act.wait_ge(mem_in, 16)
            turn_parts(1, 1)
            mean_square(1, memr, ar(MEM + 6144, D))
            act.wait_ge(lam_sum, 2)
            act.activation(lam[:, 2:4], lam[:, 0:2], ACT.Exp).then_inc(lam_exp, 1)
            act.wait_ge(grp_sq, 1)
            act.activation(st[:, 0, 0:16], st[:, 0, 0:16], ACT.Sqrt, bias=eps[:, 0:1], scale=1.0 / SGU_D).then_inc(grp_root, 1)
            act.wait_ge(grp_sq, 2)
            act.activation(st[:, 1, :], st[:, 1, :], ACT.Sqrt, bias=eps[:, 0:1], scale=1.0 / DIFF_D).then_inc(grp_root, 1)
            with act.Fori(0, DIFF_H) as i:
                for r in range(BLK):
                    hi_loop(i, BLK, U_CKV, r + LEAD)
                    if r == 0:
                        act.wait_ge(qk_turned, i + 1)
                        for c in range(2):
                            rows = slice(64 * c, 64 * c + 64)
                            act.activation(qz[rows, c], ps[2][rows, 0:TOK], ACT.Copy, scale=qkg[rows, 0:1])
                        act.activation(kz, ps[2][:, TOK:2 * TOK], ACT.Copy, scale=qkg[:, 1:2]).then_inc(qk_ready, 1)
                    if r == 5:
                        for qt in range(TT):
                            kn = P * (qt + 1)
                            act.wait_ge(logit_ready, i * 2 + (qt + 1))
                            for c in range(2):
                                ins = act.activation(logit[:, qt, c, 0:kn], logit[:, qt, c, 0:kn], ACT.Exp,
                                                     bias=sm[:, 0, 2 * qt + c:2 * qt + c + 1],
                                                     accum_out=sm[:, 1, 2 * qt + c:2 * qt + c + 1])
                            ins.then_inc(prob_ready, 1)
                    if r == 11:
                        act.wait_ge(aT_ps, i + 1)
                        act.activation(aT, ps[5][:, 0:3 * P].rearrange("p (a b) -> p a b", a=3), ACT.Copy).then_inc(aT_ready, 1)
                    if r == 14:
                        act.wait_ge(o_ps, i + 1)
                        act.activation(z[:, :, ds(i * DIFF_V + ZQ, DIFF_V)],
                                       ps[6][:, 0:TOK].rearrange("p (m d) -> p m d", m=TT), ACT.Copy).then_inc(o_out, 1)
                copy_block(i * BLK + (U_CKV + BLK), 0, lambda m: kv[:, m, ds(i * NB, NB)], lambda m: rs[:, 2 + m:3 + m])
            act.wait_ge(grp_sq, 3)
            act.activation(st[:, 0, 0:16], st[:, 0, 0:16], ACT.Sqrt, bias=eps[:, 0:1], scale=1.0 / DIFF_V).then_inc(grp_root, 1)
            turn_parts(2, None)
            with act.Fori(0, N_OUT // 2) as i:
                for r in range(2 * BLK):
                    hi_loop(i, 2 * BLK, U_OUT, r + LEAD)
            turn_parts(3, 2)
            mean_square(2, xh, ar(OC, D))
            act.wait_ge(rstds, 3)
            with act.Fori(0, N_CQ // 2) as i:
                for r in range(2 * BLK):
                    hi_loop(i, 2 * BLK, U_CQ, r + LEAD)
                    if r % BLK == BLK - 1:
                        b = r // BLK
                        copy_block(i * (2 * BLK) + (U_CQ + (b + 1) * BLK), b,
                                   lambda m: cq[:, m, ds(i * (2 * NB) + b * NB, NB)], lambda m: rs[:, 4 + m:5 + m])
            for n in range(2):
                act.wait_ge(grp_sq, 4 + n)
                act.activation(st[:, 0, 8 * n:8 * n + 8], st[:, 0, 8 * n:8 * n + 8], ACT.Sqrt, bias=eps[:, 0:1],
                               scale=1.0 / CROSS_D).then_inc(grp_root, 1)
            turn_whole(4, kT, lambda k: gains[:, 4, 4 + k % CH:5 + k % CH])
            turn_whole(5, qT, lambda k: gains[:, 4, k % CH:k % CH + 1])
            for h in range(CROSS_H):
                act.wait_ge(x_max, h + 1)
                for qt in range(TT):
                    n = 2 * h + qt
                    ins = act.activation(cp[:, h % 2, qt], ps[h % 2][:, qt * TOK:(qt + 1) * TOK], ACT.Exp,
                                         bias=sm[:, 0, n:n + 1], scale=CROSS_D ** -0.5, accum_out=sm[:, 1, n:n + 1])
                ins.then_inc(x_prob, 1)
                act.wait_ge(x_pT, h + 1)
                act.activation(cpT[:, h % 2], ps[2 + h % 2][:].rearrange("p (n q) -> p n q", q=P), ACT.Copy).then_inc(x_pT_out, 1)
            turn_parts(6, None)
            with act.Fori(0, N_CO // 2) as i:
                for r in range(2 * BLK):
                    hi_loop(i, 2 * BLK, U_CO, r + LEAD)
            act.wait_ge(added, N_OUT + N_CO)
            mean_square(3, xh, ar(OC, D))
            turn_parts(7, 3)
            with act.Fori(0, N_PQ // 2) as i:
                for r in range(2 * BLK):
                    hi_loop(i, 2 * BLK, U_PQ, r + LEAD)
                    if r % BLK == BLK - 1:
                        b = r // BLK
                        copy_block(i * (2 * BLK) + (U_PQ + (b + 1) * BLK), b,
                                   lambda m: pq[:, m, ds(i * (2 * NB) + b * NB, NB)], lambda m: 1.0)
            turn_whole(8, pqT, None)
            for n in range(8):
                act.wait_ge(sc_ps, n + 1)
                act.activation(sc[:, n // 4, 4 * (n % 4):4 * (n % 4) + 4], ps[n % 4][:].rearrange("p (a k) -> p a k", k=NK),
                               ACT.Copy).then_inc(sc_out, 1)

            def activations(i, half, it0, tokens):
                def gelu(jl):
                    act.wait_ge(used, i * 8 + (U_U[half] + 8 * it0 + 4 * (jl + 1)))
                    if half:
                        act.wait_ge(stored, 128)
                    act.activation(arena[:, ds(i * (2 * TOK) + (G + (2 * it0 + jl) * TOK), TOK)], ps[jl][:, 0:TOK],
                                   ACT.Gelu).then_inc(gelu_done, 1)

                def gates(g, tok0):
                    act.wait_ge(gate_ps, i * tokens + (8 + half * TOK + tok0 + 8))
                    act.activation(arena[:, ds(i * (tokens * HALF) + (W + tok0 * HALF), 8 * HALF)], ps[2 + g][:],
                                   ACT.Copy).then_inc(gate_out, 1)

                for r in range(8):
                    hi_loop(i, 8, U_U[half] + 8 * it0, r + LEAD)
                    if r == 5:
                        gelu(0)
                        if tokens == 16:
                            gates(0, 0)
                gelu(1)
                if tokens:
                    gates(tokens // 16, tokens - 8)

            def coefficient_hi(half, j, parity):
                act.wait_ge(coef, half * HALF + j + 1)
                act.wait_ge(used, U_V[half] + 4 * (j - 1))
                act.activation(c_hi[:, parity], arena[:, ds(j * TOK + G, TOK)], ACT.Copy).then_inc(coef_hi, 1)

            for half in range(2):
                if half == 0:
                    with act.Fori(0, PLAIN) as i:
                        activations(i, 0, 0, 0)
                    for m in range(TT):
                        act.wait_ge(gate_in, m + 1)
                        act.activation(pk_gate(m), pk_gate(m), ACT.Exp).then_inc(gate_exp, 1)
                    act.wait_ge(h_saved, 16)
                    with act.Fori(0, ITS - PLAIN) as i:
                        activations(i, 0, PLAIN, TPI[0])
                else:
                    with act.Fori(0, ITS) as i:
                        activations(i, 1, 0, TPI[1])
                coefficient_hi(half, 0, 0)
                with act.Fori(0, ITS - 1) as i:
                    for r in range(8):
                        hi_loop(i, 8, U_V[half], r + LEAD)
                        if r == 1:
                            act.wait_ge(coef, i * 2 + (half * HALF + 2))
                            act.wait_ge(used, i * 8 + U_V[half])
                            act.activation(c_hi[:, 1], arena[:, ds(i * (2 * TOK) + (G + TOK), TOK)], ACT.Copy).then_inc(coef_hi, 1)
                        if r == 5:
                            act.wait_ge(coef, i * 2 + (half * HALF + 3))
                            act.wait_ge(used, i * 8 + (U_V[half] + 4))
                            act.activation(c_hi[:, 0], arena[:, ds(i * (2 * TOK) + (G + 2 * TOK), TOK)], ACT.Copy).then_inc(coef_hi, 1)
                for r in range(8):
                    u = U_V[half] + 8 * (ITS - 1) + r + LEAD
                    if u < U_END:
                        hi(u)
                    if r == 1:
                        coefficient_hi(half, HALF - 1, 1)

        @block.vector
        def _(dve):
            st_ = Steps(dve, dve_step)
            TTT, TS, STT = dve.tensor_tensor, dve.tensor_scalar, dve.scalar_tensor_tensor

            def lo(u):
                if u < U_END:
                    dve.wait_ge(hi_done, u + 1)
                    TTT(w_lo[:, u % 4], raw[:, u % 8 // 2, u % 2], w_hi[:, u % 4].bitcast(F32), ALU.subtract).then_inc(lo_done, 1)

            def lo_loop(i, per, u0, r):
                dve.wait_ge(hi_done, i * per + (u0 + r + 1))
                TTT(w_lo[:, r % 4], raw[:, (r % 8) // 2, r % 2], w_hi[:, r % 4].bitcast(F32), ALU.subtract).then_inc(lo_done, 1)

            def turn_rest(n, n_hi, gain):
                dhi, dlo = (m_hi, m_lo) if n == 1 else (a_hi, a_lo)
                for j in range(KC // 2):
                    dve.wait_ge(turn_hi, 8 * n_hi + j + 1)
                    src = ps[4 + j % 4][:]
                    if gain is None:
                        TTT(dlo[:, 2 * j:2 * j + 2, :], src.rearrange("p (a b) -> p a b", a=2),
                            dhi[:, 2 * j:2 * j + 2, :].bitcast(F32), ALU.subtract).then_inc(turn_out, 1)
                        continue
                    for kk in range(2):
                        k = 2 * j + kk
                        ins = STT(dlo[:, k, :], src[:, kk * TOK:(kk + 1) * TOK], gains[:, gain, k:k + 1],
                                  dhi[:, k, :].bitcast(F32), ALU.mult, ALU.subtract)
                    ins.then_inc(turn_out, 1)

            def reciprocal_rms(n):
                dve.wait_ge(sums, n + 1)
                dve.reciprocal(rs[:, 2 * n:2 * n + 2], rs[:, 2 * n:2 * n + 2]).then_inc(rstds, 1)

            def spread(v, n):
                return v.unsqueeze(2).to_broadcast([P, v.shape[1], n])

            lo(0)
            lo(1)
            turn_rest(0, 0, 0)
            reciprocal_rms(0)
            with dve.Fori(0, N_IN // 2) as i:
                for r in range(2 * BLK):
                    lo_loop(i, 2 * BLK, U_IN, r + LEAD)
            turn_rest(1, 1, 1)
            reciprocal_rms(1)
            for c in range(2):
                dve.tensor_tensor_reduce(lamv[:, 2 * c], lamv[:, 2 * c], lamv[:, 2 * c + 1], 1.0, 0.0,
                                         ALU.mult, ALU.add, lam[:, c:c + 1]).then_inc(lam_sum, 1)
            st_.run(TS(subg[:], subg[:], 1.0 - LAM_INIT, None, ALU.mult))
            dve.wait_ge(lam_exp, 1)
            st_.run(TS(lam[:, 5:6], lam[:, 3:4], LAM_INIT, None, ALU.subtract))
            st_.run(TTT(lam[:, 4:5], lam[:, 5:6], lam[:, 2:3], ALU.subtract))
            dve.wait_ge(evac, N_IN)
            dve.wait_ge(toep_out, 16)
            zv = z[:, :, ZV:ZV + 1024]
            st_.run(TTT(sq.rearrange("p (m c) -> p m c", m=2), zv, zv, ALU.mult))
            dve.tensor_reduce(st[:, 0, 0:16], sq.rearrange("p (g c) -> p g c", c=SGU_D), AX.X, ALU.add).then_inc(grp_sq, 1)
            dve.wait_ge(grp_root, 1)
            st_.run(dve.reciprocal(st[:, 0, 0:16], st[:, 0, 0:16]))
            for m in range(TT):
                v = zv[:, m].rearrange("p (g c) -> p g c", c=SGU_D)
                st_.run(TTT(v, v, spread(st[:, 0, 8 * m:8 * m + 8], SGU_D), ALU.mult))
                TTT(zv[:, m], zv[:, m], sgg, ALU.mult).then_inc(vn_ready, 1)
            for m in range(TT):
                qk = z[:, m, ZQ:ZQ + 2048]
                st_.run(TTT(sq, qk, qk, ALU.mult))
                ins = dve.tensor_reduce(st[:, 1, 32 * m:32 * m + 32], sq.rearrange("p (g c) -> p g c", c=DIFF_D), AX.X, ALU.add)
                if m == 0:
                    st_.run(ins)
            ins.then_inc(grp_sq, 1)
            dve.wait_ge(grp_root, 2)
            st_.run(dve.reciprocal(st[:, 1, :], st[:, 1, :]))
            for n in range(4):
                dve.wait_ge(sgu_ps, n + 1)
                for hh in range(4):
                    m, h = n // 2, 4 * (n % 2) + hh
                    u_ = z[:, m, ZU + h * SGU_D:ZU + (h + 1) * SGU_D]
                    st_.done(STT(u_, ps[4 + n][:, hh * P:(hh + 1) * P], sgb[:, h:h + 1], u_, ALU.add, ALU.mult))
            st_.settle()
            dve.wait_ge(masked, 2)
            stg = st[:, 1, :].rearrange("p (m g) -> p m g", m=TT)
            n0 = st_.n
            with dve.Fori(0, DIFF_H) as i:
                st_.n = i * 8 + n0
                for t in range(2):
                    src = z[:, :, ds(i * P + (ZQ + 1024 * t), P)].rearrange("p m (c d) -> p m c d", c=2)
                    ins = TTT(qk_st[:, 2 * t:2 * t + 2, :].rearrange("p m (c d) -> p m c d", c=2), src,
                              stg[:, :, ds(i * 2 + 16 * t, 2)].unsqueeze(3).to_broadcast([P, TT, 2, DIFF_D]), ALU.mult)
                ins.then_inc(qk_scaled, 1)
                for r in range(BLK):
                    lo_loop(i, BLK, U_CKV, r + LEAD)
                    if r == 4:
                        for qt in range(TT):
                            kn = P * (qt + 1)
                            dve.wait_ge(score_ps, i * 2 + (qt + 1))
                            st_.run(STT(logit[:, qt, :, 0:kn], ps[3 + qt][:, 0:2 * kn].rearrange("p (c k) -> p c k", c=2),
                                        DIFF_D ** -0.5, bias[:, ds(i, 1), TOK - kn:TOK].to_broadcast([P, 2, kn]),
                                        ALU.mult, ALU.add))
                            dve.tensor_reduce(sm[:, 0, 2 * qt:2 * qt + 2], logit[:, qt, :, 0:kn], AX.X, ALU.max,
                                              negate=True).then_inc(logit_ready, 1)
                    if r == 8:
                        for qt in range(TT):
                            kn = P * (qt + 1)
                            s_ = sm[:, 1, 2 * qt:2 * qt + 2]
                            dve.wait_ge(prob_ready, i * 2 + (qt + 1))
                            st_.run(dve.reciprocal(s_, s_))
                            st_.done(TTT(s_[:, 1:2], s_[:, 1:2], lam[:, 4:5], ALU.mult))
                            st_.run(TS(logit[:, qt, 0, 0:kn], logit[:, qt, 0, 0:kn], s_[:, 0:1], None, ALU.mult))
                            STT(logit[:, qt, 0, 0:kn], logit[:, qt, 1, 0:kn], s_[:, 1:2], logit[:, qt, 0, 0:kn],
                                ALU.mult, ALU.add).then_inc(a_ready, 1)
            st_.n = n0 + 8 * DIFF_H
            dve.wait_ge(o_out, DIFF_H)
            zd = z[:, :, ZQ:ZQ + 1024]
            st_.run(TTT(sq.rearrange("p (m c) -> p m c", m=2), zd, zd, ALU.mult))
            dve.tensor_reduce(st[:, 0, 0:16], sq.rearrange("p (g c) -> p g c", c=DIFF_V), AX.X, ALU.add).then_inc(grp_sq, 1)
            dve.wait_ge(grp_root, 3)
            st_.run(dve.reciprocal(st[:, 0, 0:16], st[:, 0, 0:16]))
            for m in range(TT):
                v = zd[:, m].rearrange("p (g c) -> p g c", c=DIFF_V)
                st_.run(TTT(v, v, spread(st[:, 0, 8 * m:8 * m + 8], DIFF_V), ALU.mult))
                TTT(v, v, subg[:].unsqueeze(1).to_broadcast([P, 8, DIFF_V]), ALU.mult).then_inc(mix_ready, 1)
            turn_rest(2, 2, None)

            def add_blocks(u0):
                with dve.Fori(0, 2) as i:
                    for r in range(2 * BLK):
                        lo_loop(i, 2 * BLK, u0, r + LEAD)
                        if r % BLK == BLK - 1:
                            b = r // BLK
                            dve.wait_ge(used, i * (2 * BLK) + (u0 + (b + 1) * BLK))
                            for m in range(TT):
                                v = xh[:, m, ds(i * (2 * NB) + b * NB, NB)]
                                ins = TTT(v, ps[2 * b + m][:], v, ALU.add)
                            ins.then_inc(added, 1)

            add_blocks(U_OUT)
            turn_rest(3, 3, 2)
            reciprocal_rms(2)
            with dve.Fori(0, N_CQ // 2) as i:
                for r in range(2 * BLK):
                    lo_loop(i, 2 * BLK, U_CQ, r + LEAD)
            dve.wait_ge(evac, N_IN + N_CKV + N_CQ)
            for n, v in enumerate((kv, cq)):
                for m in range(TT):
                    st_.run(TTT(sq, v[:, m, 0:D], v[:, m, 0:D], ALU.mult))
                    ins = dve.tensor_reduce(st[:, 0, 8 * n + 4 * m:8 * n + 4 * m + 4],
                                            sq.rearrange("p (h c) -> p h c", c=CROSS_D), AX.X, ALU.add)
                    if m == 0:
                        st_.run(ins)
                ins.then_inc(grp_sq, 1)
                dve.wait_ge(grp_root, 4 + n)
                st_.run(dve.reciprocal(st[:, 0, 8 * n:8 * n + 8], st[:, 0, 8 * n:8 * n + 8]))
                for m in range(TT):
                    w = v[:, m, 0:D].rearrange("p (h c) -> p h c", c=CROSS_D)
                    ins = TTT(w, w, spread(st[:, 0, 8 * n + 4 * m:8 * n + 4 * m + 4], CROSS_D), ALU.mult)
                ins.then_inc(kc_ready if n == 0 else qc_ready, 1)

            def cross_max(h):
                dve.wait_ge(x_score, h + 1)
                st_.run(dve.tensor_reduce(sm[:, 0, 2 * h:2 * h + 2], ps[h % 2][:].rearrange("p (t k) -> p t k", t=2), AX.X,
                                          ALU.max, negate=True))
                TS(sm[:, 0, 2 * h:2 * h + 2], sm[:, 0, 2 * h:2 * h + 2], CROSS_D ** -0.5, None, ALU.mult).then_inc(x_max, 1)

            cross_max(0)
            for h in range(CROSS_H):
                if h + 1 < CROSS_H:
                    cross_max(h + 1)
                dve.wait_ge(x_prob, h + 1)
                st_.run(dve.reciprocal(sm[:, 1, 2 * h:2 * h + 2], sm[:, 1, 2 * h:2 * h + 2]))
                dve.wait_ge(x_o, h + 1)
                for qt in range(TT):
                    ins = TS(oc[:, qt, h * CROSS_D:(h + 1) * CROSS_D], ps[4 + 2 * (h % 2) + qt][:],
                             sm[:, 1, 2 * h + qt:2 * h + qt + 1], None, ALU.mult)
                ins.then_inc(x_o_out, 1)
            turn_rest(6, 4, None)
            add_blocks(U_CO)
            reciprocal_rms(3)
            dve.wait_ge(rstds, 4)
            for m in range(TT):
                ins = TS(xn[:, m], xh[:, m], rs[:, 6 + m:7 + m], None, ALU.mult)
            ins.then_inc(xn_ready, 1)
            turn_rest(7, 5, 3)
            with dve.Fori(0, N_PQ // 2) as i:
                for r in range(2 * BLK):
                    lo_loop(i, 2 * BLK, U_PQ, r + LEAD)

            nxt = [U_U[0] + LEAD]

            def stream(n):
                for _ in range(n):
                    if nxt[0] < U_U[0] + 8 * PLAIN + LEAD:
                        lo(nxt[0])
                        nxt[0] += 1

            def top16(vals, top, idx):
                for n in range(2):
                    t8, i8 = top[:, 8 * n:8 * n + 8], idx[:, 8 * n:8 * n + 8]
                    st_.run(dve.max(t8, vals))
                    st_.run(dve.max_index(i8, t8, vals))
                    if n == 0:
                        st_.run(dve.match_replace(vals, t8, vals, LOW))
                    stream(1)

            dve.wait_ge(h_saved, 16)
            for m in range(TT):
                for hc in range(2 * PH):
                    if hc % 4 == 0:
                        dve.wait_ge(sc_out, 4 * m + hc // 4 + 1)
                    top16(sc[:, m, hc], pk_top[:, m, hc], pk_idx[:, m, hc])
                st_.run(dve.tensor_copy(pk_idxf[:, m], pk_idx[:, m]))
                tv = pk_top[:, m].rearrange("p (h c) k -> p h c k", c=2)
                fi = pk_idxf[:, m].rearrange("p (h c) k -> p h c k", c=2)
                shape = [P, PH, TOPK, TOPK]
                st_.run(TTT(cand, tv[:, :, 0].unsqueeze(3).to_broadcast(shape), tv[:, :, 1].unsqueeze(2).to_broadcast(shape), ALU.add))
                stream(2)
                for h in range(PH):
                    top16(cand[:, h].rearrange("p a b -> p (a b)"), pk(1536, m)[:, h * TOPK:(h + 1) * TOPK],
                          pk(1792, m).bitcast(U32)[:, h * TOPK:(h + 1) * TOPK])
                pos = pk(1792, m).bitcast(U32)
                st_.done(TS(pk(2048, m).bitcast(U32), pos, 4, None, ALU.logical_shift_right))
                st_.run(TS(pk(2304, m).bitcast(U32), pos, 15, None, ALU.bitwise_and))
                for c in range(2):
                    st_.run(dve.tensor_copy(pk(2560, m), pk(2048 + 256 * c, m).bitcast(U32)))
                    place = pk(2560, m).rearrange("p (h k) -> p h k", h=PH)
                    st_.run(TTT(eq, iota[:, 0:TOPK].unsqueeze(1).unsqueeze(1).to_broadcast(shape),
                                place.unsqueeze(3).to_broadcast(shape), ALU.is_equal))
                    stream(2)
                    st_.run(TTT(eq, eq, fi[:, :, c].unsqueeze(2).to_broadcast(shape), ALU.mult))
                    stream(2)
                    st_.run(dve.tensor_reduce(pk(2816 + 256 * c, m).rearrange("p (h k) -> p h k", h=PH), eq, AX.X, ALU.add))
                    stream(2)
                top = pk(1536, m).rearrange("p (h k) -> p h k", h=PH)
                gate = pk_gate(m).rearrange("p (h k) -> p h k", h=PH)
                TTT(gate, top, top[:, :, 0:1].to_broadcast([P, PH, TOPK]), ALU.subtract).then_inc(gate_in, 1)
            stream(8 * PLAIN)
            for m in range(TT):
                gate = pk_gate(m).rearrange("p (h k) -> p h k", h=PH)
                dve.wait_ge(gate_exp, m + 1)
                st_.run(dve.tensor_reduce(sm[:, m, 0:PH], gate, AX.X, ALU.add))
                st_.run(dve.reciprocal(sm[:, m, 0:PH], sm[:, m, 0:PH]))
                TTT(gate, gate, spread(sm[:, m, 0:PH], TOPK), ALU.mult).then_inc(picks_ready, 1)
            dve.wait_ge(gate_ps, 8)
            for n in range(3):
                st_.done(dve.tensor_copy(pickT[:, n], ps[4 + n][:, 0:TOK]))
            st_.settle()

            def hot_rows(half, i, per, tk):
                s = tk % 8
                dve.wait_ge(gate_ps, i * per + (half * TOK + tk + 1))
                col = ds(i * per + tk, 1)
                TS(hot1[:, s], iota[:], pickT[:, 0, col], pickT[:, 2, col], ALU.is_equal, ALU.mult)
                TS(hot2[:, s], iota[:, HALF * half:HALF * (half + 1)], pickT[:, 1, col], None, ALU.is_equal).then_inc(hot_ready, 1)

            gates_by_key = ar(W, TOK, HALF).rearrange("p t j -> p j t")
            acts = ar(G, HALF, TOK)

            def product(half, j):
                v = acts[:, ds(j, 1), :]
                if isinstance(j, int) and j == 0:
                    dve.wait_ge(gelu_done, (half + 1) * HALF)
                    dve.wait_ge(gate_out, (half + 1) * TOK // 8)
                TTT(v, v, gates_by_key[:, ds(j, 1), :], ALU.mult).then_inc(coef, 1)

            def remainder(half, j, parity):
                dve.wait_ge(coef_hi, j + (half * HALF + 1))
                TTT(c_lo[:, parity:parity + 1], acts[:, ds(j, 1), :], c_hi[:, parity:parity + 1].bitcast(F32),
                    ALU.subtract).then_inc(coef_ready, 1)

            for half in range(2):
                with dve.Fori(0, ITS - PLAIN if half == 0 else ITS) as i:
                    for r in range(8):
                        lo_loop(i, 8, U_U[half] + (8 * PLAIN if half == 0 else 0), r + LEAD)
                        for n in range(TPI[half] // 8):
                            hot_rows(half, i, TPI[half], r * (TPI[half] // 8) + n)
                product(half, 0)
                remainder(half, 0, 0)
                with dve.Fori(0, ITS - 1) as i:
                    for r in range(8):
                        lo_loop(i, 8, U_V[half], r + LEAD)
                        if r % 4 == 0:
                            product(half, i * 2 + (1 + r // 4))
                        if r % 4 == 2:
                            remainder(half, i * 2 + (1 + r // 4), 1 - r // 4)
                for r in range(8):
                    lo(U_V[half] + 8 * (ITS - 1) + r + LEAD)
                    if r == 0:
                        product(half, HALF - 1)
                    if r == 2:
                        remainder(half, HALF - 1, 1)
                dve.wait_ge(res_in, 16 * (half + 1))
                for m in range(TT):
                    for s in range(4):
                        dve.wait_ge(used, U_V[half] + 4 * (HALF - 1) + s + 1)
                        v = res[:, m, s * NB:(s + 1) * NB]
                        TTT(v, ps[4 * m + s][:], v, ALU.add).then_inc(acc_out, 1)

        @block.tensor
        def _(pe):
            def turn(n, src):
                for j in range(KC // 2):
                    at_least(pe, turn_out, 8 * n + j - 3)
                    for kk in range(2):
                        for m in range(TT):
                            ins = pe.transpose(ps[4 + j % 4][:, kk * TOK + m * P:kk * TOK + (m + 1) * P], src(m, 2 * j + kk), ident[:])
                    ins.then_inc(turned, 1)

            def chunk(k, r, bank, ahi, alo):
                for m in range(TT):
                    o, sh, sl = ps[bank + m][:], ahi[:, k, m * P:(m + 1) * P], alo[:, k, m * P:(m + 1) * P]
                    pe.matmul(o, sh, w_hi[:, r % 4], start=(k == 0), stop=False)
                    pe.matmul(o, sh, w_lo[:, r % 4], start=False, stop=False)
                    ins = pe.matmul(o, sl, w_hi[:, r % 4], start=False, stop=(k == KC - 1))
                ins.then_inc(used, 1)
                return ins

            def project(i, u0, per, r, bank, ahi=a_hi, alo=a_lo):
                pe.wait_ge(lo_done, i * per + (u0 + r + 1))
                chunk(r % BLK, r, bank, ahi, alo)

            def two_blocks(i, u0, out_sem, before):
                for r in range(2 * BLK):
                    b = r // BLK
                    if r % BLK == 0:
                        at_least(pe, out_sem, i * 2 + (before + b - 1))
                    project(i, u0, 2 * BLK, r, 2 * b)

            pe.wait_ge(onehot_in, 32)
            pe.matmul(ps[3][0:8, 0:SPITCH], relb, onehot, start=True, stop=True).then_inc(toep_ps, 1)
            pe.wait_ge(consts, 4)
            pe.wait_ge(x_in, 16)
            turn(0, lambda m, k: xh[:, m, k * P:(k + 1) * P])
            pe.wait_ge(turn_out, 8)
            pe.wait_ge(toep_sb, 1)
            two_blocks(0, U_IN, evac, 0)
            with pe.Fori(1, N_IN // 2) as i:
                two_blocks(i, U_IN, evac, 0)
            pe.wait_ge(mem_in, 16)
            turn(1, lambda m, k: memr[:, m, k * P:(k + 1) * P])
            pe.wait_ge(turn_out, 16)
            pe.wait_ge(masked, 1)
            for n in range(4):
                pe.wait_ge(vn_ready, n // 2 + 1)
                for hh in range(4):
                    m, h = n // 2, 4 * (n % 2) + hh
                    ins = pe.matmul(ps[4 + n][:, hh * P:(hh + 1) * P], wst[:, h], z[:, m, ZV + h * SGU_D:ZV + (h + 1) * SGU_D],
                                    start=True, stop=True)
                ins.then_inc(sgu_ps, 1)
            with pe.Fori(0, DIFF_H) as i:
                pe.wait_ge(qk_scaled, i + 1)
                for n in range(4):
                    ins = pe.transpose(ps[2][:, n * P:(n + 1) * P], qk_st[:, n], ident[:])
                ins.then_inc(qk_turned, 1)
                pe.wait_ge(evac, i + N_IN)
                for r in range(BLK):
                    project(i, U_CKV, BLK, r, 0, m_hi, m_lo)
                    if r == 2:
                        pe.wait_ge(qk_ready, i + 1)
                        for qt in range(TT):
                            kn = P * (qt + 1)
                            for c in range(2):
                                ins = pe.matmul(ps[3 + qt][:, c * kn:(c + 1) * kn], qz[:, c, qt * P:(qt + 1) * P], kz[:, 0:kn],
                                                start=True, stop=True)
                            ins.then_inc(score_ps, 1)
                    if r == 9:
                        for qt in range(TT):
                            pe.wait_ge(a_ready, i * 2 + (qt + 1))
                            for kt in range(qt + 1):
                                ins = pe.transpose(ps[5][:, (qt + kt) * P:(qt + kt + 1) * P], logit[:, qt, 0, kt * P:(kt + 1) * P], ident[:])
                        ins.then_inc(aT_ps, 1)
                    if r == 12:
                        pe.wait_ge(aT_ready, i + 1)
                        for qt in range(TT):
                            for kt in range(qt + 1):
                                ins = pe.matmul(ps[6][:, qt * DIFF_V:(qt + 1) * DIFF_V], aT[:, qt + kt],
                                                z[:, kt, ds(i * DIFF_V + ZVD, DIFF_V)], start=(kt == 0), stop=(kt == qt))
                        ins.then_inc(o_ps, 1)
            pe.wait_ge(mix_ready, 2)
            turn(2, lambda m, k: z[:, m, (ZU if k < 8 else ZQ - 1024) + k * P:(ZU if k < 8 else ZQ - 1024) + (k + 1) * P])
            pe.wait_ge(turn_out, 24)
            two_blocks(0, U_OUT, added, 0)
            two_blocks(1, U_OUT, added, 0)
            pe.wait_ge(added, N_OUT)
            turn(3, lambda m, k: xh[:, m, k * P:(k + 1) * P])
            pe.wait_ge(turn_out, 32)
            two_blocks(0, U_CQ, evac, N_IN + N_CKV)
            two_blocks(1, U_CQ, evac, N_IN + N_CKV)
            pe.wait_ge(kc_ready, 1)
            turn(4, lambda m, k: kv[:, m, k * P:(k + 1) * P])
            pe.wait_ge(qc_ready, 1)
            turn(5, lambda m, k: cq[:, m, k * P:(k + 1) * P])
            pe.wait_ge(turn_out, 48)

            def cross_scores(h):
                if h >= 2:
                    pe.wait_ge(x_prob, h - 1)
                for qt in range(TT):
                    for c in range(CH):
                        k = h * CH + c
                        ins = pe.matmul(ps[h % 2][:, qt * TOK:(qt + 1) * TOK], qT[:, k, qt * P:(qt + 1) * P], kT[:, k, :],
                                        start=(c == 0), stop=(c == CH - 1))
                ins.then_inc(x_score, 1)

            cross_scores(0)
            for h in range(CROSS_H):
                if h + 1 < CROSS_H:
                    cross_scores(h + 1)
                pe.wait_ge(x_prob, h + 1)
                for qt in range(TT):
                    for mt in range(TT):
                        n = 2 * qt + mt
                        ins = pe.transpose(ps[2 + h % 2][:, n * P:(n + 1) * P], cp[:, h % 2, qt, mt * P:(mt + 1) * P], ident[:])
                ins.then_inc(x_pT, 1)
                pe.wait_ge(x_pT_out, h + 1)
                if h >= 2:
                    pe.wait_ge(x_o_out, h - 1)
                for qt in range(TT):
                    for mt in range(TT):
                        ins = pe.matmul(ps[4 + 2 * (h % 2) + qt][:], cpT[:, h % 2, 2 * qt + mt],
                                        kv[:, mt, D + h * CROSS_D:D + (h + 1) * CROSS_D], start=(mt == 0), stop=(mt == 1))
                ins.then_inc(x_o, 1)
            pe.wait_ge(x_o_out, CROSS_H)
            turn(6, lambda m, k: oc[:, m, k * P:(k + 1) * P])
            pe.wait_ge(turn_out, 56)
            two_blocks(0, U_CO, added, N_OUT)
            two_blocks(1, U_CO, added, N_OUT)
            pe.wait_ge(xn_ready, 1)
            turn(7, lambda m, k: xn[:, m, k * P:(k + 1) * P])
            pe.wait_ge(turn_out, 64)
            two_blocks(0, U_PQ, evac, N_IN + N_CKV + N_CQ)
            two_blocks(1, U_PQ, evac, N_IN + N_CKV + N_CQ)
            pe.wait_ge(evac, N_IN + N_CKV + N_CQ + N_PQ)
            turn(8, lambda m, k: pq[:, m, k * P:(k + 1) * P])
            pe.wait_ge(turn_out, 72)
            pe.wait_ge(keys_in, 16)
            for n in range(8):
                if n >= 4:
                    pe.wait_ge(sc_out, n - 3)
                for a in range(4):
                    m, hc = n // 4, 4 * (n % 4) + a
                    ins = pe.matmul(ps[n % 4][:, a * NK:(a + 1) * NK], pqT[:, hc, m * P:(m + 1) * P], keysT[:, hc], start=True, stop=True)
                ins.then_inc(sc_ps, 1)
            pe.wait_ge(sc_out, 8)

            def activations(i, half, it0, tokens):
                for r in range(8):
                    jl = r // 4
                    if r % 4 == 0:
                        at_least(pe, gelu_done, i * 2 + (half * HALF + 2 * it0 + jl - 1))
                    pe.wait_ge(lo_done, i * 8 + (U_U[half] + 8 * it0 + r + 1))
                    for dd in range(4):
                        k = 4 * (r % 4) + dd
                        o, uh, ul = ps[jl][:, 0:TOK], w_hi[:, r % 4, dd * P:(dd + 1) * P], w_lo[:, r % 4, dd * P:(dd + 1) * P]
                        pe.matmul(o, uh, a_hi[:, k], start=(k == 0), stop=False)
                        pe.matmul(o, uh, a_lo[:, k], start=False, stop=False)
                        ins = pe.matmul(o, ul, a_hi[:, k], start=False, stop=(k == KC - 1))
                    ins.then_inc(used, 1)
                    for n in range(tokens // 8):
                        tk = r * (tokens // 8) + n
                        if tk % 8 == 0:
                            at_least(pe, gate_out, i + 32 if half else i * 2 + (tk // 8 - 1))
                        pe.wait_ge(hot_ready, i * tokens + (half * TOK + tk + 1))
                        pe.matmul(ps[2 + (tk // 8)][:, (tk % 8) * HALF:(tk % 8 + 1) * HALF], hot1[:, tk % 8], hot2[:, tk % 8],
                                  start=True, stop=True).then_inc(gate_ps, 1)

            def outputs(i, half, first, last):
                for r in range(8):
                    j, s = r // 4, r % 4
                    if s == 0:
                        pe.wait_ge(coef_ready, i * 2 + (half * HALF + j + 1))
                    pe.wait_ge(lo_done, i * 8 + (U_V[half] + r + 1))
                    for m in range(TT):
                        o, sh, sl = ps[4 * m + s][:], c_hi[:, j, m * P:(m + 1) * P], c_lo[:, j, m * P:(m + 1) * P]
                        pe.matmul(o, sh, w_hi[:, r % 4], start=first and j == 0, stop=False)
                        pe.matmul(o, sh, w_lo[:, r % 4], start=False, stop=False)
                        ins = pe.matmul(o, sl, w_hi[:, r % 4], start=False, stop=last and j == 1)
                    ins.then_inc(used, 1)

            for half in range(2):
                if half == 0:
                    activations(0, 0, 0, 0)
                    with pe.Fori(1, PLAIN) as i:
                        activations(i, 0, 0, 0)
                    pe.wait_ge(picks_ready, 2)
                    for n, col in enumerate((2816, 3072, 3328)):
                        for m in range(TT):
                            ins = pe.transpose(ps[4 + n][:, m * P:(m + 1) * P], pk(col, m), ident[:])
                    ins.then_inc(gate_ps, 8)
                    activations(0, 0, PLAIN, TPI[0])
                    with pe.Fori(1, ITS - PLAIN) as i:
                        activations(i, 0, PLAIN, TPI[0])
                else:
                    pe.wait_ge(acc_out, 4)
                    with pe.Fori(0, ITS) as i:
                        activations(i, 1, 0, TPI[1])
                    pe.wait_ge(acc_out, 8)
                outputs(0, half, True, False)
                with pe.Fori(1, ITS - 1) as i:
                    outputs(i, half, False, False)
                outputs(ITS - 1, half, False, True)


def kernel(**inputs):
    import numpy as np
    import concourse.bacc as bacc
    from concourse import mybir as _mybir
    from concourse.bass_utils import run_bass_kernel_spmd

    a = {k: np.asarray(v) for k, v in inputs.items()}

    def projection(w):
        n = w.shape[1]
        return w.reshape(KC // 2, 2, P, n // NB, NB).transpose(3, 0, 2, 1, 4).reshape(-1, P, 2 * NB)

    def columns(g):
        return g.reshape(-1, P).T

    dist = np.maximum(2 * P - 1 - np.arange(SPITCH), 0)
    exact = 16
    large = exact + (np.log(np.maximum(dist, 1).astype(np.float32) / exact) / np.float32(np.log(128 / exact)) * (32 - exact)).astype(np.int32)
    bucket = np.where(dist < exact, dist, np.minimum(large, 31))
    onehot = (np.arange(32)[:, None] == bucket[None, :]).astype(np.float32)

    arrays = {
        "x": a["x"][0], "mem": a["mem"][0],
        "w_in": projection(a["w_in"][0]), "w_ckv": projection(a["w_ckv"][0]), "w_out": projection(a["w_out"][0]),
        "w_cq": projection(a["w_cq"][0]), "w_co": projection(a["w_co"][0]), "peer_wq": projection(a["peer_wq"][0]),
        "peer_u": a["peer_u"][0].reshape(NK, NK, 2, 8, P).transpose(1, 2, 4, 3, 0).reshape(2 * NK, P, 8 * NK),
        "peer_v": a["peer_v"][0].reshape(NK, NK, 2, 1024).transpose(1, 2, 0, 3).reshape(2 * NK, NK, 1024),
        "peer_keys": a["peer_keys"][0].reshape(2 * PH, NK, P).transpose(2, 0, 1),
        "mix_g": columns(a["norm_mix_g"][0]), "mem_g": columns(a["norm_mem_g"][0]),
        "cross_g": columns(a["norm_cross_g"][0]), "ffn_g": columns(a["norm_ffn_g"][0]),
        "sgu_g": a["sgu_norm_g"][0].reshape(-1), "sgu_w": a["sgu_w"][0].transpose(2, 0, 1), "sgu_b": a["sgu_b"][0].T,
        "q_g": a["q_norm_g"][0][:, None], "k_g": a["k_norm_g"][0][:, None],
        "lambdas": np.stack([a[n][0] for n in ("lambda_q1", "lambda_k1", "lambda_q2", "lambda_k2")]),
        "subln_g": a["diff_subln_g"][0], "rel_bias": a["rel_bias"], "bucket_of": onehot,
        "cq_g": columns(a["cq_norm_g"][0]), "ck_g": columns(a["ck_norm_g"][0]),
    }
    arrays = {f"in_{k}": np.ascontiguousarray(v) for k, v in arrays.items()}
    nc = bacc.Bacc("TRN2", target_bir_lowering=False, num_devices=1)
    args = {k[3:]: nc.dram_tensor(k, v.shape, _mybir.dt.from_np(v.dtype), kind="ExternalInput").ap() for k, v in arrays.items()}
    out = nc.dram_tensor("out", (TOK, D), _mybir.dt.float32, kind="ExternalOutput").ap()
    hybrid_layer(nc, out=out, **args)
    r = run_bass_kernel_spmd(nc, [arrays], core_ids=[0])
    return r.results[0]["out"].reshape(1, TOK, D)
```

```python
from contextlib import ExitStack

import concourse.bass as bass
from concourse import mybir

ALU = mybir.AluOpType
ACT = mybir.ActivationFunctionType
AX = mybir.AxisListType
F32 = mybir.dt.float32
F32R = mybir.dt.float32r
U32 = mybir.dt.uint32
ds = bass.ds

P = 128
D = 2048
KC = D // P
TT = 2
TOK = TT * P
EPS = 1e-6
NB = 512
SUB = 512
SLOTS = 4
LEAD = 3
SGU_H, SGU_D = 8, 128
DIFF_H, DIFF_D, DIFF_V = 8, 64, 128
CROSS_H = 4
CROSS_D = D // CROSS_H
CH = CROSS_D // P
PH, NK, TOPK = 8, 128, 16
HALF = NK // 2
LAM_INIT = 0.2
NEG = -1.0e30
LOW = -3.0e38

BLK = KC
N_IN, N_CKV, N_OUT, N_CQ, N_CO, N_PQ = 10, 8, 4, 4, 4, 4
U_IN = 0
U_CKV = U_IN + N_IN * BLK
U_OUT = U_CKV + N_CKV * BLK
U_CQ = U_OUT + N_OUT * BLK
U_CO = U_CQ + N_CQ * BLK
U_PQ = U_CO + N_CO * BLK
U_U = [U_PQ + N_PQ * BLK, 0]
U_V = [U_U[0] + HALF * 4, 0]
U_U[1] = U_V[0] + HALF * 4
U_V[1] = U_U[1] + HALF * 4
U_END = U_V[1] + HALF * 4
ITS = HALF // 2
PLAIN = 16
TPI = [TOK // (ITS - PLAIN), TOK // ITS]

MT = 0
Z = 8192
ZW = 5120
ZU, ZV, ZQ, ZK, ZVD = 0, 1024, 2048, 3072, 4096
MEM = 18432
SG, WS = 22528, 23552
KV = 18432
H = 26624
BI = 30720
KT = 8192
CQ = 12288
QT = 16384
XN = 8192
KEYS = 30720
PQ = 18432
PQT = 22528
CAND, EQ = 22528, 24576
PK = 26624
G = 0
W = 16384
R = 0
SPITCH = 384


def at_least(eng, sem, value):
    if not isinstance(value, int) or value > 0:
        eng.wait_ge(sem, value)


class Steps:

    def __init__(self, eng, sem):
        self.eng, self.sem, self.n = eng, sem, 0

    def done(self, ins):
        ins.then_inc(self.sem, 1)
        self.n = self.n + 1

    def settle(self):
        self.eng.wait_ge(self.sem, self.n)

    def run(self, ins):
        self.done(ins)
        self.settle()


def hybrid_layer(nc, x, mem, w_in, w_ckv, w_out, w_cq, w_co, peer_wq, peer_u, peer_v, peer_keys, mix_g, mem_g,
                 cross_g, ffn_g, sgu_g, sgu_w, sgu_b, q_g, k_g, lambdas, subln_g, rel_bias, bucket_of, cq_g, ck_g, out):
    ctx = ExitStack()
    with ctx:
        def sb(name, shape, dt=F32):
            return ctx.enter_context(nc.sbuf_tensor(name, shape, dt))

        def sem(name):
            return ctx.enter_context(nc.semaphore(name))

        with nc.sbuf_tensor("m_hi", [P, KC, TOK], F32R) as m_hi, nc.sbuf_tensor("m_lo", [P, KC, TOK], F32R) as m_lo:
            pass
        arena = sb("arena", [P, 32768])
        with ExitStack() as late:
            def lsb(name, shape, dt=F32):
                return late.enter_context(nc.sbuf_tensor(name, shape, dt))
            hot1 = lsb("hot1", [P, 8, NK])
            hot2 = lsb("hot2", [P, 8, HALF])
            c_hi = lsb("c_hi", [P, 2, TOK], F32R)
            c_lo = lsb("c_lo", [P, 2, TOK], F32R)
            pickT = lsb("pickT", [P, 3, TOK])
        wk = sb("wk", [P, 3328])
        raw = sb("raw", [P, SLOTS, 2, SUB])
        w_hi = sb("w_hi", [P, SLOTS, SUB], F32R)
        w_lo = sb("w_lo", [P, SLOTS, SUB], F32R)
        a_hi = sb("a_hi", [P, KC, TOK], F32R)
        a_lo = sb("a_lo", [P, KC, TOK], F32R)
        ident = sb("ident", [P, P])
        iota = sb("iota", [P, NK])
        gains = sb("gains", [P, 5, KC])
        sgb = sb("sgb", [P, SGU_H])
        qkg = sb("qkg", [P, 2])
        subg = sb("subg", [P, DIFF_V])
        eps = sb("eps", [P, 1])
        ss = sb("ss", [P, 8])
        rs = sb("rs", [P, 8])
        st = sb("st", [P, 2, 64])
        lam = sb("lam", [P, 8])
        sm = sb("sm", [P, 3, 16])

        def ar(col, *dims):
            n = 1
            for d in dims:
                n *= d
            v = arena[:, col:col + n]
            if len(dims) == 2:
                return v.rearrange("p (a b) -> p a b", b=dims[1])
            if len(dims) == 3:
                return v.rearrange("p (a b c) -> p a b c", b=dims[1], c=dims[2])
            return v

        z = ar(Z, TT, ZW)
        xh = ar(H, TT, D)
        memr = ar(MEM, TT, D)
        kv = ar(KV, TT, 2 * D)
        bias = ar(BI, DIFF_H, TOK)
        sgg, wst = ar(SG, SGU_H * SGU_D), ar(WS, SGU_H, P)
        kT = ar(KT, KC, TOK)
        qT = [ar(QT + n * CH * TOK, CH, TOK) for n in range(2)]
        cq, oc, xn = ar(CQ, TT, D), kv[:, :, 0:D], ar(XN, TT, D)
        keysT, pq, sc = ar(KEYS, 2 * PH, NK), ar(PQ, TT, D), ar(PQ, TT, 2 * PH, NK)
        pqT = ar(PQT, KC, TOK)
        cand, eq = ar(CAND, PH, TOPK, TOPK), ar(EQ, PH, TOPK, TOPK)
        res = ar(R, TT, D)
        pk_top, pk_idxf = ar(PK, TT, 2 * PH, TOPK), ar(PK + 1024, TT, 2 * PH, TOPK)
        pk_idx = ar(PK + 512, TT, 2 * PH, TOPK).bitcast(U32)

        def mix_chunks(a, i):
            return a[:].rearrange("p (s h) t -> p s h t", s=2)[:, :, ds(i, 1), :].rearrange("p s o t -> p s (o t)")

        def pk(col, m):
            return arena[:, PK + col + P * m:PK + col + P * (m + 1)]

        def pk_gate(m):
            return pk(3328, m)

        stg = st[:, 1, :].rearrange("p (m g) -> p m g", m=TT)
        sq = wk[:, 0:2048]
        qk_st = wk[:, 0:512].rearrange("p (a b) -> p a b", a=4)
        logit = wk[:, 512:1536].rearrange("p (a c k) -> p a c k", a=2, c=2)
        aT = wk[:, 1536:1920].rearrange("p (a b) -> p a b", a=3)
        qz = wk[:, 2048:2560].rearrange("p (c t) -> p c t", c=2)
        kz = wk[:, 2560:2816]
        o_st = wk[:, 0:256].rearrange("p (m d) -> p m d", m=2)
        u_st = wk[:, 3072:3328].rearrange("p (m d) -> p m d", m=2)
        junk = wk[:, 1920:2048]
        lamv = wk[:, 2816:3072].rearrange("p (a b) -> p a b", a=4)
        cp = wk[:, 0:1024].rearrange("p (b t m) -> p b t m", b=2, t=2)
        cpT = wk[:, 1024:2048].rearrange("p (b n q) -> p b n q", b=2, q=P)
        onehot = wk[0:32, 0:SPITCH]
        relb = wk[0:32, 400:408]
        toep = wk[0:8, 512:512 + SPITCH]

        ps = [ctx.enter_context(nc.psum_tensor(f"ps{i}", [P, 512], F32)) for i in range(8)]

        raw_in = [sem(f"raw_in{s}") for s in range(SLOTS)]
        hi_done = sem("hi_done")
        lo_done = sem("lo_done")
        used = sem("used")
        evac = sem("evac")
        added = sem("added")
        TURNS = ("x", "mem", "mix", "h1", "ck", "cq", "oc", "h2", "h2n", "pq")
        turned = {t: sem(f"turned_{t}") for t in TURNS}
        turn_hi = {t: sem(f"turn_hi_{t}") for t in TURNS}
        turn_out = {t: sem(f"turn_out_{t}") for t in TURNS}
        sums = sem("sums")
        rstds = sem("rstds")
        x_in, mem_in, small_in = sem("x_in"), sem("mem_in"), sem("small_in")
        onehot_in = sem("onehot_in")
        consts = sem("consts")
        masked = sem("masked")
        toep_ps, toep_sb, toep_out, bias_in = sem("toep_ps"), sem("toep_sb"), sem("toep_out"), sem("bias_in")
        dve_step, act_step, pool_step = sem("dve_step"), sem("act_step"), sem("pool_step")
        grp_sq, grp_root = sem("grp_sq"), sem("grp_root")
        lam_sum, lam_exp = sem("lam_sum"), sem("lam_exp")
        vn_ready, sgu_ps = sem("vn_ready"), sem("sgu_ps")
        qk_scaled, qk_turned, qk_ready = sem("qk_scaled"), sem("qk_turned"), sem("qk_ready")
        score_ps, logit_ready, prob_ready = sem("score_ps"), sem("logit_ready"), sem("prob_ready")
        a_ready, aT_ps, aT_ready = sem("a_ready"), sem("aT_ps"), sem("aT_ready")
        o_ps, o_rms, o_ready = sem("o_ps"), sem("o_rms"), sem("o_ready")
        sgu_out, u_staged = sem("sgu_out"), sem("u_staged")
        kc_ready, x_rms = sem("kc_ready"), sem("x_rms")
        x_score, x_max, x_prob, x_rsum = sem("x_score"), sem("x_max"), sem("x_prob"), sem("x_rsum")
        x_pT, x_pT_out, x_o, x_o_out = sem("x_pT"), sem("x_pT_out"), sem("x_o"), sem("x_o_out")
        xn_ready = sem("xn_ready")
        keys_in, h_saved = sem("keys_in"), sem("h_saved")
        sc_ps, sc_out = sem("sc_ps"), sem("sc_out")
        gate_in, gate_exp, picks_ready = sem("gate_in"), sem("gate_exp"), sem("picks_ready")
        gelu_done = sem("gelu_done")
        hot_ready, gate_ps, gate_out = sem("hot_ready"), sem("gate_ps"), sem("gate_out")
        coef, coef_hi, coef_ready = sem("coef"), sem("coef_hi"), sem("coef_ready")
        acc_out, res_in, stored = sem("acc_out"), sem("res_in"), sem("stored")

        scratch = nc.dram_tensor("toeplitz_rows", [DIFF_H, SPITCH], F32, kind="Internal").ap()
        shifted = nc.dram_tensor("toeplitz_copies", [DIFF_H, P, SPITCH], F32, kind="Internal").ap()
        x_t = x.rearrange("(t p) d -> p t d", p=P)
        mem_t = mem.rearrange("(t p) d -> p t d", p=P)
        out_t = out.rearrange("(t p) d -> p t d", p=P)

        block = ctx.enter_context(nc.Block())

        @block.sync
        def _(sp):
            def tile(u, src, row):
                s = (u // 2) % SLOTS
                if u >= 2 * SLOTS:
                    sp.wait_ge(lo_done, u - 2 * SLOTS + 2)
                sp.dma_start(raw[:, s], src[row].rearrange("p (a n) -> p a n", a=2)).then_inc(raw_in[s], 16)

            def tiles(u0, src, row0, count):
                with sp.Fori(0, count // SLOTS) as i:
                    for s in range(SLOTS):
                        sp.wait_ge(lo_done, i * (2 * SLOTS) + (u0 + 2 * s - 2 * SLOTS + 2))
                        sp.dma_start(raw[:, s], src[ds(i * SLOTS + (row0 + s), 1)]
                                     .rearrange("o p (a n) -> p (o a) n", a=2)).then_inc(raw_in[s], 16)

            sp.dma_start(xh, x_t).then_inc(x_in, 16)
            for s in range(SLOTS):
                tile(2 * s, w_in, s)
            sp.dma_start(onehot, bucket_of).then_inc(onehot_in, 16)
            sp.dma_start(relb, rel_bias).then_inc(onehot_in, 16)
            for col, g in enumerate((mix_g, mem_g, cross_g, ffn_g)):
                sp.dma_start(gains[:, col, :], g).then_inc(small_in, 16)
            sp.dma_start(gains[:, 4, 0:4], cq_g).then_inc(small_in, 16)
            sp.dma_start(gains[:, 4, 4:8], ck_g).then_inc(small_in, 16)
            sp.dma_start(sgb[:], sgu_b).then_inc(small_in, 16)
            for c in range(2):
                sp.dma_start(qkg[64 * c:64 * c + 64, 0:1], q_g).then_inc(small_in, 16)
                sp.dma_start(qkg[64 * c:64 * c + 64, 1:2], k_g).then_inc(small_in, 16)
            sp.dma_start(subg[:], subln_g.partition_broadcast(P)).then_inc(small_in, 16)
            sp.dma_start(lamv, lambdas.partition_broadcast(P)).then_inc(small_in, 16)
            sp.dma_start(sgg, sgu_g.partition_broadcast(P)).then_inc(small_in, 16)
            sp.dma_start(wst, sgu_w).then_inc(small_in, 16)
            sp.dma_start(memr, mem_t).then_inc(mem_in, 16)
            sp.wait_ge(toep_sb, 1)
            sp.dma_start(scratch, toep).then_inc(toep_out, 16)
            sp.wait_ge(toep_out, 16)
            sp.dma_start(shifted, scratch.unsqueeze(1).to_broadcast([DIFF_H, P, SPITCH])).then_inc(toep_out, 16)
            sp.wait_ge(toep_out, 32)
            sp.dma_start(bias, bass.AP(tensor=shifted.tensor, offset=P - 1,
                                       ap=[[SPITCH - 1, P], [P * SPITCH, DIFF_H], [1, TOK]])).then_inc(bias_in, 16)
            tiles(2 * SLOTS, w_in, SLOTS, N_IN * BLK // 2 - SLOTS)
            tiles(U_CKV, w_ckv, 0, N_CKV * BLK // 2)
            tiles(U_OUT, w_out, 0, N_OUT * BLK // 2)
            sp.wait_ge(logit_ready, 2 * DIFF_H)
            sp.dma_start(keysT, peer_keys).then_inc(keys_in, 16)
            tiles(U_CQ, w_cq, 0, N_CQ * BLK // 2)
            tiles(U_CO, w_co, 0, N_CO * BLK // 2)
            tiles(U_PQ, peer_wq, 0, N_PQ * BLK // 2)
            for half in range(2):
                tiles(U_U[half], peer_u, half * HALF * 2, HALF * 2)
                tiles(U_V[half], peer_v, half * HALF * 2, HALF * 2)

        @block.gpsimd
        def _(pool):
            g = Steps(pool, pool_step)
            g.run(pool.memset(ident[:], 0.0))
            pool.affine_select(out=ident[:], in_=ident[:], compare_op=ALU.not_equal, fill=1.0, base=0,
                               pattern=[[-1, P]], channel_multiplier=1).then_inc(consts, 1)
            pool.iota(iota[:], pattern=[[1, NK]], base=0, channel_multiplier=0,
                      allow_small_or_imprecise_dtypes=True).then_inc(consts, 1)
            pool.memset(eps[:], EPS).then_inc(consts, 1)
            pool.memset(qz, 0.0).then_inc(consts, 1)
            pool.wait_ge(small_in, 16 * 15)
            pool.affine_select(out=wst, in_=wst, compare_op=ALU.is_ge, fill=0.0, base=0,
                               pattern=[[0, SGU_H], [1, P]], channel_multiplier=-1).then_inc(masked, 1)
            pool.wait_ge(bias_in, 16)
            pool.affine_select(out=bias, in_=bias, compare_op=ALU.is_ge, fill=NEG, base=P,
                               pattern=[[0, DIFF_H], [-1, TOK]], channel_multiplier=1).then_inc(masked, 1)
            pool.wait_ge(sgu_out, 1)
            with pool.Fori(0, DIFF_H) as i:
                pool.wait_ge(qk_turned, i + 1)
                pool.tensor_copy(u_st, z[:, :, ds(i * P + ZU, P)]).then_inc(u_staged, 1)
            pool.wait_ge(added, N_OUT + N_CO)
            pool.dma_start(out_t, xh).then_inc(h_saved, 16)
            pool.wait_ge(h_saved, 16)
            for half in range(2):
                pool.wait_ge(coef_ready, half * HALF + 16)
                pool.dma_start(res, out_t).then_inc(res_in, 16)
                for m in range(TT):
                    for s in range(4):
                        pool.wait_ge(acc_out, half * 8 + m * 4 + s + 1)
                        pool.dma_start(out_t[:, m, s * NB:(s + 1) * NB], res[:, m, s * NB:(s + 1) * NB]).then_inc(stored, 16)
                pool.wait_ge(stored, 128 * (half + 1))

        @block.scalar
        def _(act):
            st_ = Steps(act, act_step)

            def hi(u):
                act.wait_ge(raw_in[u % 8 // 2], 16 * (u // 8 + 1))
                at_least(act, used, u - 3)
                act.activation(w_hi[:, u % 4], raw[:, u % 8 // 2, u % 2], ACT.Copy).then_inc(hi_done, 1)

            def hi_loop(i, per, u0, r):
                s = (r % 8) // 2
                act.wait_ge(raw_in[s], i * (2 * per) + 16 * ((u0 + r) // 8 + 1))
                act.wait_ge(used, i * per + (u0 + r - 3))
                act.activation(w_hi[:, r % 4], raw[:, s, r % 2], ACT.Copy).then_inc(hi_done, 1)

            def copy_block(u_end, parity, dst, scale, func=ACT.Copy):
                act.wait_ge(used, u_end)
                for m in range(TT):
                    ins = act.activation(dst(m), ps[2 * parity + m][:], func, scale=scale(m))
                ins.then_inc(evac, 1)

            def turn_part(t, j, bank, gain, dst=a_hi):
                act.wait_ge(turned[t], j + 1)
                if gain is None:
                    ins = act.activation(dst[:, 2 * j:2 * j + 2, :], ps[bank][:].rearrange("p (a b) -> p a b", a=2), ACT.Copy)
                else:
                    for kk in range(2):
                        k = 2 * j + kk
                        ins = act.activation(dst[:, k, :], ps[bank][:, kk * TOK:(kk + 1) * TOK], ACT.Copy,
                                             scale=gains[:, gain, k:k + 1])
                ins.then_inc(turn_hi[t], 1)

            def turn_whole(t, j, bank, dst, gain):
                act.wait_ge(turned[t], j + 1)
                for kk in range(2):
                    ins = act.activation(dst(kk), ps[bank][:, kk * TOK:(kk + 1) * TOK], ACT.Copy, scale=gain(kk))
                ins.then_inc(turn_out[t], 1)

            def square(n, m, src, junk_):
                st_.run(act.activation(junk_, src[:, m], ACT.Square, accum_out=ss[:, 2 * n + m:2 * n + m + 1]))

            def root(n):
                act.activation(rs[:, 2 * n:2 * n + 2], ss[:, 2 * n:2 * n + 2], ACT.Sqrt, bias=eps[:, 0:1],
                               scale=1.0 / D).then_inc(sums, 1)

            for u in range(LEAD):
                hi(u)
            act.wait_ge(small_in, 16 * 15)
            act.wait_ge(consts, 4)
            for j in range(KC // 2):
                turn_part("x", j, 4 + j % 4, 0)
            act.wait_ge(x_in, 16)
            for m in range(TT):
                square(0, m, xh, z[:, 0, 0:D])
            root(0)
            act.wait_ge(toep_ps, 1)
            act.activation(toep, ps[3][0:8, 0:SPITCH], ACT.Copy).then_inc(toep_sb, 1)
            for b in range(N_IN):
                for r in range(BLK):
                    hi(U_IN + b * BLK + r + LEAD)
                    if b == 2 and r % 2:
                        turn_part("mem", r // 2, 4 + r // 2 % 4, 1, m_hi)
                    if b == 3 and r in (2, 5):
                        square(1, r // 4, memr, ar(MEM + 6144, D))
                    if b == 3 and r == 7:
                        root(1)
                    if b == 5 and r == 0:
                        act.wait_ge(grp_sq, 1)
                        act.activation(st[:, 0, 0:16], st[:, 0, 0:16], ACT.Sqrt, bias=eps[:, 0:1],
                                       scale=1.0 / SGU_D).then_inc(grp_root, 1)
                    if b in (7, 9) and r == 0:
                        n = (b - 7) // 2
                        act.wait_ge(grp_sq, 2 + n)
                        act.activation(stg[:, :, 16 * n:16 * n + 16], stg[:, :, 16 * n:16 * n + 16], ACT.Sqrt,
                                       bias=eps[:, 0:1], scale=1.0 / DIFF_D).then_inc(grp_root, 1)
                    if b == 9 and r == 2:
                        act.wait_ge(lam_sum, 2)
                        act.activation(lam[:, 2:4], lam[:, 0:2], ACT.Exp).then_inc(lam_exp, 1)
                if b == 0:
                    act.wait_ge(rstds, 1)
                copy_block(U_IN + (b + 1) * BLK, b % 2, lambda m: z[:, m, b * NB:(b + 1) * NB], lambda m: rs[:, m:m + 1],
                           ACT.Gelu if b < 4 else ACT.Copy)
            act_n0 = st_.n
            with act.Fori(0, DIFF_H) as i:
                st_.n = i * 2 + act_n0
                for r in range(BLK):
                    hi_loop(i, BLK, U_CKV, r + LEAD)
                    if r == 0:
                        act.wait_ge(qk_turned, i + 1)
                        for c in range(2):
                            rows = slice(64 * c, 64 * c + 64)
                            act.activation(qz[rows, c], ps[2][rows, 0:TOK], ACT.Copy, scale=qkg[rows, 0:1])
                        act.activation(kz, ps[2][:, TOK:2 * TOK], ACT.Copy, scale=qkg[:, 1:2]).then_inc(qk_ready, 1)
                    if r == 3:
                        for qt in range(TT):
                            kn = P * (qt + 1)
                            act.wait_ge(logit_ready, i * 2 + (qt + 1))
                            for c in range(2):
                                ins = act.activation(logit[:, qt, c, 0:kn], logit[:, qt, c, 0:kn], ACT.Exp,
                                                     bias=sm[:, 0, 2 * qt + c:2 * qt + c + 1],
                                                     accum_out=sm[:, 1, 2 * qt + c:2 * qt + c + 1])
                            ins.then_inc(prob_ready, 1)
                    if r == 8:
                        act.wait_ge(aT_ps, i + 1)
                        act.activation(aT, ps[5][:, 0:3 * P].rearrange("p (a b) -> p a b", a=3), ACT.Copy).then_inc(aT_ready, 1)
                    if r == 10:
                        act.wait_ge(o_ps, i + 1)
                        for m in range(TT):
                            st_.run(act.activation(junk, ps[6][:, m * DIFF_V:(m + 1) * DIFF_V], ACT.Square,
                                                   accum_out=sm[:, 1, 8 + m:9 + m]))
                        act.activation(sm[:, 1, 8:10], sm[:, 1, 8:10], ACT.Sqrt, bias=eps[:, 0:1],
                                       scale=1.0 / DIFF_V).then_inc(o_rms, 1)
                    if r == 15:
                        act.wait_ge(turned["mix"], i + 1)
                        act.activation(mix_chunks(a_hi, i), ps[7][:].rearrange("p (a b) -> p a b", a=2),
                                       ACT.Copy).then_inc(turn_hi["mix"], 1)
                copy_block(i * BLK + (U_CKV + BLK), 0, lambda m: kv[:, m, ds(i * NB, NB)], lambda m: rs[:, 2 + m:3 + m])
            st_.n = act_n0 + 2 * DIFF_H

            def cross(h, r):
                if r == 1:
                    for g in range(2):
                        turn_whole("cq", 2 * h + g, 4 + g, lambda kk: qT[h % 2][:, 2 * g + kk],
                                   lambda kk: gains[:, 4, 2 * g + kk:2 * g + kk + 1])
                if r == 2:
                    for m in range(TT):
                        st_.run(act.activation(wk[:, 2048:2560], cq[:, m, h * CROSS_D:(h + 1) * CROSS_D], ACT.Square,
                                               accum_out=sm[:, 2, 2 * h + m:2 * h + m + 1]))
                    act.activation(sm[:, 2, 2 * h:2 * h + 2], sm[:, 2, 2 * h:2 * h + 2], ACT.Sqrt, bias=eps[:, 0:1],
                                   scale=1.0 / CROSS_D).then_inc(x_rms, 1)
                if r == 5:
                    act.wait_ge(x_max, h + 1)
                    for qt in range(TT):
                        n = 2 * h + qt
                        ins = act.activation(cp[:, h % 2, qt], ps[6][:, qt * TOK:(qt + 1) * TOK], ACT.Exp,
                                             bias=sm[:, 0, n:n + 1], scale=sm[:, 2, n:n + 1], accum_out=sm[:, 1, n:n + 1])
                    ins.then_inc(x_prob, 1)
                if r == 7:
                    act.wait_ge(x_pT, h + 1)
                    act.activation(cpT[:, h % 2], ps[7][:].rearrange("p (n q) -> p n q", q=P), ACT.Copy).then_inc(x_pT_out, 1)
                if r == 11:
                    for g in range(2):
                        turn_part("oc", 2 * h + g, 6 + g, None)

            for b in range(N_OUT):
                for r in range(BLK):
                    hi(U_OUT + b * BLK + r + LEAD)
                    if b and r in (3, 5):
                        turn_part("h1", 2 * (b - 1) + r // 4, 6 + r // 4, 2, m_hi)
                    if b == 1 and r == 0:
                        act.wait_ge(grp_sq, 4)
                        act.activation(st[:, 0, 0:8], st[:, 0, 0:8], ACT.Sqrt, bias=eps[:, 0:1],
                                       scale=1.0 / CROSS_D).then_inc(grp_root, 1)
                    if b == 2 and r % 2:
                        j = r // 2
                        turn_whole("ck", j, 4 + j % 2, lambda kk: kT[:, 2 * j + kk],
                                   lambda kk: gains[:, 4, 4 + (2 * j + kk) % CH:5 + (2 * j + kk) % CH])
            for b in range(N_CQ):
                for r in range(BLK):
                    hi(U_CQ + b * BLK + r + LEAD)
                    if b == 0:
                        if r in (3, 5):
                            turn_part("h1", 6 + r // 4, 6 + r // 4, 2, m_hi)
                        if r in (7, 9):
                            act.wait_ge(added, N_OUT)
                            square(2, (r - 7) // 2, xh, ar(QT, D))
                        if r == 11:
                            root(2)
                    else:
                        cross(b - 1, r)
                if b == 0:
                    act.wait_ge(rstds, 3)
                copy_block(U_CQ + (b + 1) * BLK, b % 2, lambda m: cq[:, m, b * NB:(b + 1) * NB], lambda m: rs[:, 4 + m:5 + m])
            for b in range(N_CO):
                for r in range(BLK):
                    hi(U_CO + b * BLK + r + LEAD)
                    if b == 0:
                        cross(CROSS_H - 1, r)
                    elif r in (3, 5):
                        turn_part("h2", 2 * (b - 1) + r // 4, 6 + r // 4, 3, m_hi)

            def peer_queries(b, r):
                if r == 1:
                    for g in range(2):
                        turn_whole("pq", 2 * b + g, 4 + g, lambda kk: pqT[:, 4 * b + 2 * g + kk], lambda kk: 1.0)
                if r == 5:
                    for m in range(TT):
                        act.wait_ge(sc_ps, 2 * b + m + 1)
                        act.activation(sc[:, m, 4 * b:4 * b + 4], ps[4 + m][:].rearrange("p (a k) -> p a k", k=NK),
                                       ACT.Copy).then_inc(sc_out, 1)

            for b in range(N_PQ):
                for r in range(BLK):
                    hi(U_PQ + b * BLK + r + LEAD)
                    if b == 0:
                        if r in (3, 5):
                            turn_part("h2", 6 + r // 4, 6 + r // 4, 3, m_hi)
                        if r in (7, 9):
                            act.wait_ge(added, N_OUT + N_CO)
                            square(3, (r - 7) // 2, xh, ar(QT, D))
                        if r == 11:
                            root(3)
                    else:
                        peer_queries(b - 1, r)
                    if b == 1 and r % 2:
                        turn_part("h2n", r // 2, 6 + r // 2 % 2, 3)
                if b == 0:
                    act.wait_ge(rstds, 4)
                copy_block(U_PQ + (b + 1) * BLK, b % 2, lambda m: pq[:, m, b * NB:(b + 1) * NB], lambda m: rs[:, 6 + m:7 + m])

            def activations(i, half, it0, tokens):
                def gelu(jl):
                    act.wait_ge(used, i * 8 + (U_U[half] + 8 * it0 + 4 * (jl + 1)))
                    if half:
                        act.wait_ge(stored, 128)
                    act.activation(arena[:, ds(i * (2 * TOK) + (G + (2 * it0 + jl) * TOK), TOK)], ps[jl][:, 0:TOK],
                                   ACT.Gelu).then_inc(gelu_done, 1)

                def gates(g, tok0):
                    act.wait_ge(gate_ps, i * tokens + (8 + half * TOK + tok0 + 8))
                    act.activation(arena[:, ds(i * (tokens * HALF) + (W + tok0 * HALF), 8 * HALF)], ps[2 + g][:],
                                   ACT.Copy).then_inc(gate_out, 1)

                for r in range(8):
                    if isinstance(i, int):
                        hi(U_U[half] + 8 * (it0 + i) + r + LEAD)
                        peer_queries(N_PQ - 1, r)
                    else:
                        hi_loop(i, 8, U_U[half] + 8 * it0, r + LEAD)
                    if r == 5:
                        gelu(0)
                        if tokens == 16:
                            gates(0, 0)
                gelu(1)
                if tokens:
                    gates(tokens // 16, tokens - 8)

            def coefficient_hi(half, j, parity):
                act.wait_ge(coef, half * HALF + j + 1)
                act.wait_ge(used, U_V[half] + 4 * (j - 1))
                act.activation(c_hi[:, parity], arena[:, ds(j * TOK + G, TOK)], ACT.Copy).then_inc(coef_hi, 1)

            for half in range(2):
                if half == 0:
                    activations(0, 0, 0, 0)
                    with act.Fori(1, PLAIN) as i:
                        activations(i, 0, 0, 0)
                    for m in range(TT):
                        act.wait_ge(gate_in, m + 1)
                        act.activation(pk_gate(m), pk_gate(m), ACT.Exp).then_inc(gate_exp, 1)
                    act.wait_ge(h_saved, 16)
                    with act.Fori(0, ITS - PLAIN) as i:
                        activations(i, 0, PLAIN, TPI[0])
                else:
                    with act.Fori(0, ITS) as i:
                        activations(i, 1, 0, TPI[1])
                coefficient_hi(half, 0, 0)
                with act.Fori(0, ITS - 1) as i:
                    for r in range(8):
                        hi_loop(i, 8, U_V[half], r + LEAD)
                        if r == 1:
                            act.wait_ge(coef, i * 2 + (half * HALF + 2))
                            act.wait_ge(used, i * 8 + U_V[half])
                            act.activation(c_hi[:, 1], arena[:, ds(i * (2 * TOK) + (G + TOK), TOK)], ACT.Copy).then_inc(coef_hi, 1)
                        if r == 5:
                            act.wait_ge(coef, i * 2 + (half * HALF + 3))
                            act.wait_ge(used, i * 8 + (U_V[half] + 4))
                            act.activation(c_hi[:, 0], arena[:, ds(i * (2 * TOK) + (G + 2 * TOK), TOK)], ACT.Copy).then_inc(coef_hi, 1)
                for r in range(8):
                    u = U_V[half] + 8 * (ITS - 1) + r + LEAD
                    if u < U_END:
                        hi(u)
                    if r == 1:
                        coefficient_hi(half, HALF - 1, 1)

        @block.vector
        def _(dve):
            st_ = Steps(dve, dve_step)
            TTT, TS, STT = dve.tensor_tensor, dve.tensor_scalar, dve.scalar_tensor_tensor

            def lo(u):
                if u < U_END:
                    dve.wait_ge(hi_done, u + 1)
                    TTT(w_lo[:, u % 4], raw[:, u % 8 // 2, u % 2], w_hi[:, u % 4].bitcast(F32), ALU.subtract).then_inc(lo_done, 1)

            def lo_loop(i, per, u0, r):
                dve.wait_ge(hi_done, i * per + (u0 + r + 1))
                TTT(w_lo[:, r % 4], raw[:, (r % 8) // 2, r % 2], w_hi[:, r % 4].bitcast(F32), ALU.subtract).then_inc(lo_done, 1)

            def turn_rest(t, j, bank, gain, dhi=a_hi, dlo=a_lo):
                dve.wait_ge(turn_hi[t], j + 1)
                src = ps[bank][:]
                if gain is None:
                    ins = TTT(dlo[:, 2 * j:2 * j + 2, :], src.rearrange("p (a b) -> p a b", a=2),
                              dhi[:, 2 * j:2 * j + 2, :].bitcast(F32), ALU.subtract)
                else:
                    for kk in range(2):
                        k = 2 * j + kk
                        ins = STT(dlo[:, k, :], src[:, kk * TOK:(kk + 1) * TOK], gains[:, gain, k:k + 1],
                                  dhi[:, k, :].bitcast(F32), ALU.mult, ALU.subtract)
                ins.then_inc(turn_out[t], 1)

            def reciprocal_rms(n):
                dve.wait_ge(sums, n + 1)
                dve.reciprocal(rs[:, 2 * n:2 * n + 2], rs[:, 2 * n:2 * n + 2]).then_inc(rstds, 1)

            def spread(v, n):
                return v.unsqueeze(2).to_broadcast([P, v.shape[1], n])

            for u in range(LEAD):
                lo(u)
            for j in range(KC // 2):
                turn_rest("x", j, 4 + j % 4, 0)
            reciprocal_rms(0)
            zv = z[:, :, ZV:ZV + 1024]

            def group_squares(src, out_, width):
                st_.run(TTT(sq.rearrange("p (m c) -> p m c", m=2), src, src, ALU.mult))
                dve.tensor_reduce(out_, sq.rearrange("p (m g c) -> p m g c", m=2, c=width), AX.X, ALU.add).then_inc(grp_sq, 1)

            for b in range(N_IN):
                for r in range(BLK):
                    lo(U_IN + b * BLK + r + LEAD)
                    if b == 2 and r % 2:
                        turn_rest("mem", r // 2, 4 + r // 2 % 4, 1, m_hi, m_lo)
                    if b == 3 and r == 9:
                        reciprocal_rms(1)
                    if b == 3 and r == 11:
                        for c in range(2):
                            dve.tensor_tensor_reduce(lamv[:, 2 * c], lamv[:, 2 * c], lamv[:, 2 * c + 1], 1.0, 0.0,
                                                     ALU.mult, ALU.add, lam[:, c:c + 1]).then_inc(lam_sum, 1)
                        st_.run(TS(subg[:], subg[:], 1.0 - LAM_INIT, None, ALU.mult))
                    if b == 4 and r == 2:
                        dve.wait_ge(evac, 4)
                        dve.wait_ge(toep_out, 16)
                        group_squares(zv, st[:, 0, 0:16], SGU_D)
                    if b == 5 and r == 3:
                        dve.wait_ge(grp_root, 1)
                        st_.run(dve.reciprocal(st[:, 0, 0:16], st[:, 0, 0:16]))
                    if b == 5 and r in (5, 9):
                        m = r // 8
                        v = zv[:, m].rearrange("p (g c) -> p g c", c=SGU_D)
                        st_.run(TTT(v, v, spread(st[:, 0, 8 * m:8 * m + 8], SGU_D), ALU.mult))
                    if b == 5 and r in (7, 11):
                        m = r // 8
                        TTT(zv[:, m], zv[:, m], sgg, ALU.mult).then_inc(vn_ready, 1)
                    if b in (6, 8) and r == 2:
                        n = (b - 6) // 2
                        dve.wait_ge(evac, b)
                        group_squares(z[:, :, ZQ + 1024 * n:ZQ + 1024 * (n + 1)], stg[:, :, 16 * n:16 * n + 16], DIFF_D)
                    if b in (7, 9) and r == 3:
                        n = (b - 7) // 2
                        dve.wait_ge(grp_root, 2 + n)
                        st_.run(dve.reciprocal(stg[:, :, 16 * n:16 * n + 16], stg[:, :, 16 * n:16 * n + 16]))
                    if b == 9 and r == 5:
                        dve.wait_ge(lam_exp, 1)
                        st_.run(TS(lam[:, 5:6], lam[:, 3:4], LAM_INIT, None, ALU.subtract))
                        st_.run(TTT(lam[:, 4:5], lam[:, 5:6], lam[:, 2:3], ALU.subtract))
            dve.wait_ge(evac, N_IN)
            for n in range(4):
                dve.wait_ge(sgu_ps, n + 1)
                for hh in range(4):
                    m, h = n // 2, 4 * (n % 2) + hh
                    u_ = z[:, m, ZU + h * SGU_D:ZU + (h + 1) * SGU_D]
                    ins = STT(u_, ps[4 + n][:, hh * P:(hh + 1) * P], sgb[:, h:h + 1], u_, ALU.add, ALU.mult)
            ins.then_inc(sgu_out, 1)
            dve.wait_ge(masked, 2)
            n0 = st_.n
            with dve.Fori(0, DIFF_H) as i:
                st_.n = i * 10 + n0
                for t in range(2):
                    src = z[:, :, ds(i * P + (ZQ + 1024 * t), P)].rearrange("p m (c d) -> p m c d", c=2)
                    ins = TTT(qk_st[:, 2 * t:2 * t + 2, :].rearrange("p m (c d) -> p m c d", c=2), src,
                              stg[:, :, ds(i * 2 + 16 * t, 2)].unsqueeze(3).to_broadcast([P, TT, 2, DIFF_D]), ALU.mult)
                ins.then_inc(qk_scaled, 1)
                for r in range(BLK):
                    lo_loop(i, BLK, U_CKV, r + LEAD)
                    if r == 2:
                        for qt in range(TT):
                            kn = P * (qt + 1)
                            dve.wait_ge(score_ps, i * 2 + (qt + 1))
                            st_.run(STT(logit[:, qt, :, 0:kn], ps[3 + qt][:, 0:2 * kn].rearrange("p (c k) -> p c k", c=2),
                                        DIFF_D ** -0.5, bias[:, ds(i, 1), TOK - kn:TOK].to_broadcast([P, 2, kn]),
                                        ALU.mult, ALU.add))
                            dve.tensor_reduce(sm[:, 0, 2 * qt:2 * qt + 2], logit[:, qt, :, 0:kn], AX.X, ALU.max,
                                              negate=True).then_inc(logit_ready, 1)
                    if r == 5:
                        for qt in range(TT):
                            kn = P * (qt + 1)
                            s_ = sm[:, 1, 2 * qt:2 * qt + 2]
                            dve.wait_ge(prob_ready, i * 2 + (qt + 1))
                            st_.run(dve.reciprocal(s_, s_))
                            st_.done(TTT(s_[:, 1:2], s_[:, 1:2], lam[:, 4:5], ALU.mult))
                            st_.run(TS(logit[:, qt, 0, 0:kn], logit[:, qt, 0, 0:kn], s_[:, 0:1], None, ALU.mult))
                            STT(logit[:, qt, 0, 0:kn], logit[:, qt, 1, 0:kn], s_[:, 1:2], logit[:, qt, 0, 0:kn],
                                ALU.mult, ALU.add).then_inc(a_ready, 1)
                    if r == 11:
                        dve.wait_ge(o_rms, i + 1)
                        st_.run(dve.reciprocal(sm[:, 1, 8:10], sm[:, 1, 8:10]))
                        st_.run(TTT(o_st, ps[6][:, 0:TOK].rearrange("p (m d) -> p m d", m=TT), spread(sm[:, 1, 8:10], DIFF_V), ALU.mult))
                        TTT(o_st, o_st, subg[:].unsqueeze(1).to_broadcast([P, TT, DIFF_V]), ALU.mult).then_inc(o_ready, 1)
                    if r == 15:
                        dve.wait_ge(turn_hi["mix"], i + 1)
                        TTT(mix_chunks(a_lo, i), ps[7][:].rearrange("p (a b) -> p a b", a=2), mix_chunks(a_hi, i).bitcast(F32),
                            ALU.subtract).then_inc(turn_out["mix"], 1)
            st_.n = n0 + 10 * DIFF_H

            def add_block(u_end, b):
                dve.wait_ge(used, u_end)
                for m in range(TT):
                    v = xh[:, m, b * NB:(b + 1) * NB]
                    ins = TTT(v, ps[2 * (b % 2) + m][:], v, ALU.add)
                ins.then_inc(added, 1)

            def cross(h, r):
                n = slice(2 * h, 2 * h + 2)
                if r == 4:
                    dve.wait_ge(x_rms, h + 1)
                    st_.run(dve.reciprocal(sm[:, 2, n], sm[:, 2, n]))
                    st_.run(TS(sm[:, 2, n], sm[:, 2, n], CROSS_D ** -0.5, None, ALU.mult))
                    dve.wait_ge(x_score, h + 1)
                    st_.run(dve.tensor_reduce(sm[:, 0, n], ps[6][:].rearrange("p (t k) -> p t k", t=2), AX.X, ALU.max, negate=True))
                    TTT(sm[:, 0, n], sm[:, 0, n], sm[:, 2, n], ALU.mult).then_inc(x_max, 1)
                if r == 9:
                    dve.wait_ge(x_prob, h + 1)
                    st_.run(dve.reciprocal(sm[:, 1, n], sm[:, 1, n]))
                    dve.wait_ge(x_o, h + 1)
                    for qt in range(TT):
                        ins = TS(oc[:, qt, h * CROSS_D:(h + 1) * CROSS_D], ps[4 + qt][:], sm[:, 1, 2 * h + qt:2 * h + qt + 1],
                                 None, ALU.mult)
                    ins.then_inc(x_o_out, 1)
                if r == 11:
                    for g in range(2):
                        turn_rest("oc", 2 * h + g, 6 + g, None)

            for b in range(N_OUT):
                for r in range(BLK):
                    lo(U_OUT + b * BLK + r + LEAD)
                    if b and r in (3, 5):
                        turn_rest("h1", 2 * (b - 1) + r // 4, 6 + r // 4, 2, m_hi, m_lo)
                    if b == 0 and r == 1:
                        dve.wait_ge(evac, N_IN + N_CKV)
                    if b == 0 and r in (2, 8):
                        m = r // 8
                        st_.run(TTT(sq, kv[:, m, 0:D], kv[:, m, 0:D], ALU.mult))
                    if b == 0 and r in (5, 11):
                        m = r // 8
                        ins = dve.tensor_reduce(st[:, 0, 4 * m:4 * m + 4], sq.rearrange("p (h c) -> p h c", c=CROSS_D), AX.X, ALU.add)
                        if m == 0:
                            st_.run(ins)
                        else:
                            ins.then_inc(grp_sq, 1)
                    if b == 1 and r == 2:
                        dve.wait_ge(grp_root, 4)
                        st_.run(dve.reciprocal(st[:, 0, 0:8], st[:, 0, 0:8]))
                    if b == 1 and r in (8, 11):
                        m = (r - 8) // 3
                        v = kv[:, m, 0:D].rearrange("p (h c) -> p h c", c=CROSS_D)
                        TTT(v, v, spread(st[:, 0, 4 * m:4 * m + 4], CROSS_D), ALU.mult).then_inc(kc_ready, 1)
                add_block(U_OUT + (b + 1) * BLK, b)
            for b in range(N_CQ):
                for r in range(BLK):
                    lo(U_CQ + b * BLK + r + LEAD)
                    if b == 0:
                        if r in (3, 5):
                            turn_rest("h1", 6 + r // 4, 6 + r // 4, 2, m_hi, m_lo)
                        if r == 13:
                            reciprocal_rms(2)
                    else:
                        cross(b - 1, r)
            for b in range(N_CO):
                for r in range(BLK):
                    lo(U_CO + b * BLK + r + LEAD)
                    if b == 0:
                        cross(CROSS_H - 1, r)
                    elif r in (3, 5):
                        turn_rest("h2", 2 * (b - 1) + r // 4, 6 + r // 4, 3, m_hi, m_lo)
                add_block(U_CO + (b + 1) * BLK, b)

            def top8(n, vals, top, idx):
                t8, i8 = top[:, 8 * n:8 * n + 8], idx[:, 8 * n:8 * n + 8]
                st_.run(dve.max(t8, vals))
                st_.run(dve.max_index(i8, t8, vals))
                if n == 0:
                    st_.run(dve.match_replace(vals, t8, vals, LOW))

            def pick_keys(b, n):
                m, hc = n // 8, 4 * b + n // 2 % 4
                if n % 8 == 0:
                    dve.wait_ge(sc_out, 2 * b + m + 1)
                top8(n % 2, sc[:, m, hc], pk_top[:, m, hc], pk_idx[:, m, hc])

            for b in range(N_PQ):
                for r in range(BLK):
                    lo(U_PQ + b * BLK + r + LEAD)
                    if b == 0:
                        if r in (3, 5):
                            turn_rest("h2", 6 + r // 4, 6 + r // 4, 3, m_hi, m_lo)
                        if r == 13:
                            reciprocal_rms(3)
                            dve.wait_ge(rstds, 4)
                        if r in (14, 15):
                            m = r - 14
                            TS(xn[:, m], xh[:, m], rs[:, 6 + m:7 + m], None, ALU.mult).then_inc(xn_ready, 1)
                    if b == 1 and r % 2:
                        turn_rest("h2n", r // 2, 6 + r // 2 % 2, 3)
                    if b == 2 and r == 0:
                        dve.wait_ge(h_saved, 16)
                    if b == 2:
                        pick_keys(0, r)
                    if b == 3:
                        pick_keys(1, r)

            nxt = [U_U[0] + LEAD]

            def stream(n):
                for _ in range(n):
                    if nxt[0] < U_U[0] + 8 * PLAIN + LEAD:
                        lo(nxt[0])
                        nxt[0] += 1

            def top16(vals, top, idx):
                for n in range(2):
                    top8(n, vals, top, idx)
                    stream(1)

            stream(4)
            for b in (2, 3):
                for n in range(16):
                    pick_keys(b, n)
                    stream(1)
            for m in range(TT):
                st_.run(dve.tensor_copy(pk_idxf[:, m], pk_idx[:, m]))
                tv = pk_top[:, m].rearrange("p (h c) k -> p h c k", c=2)
                fi = pk_idxf[:, m].rearrange("p (h c) k -> p h c k", c=2)
                shape = [P, PH, TOPK, TOPK]
                st_.run(TTT(cand, tv[:, :, 0].unsqueeze(3).to_broadcast(shape), tv[:, :, 1].unsqueeze(2).to_broadcast(shape), ALU.add))
                stream(2)
                for h in range(PH):
                    top16(cand[:, h].rearrange("p a b -> p (a b)"), pk(1536, m)[:, h * TOPK:(h + 1) * TOPK],
                          pk(1792, m).bitcast(U32)[:, h * TOPK:(h + 1) * TOPK])
                pos = pk(1792, m).bitcast(U32)
                st_.done(TS(pk(2048, m).bitcast(U32), pos, 4, None, ALU.logical_shift_right))
                st_.run(TS(pk(2304, m).bitcast(U32), pos, 15, None, ALU.bitwise_and))
                for c in range(2):
                    st_.run(dve.tensor_copy(pk(2560, m), pk(2048 + 256 * c, m).bitcast(U32)))
                    place = pk(2560, m).rearrange("p (h k) -> p h k", h=PH)
                    st_.run(TTT(eq, iota[:, 0:TOPK].unsqueeze(1).unsqueeze(1).to_broadcast(shape),
                                place.unsqueeze(3).to_broadcast(shape), ALU.is_equal))
                    stream(2)
                    st_.run(TTT(eq, eq, fi[:, :, c].unsqueeze(2).to_broadcast(shape), ALU.mult))
                    stream(2)
                    st_.run(dve.tensor_reduce(pk(2816 + 256 * c, m).rearrange("p (h k) -> p h k", h=PH), eq, AX.X, ALU.add))
                    stream(2)
                top = pk(1536, m).rearrange("p (h k) -> p h k", h=PH)
                gate = pk_gate(m).rearrange("p (h k) -> p h k", h=PH)
                TTT(gate, top, top[:, :, 0:1].to_broadcast([P, PH, TOPK]), ALU.subtract).then_inc(gate_in, 1)
            stream(8 * PLAIN)
            for m in range(TT):
                gate = pk_gate(m).rearrange("p (h k) -> p h k", h=PH)
                dve.wait_ge(gate_exp, m + 1)
                st_.run(dve.tensor_reduce(sm[:, m, 0:PH], gate, AX.X, ALU.add))
                st_.run(dve.reciprocal(sm[:, m, 0:PH], sm[:, m, 0:PH]))
                TTT(gate, gate, spread(sm[:, m, 0:PH], TOPK), ALU.mult).then_inc(picks_ready, 1)
            dve.wait_ge(gate_ps, 8)
            for n in range(3):
                st_.done(dve.tensor_copy(pickT[:, n], ps[4 + n][:, 0:TOK]))
            st_.settle()

            def hot_rows(half, i, per, tk):
                s = tk % 8
                dve.wait_ge(gate_ps, i * per + (half * TOK + tk + 1))
                col = ds(i * per + tk, 1)
                TS(hot1[:, s], iota[:], pickT[:, 0, col], pickT[:, 2, col], ALU.is_equal, ALU.mult)
                TS(hot2[:, s], iota[:, HALF * half:HALF * (half + 1)], pickT[:, 1, col], None, ALU.is_equal).then_inc(hot_ready, 1)

            gates_by_key = ar(W, TOK, HALF).rearrange("p t j -> p j t")
            acts = ar(G, HALF, TOK)

            def product(half, j):
                v = acts[:, ds(j, 1), :]
                if isinstance(j, int) and j == 0:
                    dve.wait_ge(gelu_done, (half + 1) * HALF)
                    dve.wait_ge(gate_out, (half + 1) * TOK // 8)
                TTT(v, v, gates_by_key[:, ds(j, 1), :], ALU.mult).then_inc(coef, 1)

            def remainder(half, j, parity):
                dve.wait_ge(coef_hi, j + (half * HALF + 1))
                TTT(c_lo[:, parity:parity + 1], acts[:, ds(j, 1), :], c_hi[:, parity:parity + 1].bitcast(F32),
                    ALU.subtract).then_inc(coef_ready, 1)

            for half in range(2):
                with dve.Fori(0, ITS - PLAIN if half == 0 else ITS) as i:
                    for r in range(8):
                        for n in range(TPI[half] // 8):
                            hot_rows(half, i, TPI[half], r * (TPI[half] // 8) + n)
                        lo_loop(i, 8, U_U[half] + (8 * PLAIN if half == 0 else 0), r + LEAD)
                product(half, 0)
                remainder(half, 0, 0)
                with dve.Fori(0, ITS - 1) as i:
                    for r in range(8):
                        lo_loop(i, 8, U_V[half], r + LEAD)
                        if r % 4 == 0:
                            product(half, i * 2 + (1 + r // 4))
                        if r % 4 == 2:
                            remainder(half, i * 2 + (1 + r // 4), 1 - r // 4)
                for r in range(8):
                    lo(U_V[half] + 8 * (ITS - 1) + r + LEAD)
                    if r == 0:
                        product(half, HALF - 1)
                    if r == 2:
                        remainder(half, HALF - 1, 1)
                dve.wait_ge(res_in, 16 * (half + 1))
                for m in range(TT):
                    for s in range(4):
                        dve.wait_ge(used, U_V[half] + 4 * (HALF - 1) + s + 1)
                        v = res[:, m, s * NB:(s + 1) * NB]
                        TTT(v, ps[4 * m + s][:], v, ALU.add).then_inc(acc_out, 1)

        @block.tensor
        def _(pe):
            def turn(t, j, bank, src):
                for kk in range(2):
                    for m in range(TT):
                        ins = pe.transpose(ps[bank][:, kk * TOK + m * P:kk * TOK + (m + 1) * P], src(m, 2 * j + kk), ident[:])
                ins.then_inc(turned[t], 1)

            def columns_of(v):
                return lambda m, k: v[:, m, k * P:(k + 1) * P]

            def chunk(k, r, bank, ahi, alo):
                for m in range(TT):
                    o, sh, sl = ps[bank + m][:], ahi[:, k, m * P:(m + 1) * P], alo[:, k, m * P:(m + 1) * P]
                    pe.matmul(o, sh, w_hi[:, r % 4], start=(k == 0), stop=False)
                    pe.matmul(o, sh, w_lo[:, r % 4], start=False, stop=False)
                    ins = pe.matmul(o, sl, w_hi[:, r % 4], start=False, stop=(k == KC - 1))
                ins.then_inc(used, 1)
                return ins

            def project(i, u0, per, r, bank, ahi=a_hi, alo=a_lo):
                pe.wait_ge(lo_done, i * per + (u0 + r + 1))
                chunk(r % BLK, r, bank, ahi, alo)

            def two_blocks(i, u0, out_sem, before):
                for r in range(2 * BLK):
                    b = r // BLK
                    if r % BLK == 0:
                        at_least(pe, out_sem, i * 2 + (before + b - 1))
                    project(i, u0, 2 * BLK, r, 2 * b)

            pe.wait_ge(onehot_in, 32)
            pe.matmul(ps[3][0:8, 0:SPITCH], relb, onehot, start=True, stop=True).then_inc(toep_ps, 1)
            pe.wait_ge(consts, 4)
            pe.wait_ge(x_in, 16)
            for j in range(KC // 2):
                at_least(pe, turn_out["x"], j - 3)
                turn("x", j, 4 + j % 4, columns_of(xh))
            pe.wait_ge(toep_sb, 1)

            def block(u0, b, ahi=a_hi, alo=a_lo, before=None, after=None):
                for r in range(BLK):
                    if before:
                        before(r)
                    project(0, u0 + b * BLK, BLK, r, 2 * (b % 2), ahi, alo)
                    if after:
                        after(r)

            def parts_of(t):
                def before(r):
                    if r % 2 == 0:
                        pe.wait_ge(turn_out[t], r // 2 + 1)
                return before

            def memory_turn(r):
                if r % 2 == 0:
                    j = r // 2
                    if j == 0:
                        pe.wait_ge(mem_in, 16)
                    at_least(pe, turn_out["mem"], j - 3)
                    turn("mem", j, 4 + j % 4, columns_of(memr))

            block(U_IN, 0, before=parts_of("x"))
            block(U_IN, 1)
            pe.wait_ge(evac, 1)
            block(U_IN, 2, after=memory_turn)
            pe.wait_ge(evac, 2)
            block(U_IN, 3)
            with pe.Fori(2, N_IN // 2) as i:
                two_blocks(i, U_IN, evac, 0)
            pe.wait_ge(turn_out["mem"], 8)
            pe.wait_ge(masked, 1)
            for n in range(4):
                pe.wait_ge(vn_ready, n // 2 + 1)
                for hh in range(4):
                    m, h = n // 2, 4 * (n % 2) + hh
                    ins = pe.matmul(ps[4 + n][:, hh * P:(hh + 1) * P], wst[:, h], z[:, m, ZV + h * SGU_D:ZV + (h + 1) * SGU_D],
                                    start=True, stop=True)
                ins.then_inc(sgu_ps, 1)
            with pe.Fori(0, DIFF_H) as i:
                pe.wait_ge(qk_scaled, i + 1)
                for n in range(4):
                    ins = pe.transpose(ps[2][:, n * P:(n + 1) * P], qk_st[:, n], ident[:])
                ins.then_inc(qk_turned, 1)
                pe.wait_ge(evac, i + N_IN)
                for r in range(BLK):
                    project(i, U_CKV, BLK, r, 0, m_hi, m_lo)
                    if r == 1:
                        pe.wait_ge(qk_ready, i + 1)
                        for qt in range(TT):
                            kn = P * (qt + 1)
                            for c in range(2):
                                ins = pe.matmul(ps[3 + qt][:, c * kn:(c + 1) * kn], qz[:, c, qt * P:(qt + 1) * P], kz[:, 0:kn],
                                                start=True, stop=True)
                            ins.then_inc(score_ps, 1)
                    if r == 6:
                        for qt in range(TT):
                            pe.wait_ge(a_ready, i * 2 + (qt + 1))
                            for kt in range(qt + 1):
                                ins = pe.transpose(ps[5][:, (qt + kt) * P:(qt + kt + 1) * P], logit[:, qt, 0, kt * P:(kt + 1) * P], ident[:])
                        ins.then_inc(aT_ps, 1)
                    if r == 8:
                        pe.wait_ge(aT_ready, i + 1)
                        for qt in range(TT):
                            for kt in range(qt + 1):
                                ins = pe.matmul(ps[6][:, qt * DIFF_V:(qt + 1) * DIFF_V], aT[:, qt + kt],
                                                z[:, kt, ds(i * DIFF_V + ZVD, DIFF_V)], start=(kt == 0), stop=(kt == qt))
                        ins.then_inc(o_ps, 1)
                    if r == 13:
                        pe.wait_ge(u_staged, i + 1)
                        pe.wait_ge(o_ready, i + 1)
                        for n in range(4):
                            ins = pe.transpose(ps[7][:, n * P:(n + 1) * P], (u_st if n < 2 else o_st)[:, n % 2], ident[:])
                        ins.then_inc(turned["mix"], 1)

            def last_head(r):
                pe.wait_ge(turn_out["mix"], DIFF_H if r == KC - 1 else DIFF_H - 1)

            def residual_turn(t, b):
                def after(r):
                    if r in (2, 4):
                        j = 2 * (b - 1) + r // 4
                        if r == 2:
                            pe.wait_ge(added, (N_OUT if t == "h2" else 0) + b)
                        turn(t, j, 6 + r // 4, columns_of(xh))
                return after

            def keys_turn(r):
                residual_turn("h1", 2)(r)
                if r % 2 == 0:
                    j = r // 2
                    if j == 0:
                        pe.wait_ge(kc_ready, 2)
                    at_least(pe, turn_out["ck"], j - 1)
                    turn("ck", j, 4 + j % 2, columns_of(kv))

            pe.wait_ge(evac, N_IN + N_CKV)
            block(U_OUT, 0, before=last_head)
            block(U_OUT, 1, after=residual_turn("h1", 1))
            pe.wait_ge(added, 1)
            block(U_OUT, 2, after=keys_turn)
            pe.wait_ge(added, 2)
            block(U_OUT, 3, after=residual_turn("h1", 3))

            def cross(h):
                def after(r):
                    if r == 0:
                        pe.wait_ge(evac, N_IN + N_CKV + h + 1)
                        for g in range(2):
                            turn("cq", 2 * h + g, 4 + g, columns_of(cq))
                    if r == 2:
                        pe.wait_ge(turn_out["cq"], 2 * h + 2)
                        pe.wait_ge(turn_out["ck"], 8)
                        for qt in range(TT):
                            for c in range(CH):
                                ins = pe.matmul(ps[6][:, qt * TOK:(qt + 1) * TOK], qT[h % 2][:, c, qt * P:(qt + 1) * P],
                                                kT[:, h * CH + c, :], start=(c == 0), stop=(c == CH - 1))
                        ins.then_inc(x_score, 1)
                    if r == 6:
                        pe.wait_ge(x_prob, h + 1)
                        for qt in range(TT):
                            for mt in range(TT):
                                n = 2 * qt + mt
                                ins = pe.transpose(ps[7][:, n * P:(n + 1) * P], cp[:, h % 2, qt, mt * P:(mt + 1) * P], ident[:])
                        ins.then_inc(x_pT, 1)
                    if r == 8:
                        pe.wait_ge(x_pT_out, h + 1)
                        for qt in range(TT):
                            for mt in range(TT):
                                ins = pe.matmul(ps[4 + qt][:], cpT[:, h % 2, 2 * qt + mt],
                                                kv[:, mt, D + h * CROSS_D:D + (h + 1) * CROSS_D], start=(mt == 0), stop=(mt == 1))
                        ins.then_inc(x_o, 1)
                    if r == 10:
                        pe.wait_ge(x_o_out, h + 1)
                        for g in range(2):
                            turn("oc", 2 * h + g, 6 + g, columns_of(oc))
                return after

            pe.wait_ge(added, 3)
            block(U_CQ, 0, m_hi, m_lo, before=parts_of("h1"), after=residual_turn("h1", 4))
            for b in range(1, N_CQ):
                if b >= 2:
                    pe.wait_ge(evac, N_IN + N_CKV + b - 1)
                block(U_CQ, b, m_hi, m_lo, after=cross(b - 1))
            pe.wait_ge(evac, N_IN + N_CKV + 3)
            block(U_CO, 0, before=parts_of("oc"), after=cross(CROSS_H - 1))
            for b in range(1, N_CO):
                if b >= 2:
                    pe.wait_ge(added, N_OUT + b - 1)
                block(U_CO, b, after=residual_turn("h2", b))

            def peer_queries(b, r):
                if r == 0:
                    pe.wait_ge(evac, N_IN + N_CKV + N_CQ + b + 1)
                    for g in range(2):
                        turn("pq", 2 * b + g, 4 + g, columns_of(pq))
                if r == 3:
                    pe.wait_ge(turn_out["pq"], 2 * b + 2)
                    pe.wait_ge(keys_in, 16)
                    for m in range(TT):
                        for a in range(4):
                            hc = 4 * b + a
                            ins = pe.matmul(ps[4 + m][:, a * NK:(a + 1) * NK], pqT[:, hc, m * P:(m + 1) * P], keysT[:, hc],
                                            start=True, stop=True)
                        ins.then_inc(sc_ps, 1)

            def queries_and_turn(r):
                peer_queries(0, r)
                if r % 2 == 0:
                    j = r // 2
                    if j == 0:
                        pe.wait_ge(xn_ready, 2)
                    at_least(pe, turn_out["h2n"], j - 1)
                    turn("h2n", j, 6 + j % 2, columns_of(xn))

            pe.wait_ge(added, N_OUT + 3)
            block(U_PQ, 0, m_hi, m_lo, before=parts_of("h2"), after=residual_turn("h2", 4))
            block(U_PQ, 1, m_hi, m_lo, after=queries_and_turn)
            for b in (2, 3):
                pe.wait_ge(evac, N_IN + N_CKV + N_CQ + b - 1)
                block(U_PQ, b, m_hi, m_lo, after=lambda r: peer_queries(b - 1, r))
            pe.wait_ge(turn_out["h2n"], 8)
            pe.wait_ge(evac, N_IN + N_CKV + N_CQ + 3)

            def activations(i, half, it0, tokens):
                for r in range(8):
                    jl = r // 4
                    if r % 4 == 0:
                        at_least(pe, gelu_done, i * 2 + (half * HALF + 2 * it0 + jl - 1))
                    pe.wait_ge(lo_done, i * 8 + (U_U[half] + 8 * it0 + r + 1))
                    for dd in range(4):
                        k = 4 * (r % 4) + dd
                        o, uh, ul = ps[jl][:, 0:TOK], w_hi[:, r % 4, dd * P:(dd + 1) * P], w_lo[:, r % 4, dd * P:(dd + 1) * P]
                        pe.matmul(o, uh, a_hi[:, k], start=(k == 0), stop=False)
                        pe.matmul(o, uh, a_lo[:, k], start=False, stop=False)
                        ins = pe.matmul(o, ul, a_hi[:, k], start=False, stop=(k == KC - 1))
                    ins.then_inc(used, 1)
                    if isinstance(i, int) and tokens == 0:
                        peer_queries(N_PQ - 1, r)
                    for n in range(tokens // 8):
                        tk = r * (tokens // 8) + n
                        if tk % 8 == 0:
                            at_least(pe, gate_out, i + 32 if half else i * 2 + (tk // 8 - 1))
                        pe.wait_ge(hot_ready, i * tokens + (half * TOK + tk + 1))
                        pe.matmul(ps[2 + (tk // 8)][:, (tk % 8) * HALF:(tk % 8 + 1) * HALF], hot1[:, tk % 8], hot2[:, tk % 8],
                                  start=True, stop=True).then_inc(gate_ps, 1)

            def outputs(i, half, first, last):
                for r in range(8):
                    j, s = r // 4, r % 4
                    if s == 0:
                        pe.wait_ge(coef_ready, i * 2 + (half * HALF + j + 1))
                    pe.wait_ge(lo_done, i * 8 + (U_V[half] + r + 1))
                    for m in range(TT):
                        o, sh, sl = ps[4 * m + s][:], c_hi[:, j, m * P:(m + 1) * P], c_lo[:, j, m * P:(m + 1) * P]
                        pe.matmul(o, sh, w_hi[:, r % 4], start=first and j == 0, stop=False)
                        pe.matmul(o, sh, w_lo[:, r % 4], start=False, stop=False)
                        ins = pe.matmul(o, sl, w_hi[:, r % 4], start=False, stop=last and j == 1)
                    ins.then_inc(used, 1)

            for half in range(2):
                if half == 0:
                    activations(0, 0, 0, 0)
                    with pe.Fori(1, PLAIN) as i:
                        activations(i, 0, 0, 0)
                    pe.wait_ge(picks_ready, 2)
                    for n, col in enumerate((2816, 3072, 3328)):
                        for m in range(TT):
                            ins = pe.transpose(ps[4 + n][:, m * P:(m + 1) * P], pk(col, m), ident[:])
                    ins.then_inc(gate_ps, 8)
                    activations(0, 0, PLAIN, TPI[0])
                    with pe.Fori(1, ITS - PLAIN) as i:
                        activations(i, 0, PLAIN, TPI[0])
                else:
                    pe.wait_ge(acc_out, 4)
                    with pe.Fori(0, ITS) as i:
                        activations(i, 1, 0, TPI[1])
                    pe.wait_ge(acc_out, 8)
                outputs(0, half, True, False)
                with pe.Fori(1, ITS - 1) as i:
                    outputs(i, half, False, False)
                outputs(ITS - 1, half, False, True)


def kernel(**inputs):
    import numpy as np
    import concourse.bacc as bacc
    from concourse import mybir as _mybir
    from concourse.bass_utils import run_bass_kernel_spmd

    a = {k: np.asarray(v) for k, v in inputs.items()}

    def projection(w):
        n = w.shape[1]
        return w.reshape(KC // 2, 2, P, n // NB, NB).transpose(3, 0, 2, 1, 4).reshape(-1, P, 2 * NB)

    def columns(g):
        return g.reshape(-1, P).T

    dist = np.maximum(2 * P - 1 - np.arange(SPITCH), 0)
    exact = 16
    large = exact + (np.log(np.maximum(dist, 1).astype(np.float32) / exact) / np.float32(np.log(128 / exact)) * (32 - exact)).astype(np.int32)
    bucket = np.where(dist < exact, dist, np.minimum(large, 31))
    onehot = (np.arange(32)[:, None] == bucket[None, :]).astype(np.float32)

    arrays = {
        "x": a["x"][0], "mem": a["mem"][0],
        "w_in": projection(a["w_in"][0]), "w_ckv": projection(a["w_ckv"][0]), "w_out": projection(a["w_out"][0]),
        "w_cq": projection(a["w_cq"][0]), "w_co": projection(a["w_co"][0]), "peer_wq": projection(a["peer_wq"][0]),
        "peer_u": a["peer_u"][0].reshape(NK, NK, 2, 8, P).transpose(1, 2, 4, 3, 0).reshape(2 * NK, P, 8 * NK),
        "peer_v": a["peer_v"][0].reshape(NK, NK, 2, 1024).transpose(1, 2, 0, 3).reshape(2 * NK, NK, 1024),
        "peer_keys": a["peer_keys"][0].reshape(2 * PH, NK, P).transpose(2, 0, 1),
        "mix_g": columns(a["norm_mix_g"][0]), "mem_g": columns(a["norm_mem_g"][0]),
        "cross_g": columns(a["norm_cross_g"][0]), "ffn_g": columns(a["norm_ffn_g"][0]),
        "sgu_g": a["sgu_norm_g"][0].reshape(-1), "sgu_w": a["sgu_w"][0].transpose(2, 0, 1), "sgu_b": a["sgu_b"][0].T,
        "q_g": a["q_norm_g"][0][:, None], "k_g": a["k_norm_g"][0][:, None],
        "lambdas": np.stack([a[n][0] for n in ("lambda_q1", "lambda_k1", "lambda_q2", "lambda_k2")]),
        "subln_g": a["diff_subln_g"][0], "rel_bias": a["rel_bias"], "bucket_of": onehot,
        "cq_g": columns(a["cq_norm_g"][0]), "ck_g": columns(a["ck_norm_g"][0]),
    }
    arrays = {f"in_{k}": np.ascontiguousarray(v) for k, v in arrays.items()}
    nc = bacc.Bacc("TRN2", target_bir_lowering=False, num_devices=1)
    args = {k[3:]: nc.dram_tensor(k, v.shape, _mybir.dt.from_np(v.dtype), kind="ExternalInput").ap() for k, v in arrays.items()}
    out = nc.dram_tensor("out", (TOK, D), _mybir.dt.float32, kind="ExternalOutput").ap()
    hybrid_layer(nc, out=out, **args)
    r = run_bass_kernel_spmd(nc, [arrays], core_ids=[0])
    return r.results[0]["out"].reshape(1, TOK, D)
```

```python
from contextlib import ExitStack

import concourse.bass as bass
from concourse import mybir

ALU = mybir.AluOpType
ACT = mybir.ActivationFunctionType
AX = mybir.AxisListType
F32 = mybir.dt.float32
F32R = mybir.dt.float32r
U32 = mybir.dt.uint32
ds = bass.ds

P = 128
D = 2048
KC = D // P
TT = 2
TOK = TT * P
EPS = 1e-6
NB = 512
SUB = 512
SLOTS = 4
SMALLS = 12
EARLY = 3
FREE = 610
LEAD = 3
SGU_H, SGU_D = 8, 128
DIFF_H, DIFF_D, DIFF_V = 8, 64, 128
CROSS_H = 4
CROSS_D = D // CROSS_H
CH = CROSS_D // P
PH, NK, TOPK = 8, 128, 16
HALF = NK // 2
LAM_INIT = 0.2
NEG = -1.0e30
LOW = -3.0e38

BLK = KC
N_IN, N_CKV, N_OUT, N_CQ, N_CO, N_PQ = 10, 8, 4, 4, 4, 4
U_IN = 0
U_CKV = U_IN + N_IN * BLK
U_OUT = U_CKV + N_CKV * BLK
U_CQ = U_OUT + N_OUT * BLK
U_CO = U_CQ + N_CQ * BLK
U_PQ = U_CO + N_CO * BLK
U_U = [U_PQ + N_PQ * BLK, 0]
U_V = [U_U[0] + HALF * 4, 0]
U_U[1] = U_V[0] + HALF * 4
U_V[1] = U_U[1] + HALF * 4
U_END = U_V[1] + HALF * 4
ITS = HALF // 2
TPI = 16
PLAIN = ITS - TOK // TPI - 1
HOT = 4

Z = 8192
ZW = 5120
ZU, ZV, ZQ, ZK, ZVD = 0, 1024, 2048, 3072, 4096
MEM = 18432
XT = Z + ZW
SG, WS = 22528, 23552
KV = 18432
H = 26624
BI = 30720
KT = 8192
CQ = 12288
QT = 16384
XN = 8192
KEYS = 30720
SC = 18432
PQT = 22528
CAND, EQ = 22528, 24576
PK = 26624
G = 0
W = 16384
R = G + HALF // 2 * TOK
SPITCH = 384


def at_least(eng, sem, value):
    if not isinstance(value, int) or value > 0:
        eng.wait_ge(sem, value)


class Steps:

    def __init__(self, eng, sem):
        self.eng, self.sem, self.n = eng, sem, 0

    def done(self, ins):
        ins.then_inc(self.sem, 1)
        self.n = self.n + 1
        return self.n

    def upto(self, n):
        self.eng.wait_ge(self.sem, n)

    def settle(self):
        self.eng.wait_ge(self.sem, self.n)

    def run(self, ins):
        self.done(ins)
        self.settle()


def hybrid_layer(nc, x, x_cols, mem, mem_cols, w_in, w_ckv, w_out, w_cq, w_co, peer_wq, peer_u, peer_v, peer_keys, mix_g, mem_g,
                 cross_g, ffn_g, sgu_g, sgu_w, sgu_b, q_g, k_g, lambdas, subln_g, rel_bias, bucket_of, cq_g, ck_g, out):
    ctx = ExitStack()
    with ctx:
        def sb(name, shape, dt=F32):
            return ctx.enter_context(nc.sbuf_tensor(name, shape, dt))

        def sem(name):
            return ctx.enter_context(nc.semaphore(name))

        with nc.sbuf_tensor("m_hi", [P, KC, TOK], F32R) as m_hi, nc.sbuf_tensor("m_lo", [P, KC, TOK], F32R) as m_lo:
            pass
        arena = sb("arena", [P, 32768])
        with ExitStack() as late:
            def lsb(name, shape, dt=F32):
                return late.enter_context(nc.sbuf_tensor(name, shape, dt))
            hot1 = lsb("hot1", [P, HOT, NK])
            hot2 = lsb("hot2", [P, HOT, NK])
            pickT = lsb("pickT", [P, 3, TOK])
            with nc.sbuf_tensor("gate_st", [P, 2, 8, HALF], F32) as gate_st:
                pass
            c_hi = lsb("c_hi", [P, 2, TOK], F32R)
            c_lo = lsb("c_lo", [P, 2, TOK], F32R)
        wk = sb("wk", [P, 3328])
        raw = sb("raw", [P, SLOTS, 2, SUB])
        w_hi = sb("w_hi", [P, SLOTS, SUB], F32R)
        w_lo = sb("w_lo", [P, SLOTS, SUB], F32R)
        a_hi = sb("a_hi", [P, KC, TOK], F32R)
        a_lo = sb("a_lo", [P, KC, TOK], F32R)
        ident = sb("ident", [P, P])
        iota = sb("iota", [P, NK])
        gains = sb("gains", [P, 5, KC])
        sgb = sb("sgb", [P, SGU_H])
        qkg = sb("qkg", [P, 2])
        subg = sb("subg", [P, DIFF_V])
        eps = sb("eps", [P, 1])
        ss = sb("ss", [P, 8])
        rs = sb("rs", [P, 8])
        st = sb("st", [P, 2, 64])
        lam = sb("lam", [P, 8])
        sm = sb("sm", [P, 3, 16])

        def ar(col, *dims):
            n = 1
            for d in dims:
                n *= d
            v = arena[:, col:col + n]
            if len(dims) == 2:
                return v.rearrange("p (a b) -> p a b", b=dims[1])
            if len(dims) == 3:
                return v.rearrange("p (a b c) -> p a b c", b=dims[1], c=dims[2])
            return v

        z = ar(Z, TT, ZW)
        xh = ar(H, TT, D)
        xT, memT, memr = ar(XT, KC, TOK), ar(MEM, KC, TOK), ar(MEM, TT, D)
        kv = ar(KV, TT, 2 * D)
        bias = ar(BI, DIFF_H, TOK)
        sgg, wst = ar(SG, SGU_H * SGU_D), ar(WS, SGU_H, P)
        kT = ar(KT, KC, TOK)
        qT = [ar(QT + n * CH * TOK, CH, TOK) for n in range(2)]
        cq, xn = ar(CQ, TT, D), ar(XN, TT, D)
        keysT, sc = ar(KEYS, 2 * PH, NK), ar(SC, TT, 2 * PH, NK)
        pqT = ar(PQT, KC, TOK)
        cand, eq = ar(CAND, PH, TOPK, TOPK), ar(EQ, PH, TOPK, TOPK)
        res = ar(R, TT, D)
        pk_top, pk_idxf = ar(PK, TT, 2 * PH, TOPK), ar(PK + 1024, TT, 2 * PH, TOPK)
        pk_idx = ar(PK + 512, TT, 2 * PH, TOPK).bitcast(U32)

        def mix_chunks(a, i):
            return a[:].rearrange("p (s h) t -> p s h t", s=2)[:, :, ds(i, 1), :].rearrange("p s o t -> p s (o t)")

        def pk(col, m):
            return arena[:, PK + col + P * m:PK + col + P * (m + 1)]

        def pk_gate(m):
            return pk(3328, m)

        stg = st[:, 1, :].rearrange("p (m g) -> p m g", m=TT)
        sq = wk[:, 0:2048]
        qk_st = wk[:, 0:512].rearrange("p (a b) -> p a b", a=4)
        logit = wk[:, 512:1536].rearrange("p (a c k) -> p a c k", a=2, c=2)
        aT = wk[:, 1536:1920].rearrange("p (a b) -> p a b", a=3)
        qz = wk[:, 2048:2560].rearrange("p (c t) -> p c t", c=2)
        kz = wk[:, 2560:2816]
        o_st = wk[:, 0:256].rearrange("p (m d) -> p m d", m=2)
        u_st = wk[:, 3072:3328].rearrange("p (m d) -> p m d", m=2)
        junk = wk[:, 1920:2048]
        lamv = wk[:, 2816:3072].rearrange("p (a b) -> p a b", a=4)
        cp = wk[:, 0:1024].rearrange("p (b t m) -> p b t m", b=2, t=2)
        cpT = wk[:, 1024:2048].rearrange("p (b n q) -> p b n q", b=2, q=P)
        onehot = wk[0:32, 0:SPITCH]
        relb = wk[0:32, 400:408]
        toep = wk[0:8, 512:512 + SPITCH]

        ps = [ctx.enter_context(nc.psum_tensor(f"ps{i}", [P, 512], F32)) for i in range(8)]

        raw_in = [sem(f"raw_in{s}") for s in range(SLOTS)]
        hi_done = sem("hi_done")
        lo_done = sem("lo_done")
        used = sem("used")
        evac = sem("evac")
        added = sem("added")
        TURNS = ("x", "mem", "mix", "h1", "ck", "cq", "oc", "h2", "h2n")
        turned = {t: sem(f"turned_{t}") for t in TURNS}
        turn_hi = {t: sem(f"turn_hi_{t}") for t in TURNS}
        turn_out = {t: sem(f"turn_out_{t}") for t in TURNS}
        sums = sem("sums")
        rstds = sem("rstds")
        xT_in = [sem(f"xT_in{s}") for s in range(SLOTS)]
        x_in, memT_in = sem("x_in"), sem("memT_in")
        gain_in, mem_in, small_in = sem("gain_in"), sem("mem_in"), sem("small_in")
        sgg_in, wst_in = sem("sgg_in"), sem("wst_in")
        onehot_in = sem("onehot_in")
        consts = sem("consts")
        masked = sem("masked")
        toep_ps, toep_sb, toep_out, bias_in = sem("toep_ps"), sem("toep_sb"), sem("toep_out"), sem("bias_in")
        dve_step, act_step, pool_step = sem("dve_step"), sem("act_step"), sem("pool_step")
        grp_sq, grp_root = sem("grp_sq"), sem("grp_root")
        lam_sum, lam_exp = sem("lam_sum"), sem("lam_exp")
        vn_ready, sgu_ps = sem("vn_ready"), sem("sgu_ps")
        qk_scaled, qk_turned, qk_ready = sem("qk_scaled"), sem("qk_turned"), sem("qk_ready")
        score_ps, logit_ready, prob_ready = sem("score_ps"), sem("logit_ready"), sem("prob_ready")
        a_ready, aT_ps, aT_ready = sem("a_ready"), sem("aT_ps"), sem("aT_ready")
        o_ps, o_rms, o_ready = sem("o_ps"), sem("o_rms"), sem("o_ready")
        sgu_out, u_staged = sem("sgu_out"), sem("u_staged")
        kc_ready, x_rms = sem("kc_ready"), sem("x_rms")
        x_score, x_max, x_prob, x_rsum = sem("x_score"), sem("x_max"), sem("x_prob"), sem("x_rsum")
        x_norm, x_pT, x_pT_out = sem("x_norm"), sem("x_pT"), sem("x_pT_out")
        xn_ready = sem("xn_ready")
        keys_in, h_saved = sem("keys_in"), sem("h_saved")
        sc_ps, sc_out = sem("sc_ps"), sem("sc_out")
        gate_in, gate_exp, picks_ready = sem("gate_in"), sem("gate_exp"), sem("picks_ready")
        gelu_done = sem("gelu_done")
        hot_ready, gate_ps, gate_out = sem("hot_ready"), sem("gate_ps"), sem("gate_out")
        gates_saved = [sem(f"gates_saved{b}") for b in range(2)]
        gates_back = sem("gates_back")
        coef, coef_hi, coef_ready = sem("coef"), sem("coef_hi"), sem("coef_ready")
        acc_out, res_in, stored = sem("acc_out"), sem("res_in"), sem("stored")
        finished = sem("finished")

        scratch = nc.dram_tensor("toeplitz_rows", [DIFF_H, SPITCH], F32, kind="Internal").ap()
        shifted = nc.dram_tensor("toeplitz_copies", [DIFF_H, P, SPITCH], F32, kind="Internal").ap()
        later_gates = nc.dram_tensor("later_gates", [P, TOK * HALF], F32, kind="Internal").ap()
        x_t = x.rearrange("(t p) d -> p t d", p=P)
        mem_t = mem.rearrange("(t p) d -> p t d", p=P)
        out_t = out.rearrange("(t p) d -> p t d", p=P)

        block = ctx.enter_context(nc.Block())

        @block.sync
        def _(sp):
            def tile(u, src, row):
                s = (u // 2) % SLOTS
                if u >= 2 * SLOTS:
                    sp.wait_ge(lo_done, u - 2 * SLOTS + 2)
                sp.dma_start(raw[:, s], src[row].rearrange("p (a n) -> p a n", a=2)).then_inc(raw_in[s], 16)

            def tiles(u0, src, row0, count):
                with sp.Fori(0, count // SLOTS) as i:
                    for s in range(SLOTS):
                        sp.wait_ge(lo_done, i * (2 * SLOTS) + (u0 + 2 * s - 2 * SLOTS + 2))
                        sp.dma_start(raw[:, s], src[ds(i * SLOTS + (row0 + s), 1)]
                                     .rearrange("o p (a n) -> p (o a) n", a=2)).then_inc(raw_in[s], 16)

            sp.dma_start(gains[:, 0, :], mix_g).then_inc(gain_in, 16)
            for s in range(SLOTS):
                sp.dma_start(xT[:, 4 * s:4 * s + 4], x_cols[:, 4 * s:4 * s + 4]).then_inc(xT_in[s], 16)
                tile(2 * s, w_in, s)
            sp.dma_start(onehot, bucket_of).then_inc(onehot_in, 16)
            sp.dma_start(relb, rel_bias).then_inc(onehot_in, 16)
            for col, g in enumerate((mem_g, cross_g, ffn_g)):
                sp.dma_start(gains[:, col + 1, :], g).then_inc(small_in, 16)
            sp.dma_start(gains[:, 4, 0:4], cq_g).then_inc(small_in, 16)
            sp.dma_start(gains[:, 4, 4:8], ck_g).then_inc(small_in, 16)
            sp.dma_start(sgb[:], sgu_b).then_inc(small_in, 16)
            for c in range(2):
                sp.dma_start(qkg[64 * c:64 * c + 64, 0:1], q_g).then_inc(small_in, 16)
                sp.dma_start(qkg[64 * c:64 * c + 64, 1:2], k_g).then_inc(small_in, 16)
            sp.dma_start(subg[:], subln_g.partition_broadcast(P)).then_inc(small_in, 16)
            sp.dma_start(lamv, lambdas.partition_broadcast(P)).then_inc(small_in, 16)
            tiles(2 * SLOTS, w_in, SLOTS, N_IN * BLK // 2 - SLOTS)
            tiles(U_CKV, w_ckv, 0, N_CKV * BLK // 2)
            tiles(U_OUT, w_out, 0, N_OUT * BLK // 2)
            sp.wait_ge(logit_ready, 2 * DIFF_H)
            sp.dma_start(keysT, peer_keys).then_inc(keys_in, 16)
            tiles(U_CQ, w_cq, 0, N_CQ * BLK // 2)
            tiles(U_CO, w_co, 0, N_CO * BLK // 2)
            tiles(U_PQ, peer_wq, 0, N_PQ * BLK // 2)
            for half in range(2):
                tiles(U_U[half], peer_u, half * HALF * 2, HALF * 2)
                tiles(U_V[half], peer_v, half * HALF * 2, HALF * 2)
            for n in range(8):
                s, m = n // 2, n % 2
                sp.wait_ge(acc_out, 8 + n + 1)
                sp.dma_start(out_t[:, m, s * NB:(s + 1) * NB], res[:, m, s * NB:(s + 1) * NB]).then_inc(finished, 16)
            sp.wait_ge(finished, 8 * 16)

        @block.gpsimd
        def _(pool):
            g = Steps(pool, pool_step)
            g.run(pool.memset(ident[:], 0.0))
            pool.affine_select(out=ident[:], in_=ident[:], compare_op=ALU.not_equal, fill=1.0, base=0,
                               pattern=[[-1, P]], channel_multiplier=1).then_inc(consts, 1)
            pool.iota(iota[:], pattern=[[1, NK]], base=0, channel_multiplier=0,
                      allow_small_or_imprecise_dtypes=True).then_inc(consts, 1)
            pool.memset(eps[:], EPS).then_inc(consts, 1)
            pool.memset(qz, 0.0).then_inc(consts, 1)
            def quarters(dst, src, arrived, first):
                for n in range(4):
                    pool.wait_ge(used, first + 3 * n)
                    pool.dma_start(dst(n), src(n)).then_inc(arrived, 16)

            quarters(lambda n: xh[:, :, n * NB:(n + 1) * NB], lambda n: x_t[:, :, n * NB:(n + 1) * NB], x_in, 3)
            quarters(lambda n: memT[:, 4 * n:4 * n + 4], lambda n: mem_cols[:, 4 * n:4 * n + 4], memT_in, 15)
            pool.wait_ge(used, 27)
            pool.dma_start(sgg, sgu_g.partition_broadcast(P)).then_inc(sgg_in, 16)
            pool.wait_ge(used, 31)
            pool.dma_start(wst, sgu_w).then_inc(wst_in, 16)
            pool.wait_ge(wst_in, 16)
            pool.affine_select(out=wst, in_=wst, compare_op=ALU.is_ge, fill=0.0, base=0,
                               pattern=[[0, SGU_H], [1, P]], channel_multiplier=-1).then_inc(masked, 1)
            pool.wait_ge(turn_out["mem"], 8)
            quarters(lambda n: memr[:, :, n * NB:(n + 1) * NB], lambda n: mem_t[:, :, n * NB:(n + 1) * NB], mem_in, 3 * BLK + 1)
            pool.wait_ge(toep_sb, 1)
            pool.dma_start(scratch, toep).then_inc(toep_out, 16)
            pool.wait_ge(toep_out, 16)
            pool.dma_start(shifted, scratch.unsqueeze(1).to_broadcast([DIFF_H, P, SPITCH])).then_inc(toep_out, 16)
            pool.wait_ge(toep_out, 32)
            pool.dma_start(bias, bass.AP(tensor=shifted.tensor, offset=P - 1,
                                         ap=[[SPITCH - 1, P], [P * SPITCH, DIFF_H], [1, TOK]])).then_inc(bias_in, 16)
            pool.wait_ge(bias_in, 16)
            pool.affine_select(out=bias, in_=bias, compare_op=ALU.is_ge, fill=NEG, base=P,
                               pattern=[[0, DIFF_H], [-1, TOK]], channel_multiplier=1).then_inc(masked, 1)
            pool.wait_ge(sgu_out, 1)
            with pool.Fori(0, DIFF_H) as i:
                pool.wait_ge(qk_turned, i + 1)
                pool.tensor_copy(u_st, z[:, :, ds(i * P + ZU, P)]).then_inc(u_staged, 1)
            pool.wait_ge(added, N_OUT + N_CO)
            pool.dma_start(out_t, xh).then_inc(h_saved, 16)
            pool.wait_ge(h_saved, 16)
            with pool.Fori(0, TOK // TPI) as i:
                for b in range(2):
                    pool.wait_ge(gate_out, i * 4 + (2 * b + 2))
                    pool.dma_start(later_gates[:, ds(i * (TPI * HALF) + 8 * b * HALF, 8 * HALF)],
                                   gate_st[:, b].rearrange("p a b -> p (a b)")).then_inc(gates_saved[b], 16)
            for half in range(2):
                if half:
                    pool.wait_ge(coef, HALF)
                    for b in range(2):
                        pool.wait_ge(gates_saved[b], 16 * TOK // TPI)
                    with pool.Fori(0, TOK // TPI) as i:
                        pool.wait_ge(used, i * 8 + U_U[1])
                        pool.dma_start(arena[:, ds(i * (TPI * HALF) + W, TPI * HALF)],
                                       later_gates[:, ds(i * (TPI * HALF), TPI * HALF)]).then_inc(gates_back, 16)
                pool.wait_ge(coef_ready, half * HALF + HALF // 2 + 16)
                pool.dma_start(res, out_t).then_inc(res_in, 16)
                if half == 0:
                    for n in range(8):
                        s, m = n // 2, n % 2
                        pool.wait_ge(acc_out, n + 1)
                        pool.dma_start(out_t[:, m, s * NB:(s + 1) * NB], res[:, m, s * NB:(s + 1) * NB]).then_inc(stored, 16)
                    pool.wait_ge(stored, 8 * 16)

        @block.scalar
        def _(act):
            st_ = Steps(act, act_step)

            def hi(u):
                act.wait_ge(raw_in[u % 8 // 2], 16 * (u // 8 + 1))
                at_least(act, used, u - 3)
                act.activation(w_hi[:, u % 4], raw[:, u % 8 // 2, u % 2], ACT.Copy).then_inc(hi_done, 1)

            def hi_loop(i, per, u0, r):
                s = (r % 8) // 2
                act.wait_ge(raw_in[s], i * (2 * per) + 16 * ((u0 + r) // 8 + 1))
                act.wait_ge(used, i * per + (u0 + r - 3))
                act.activation(w_hi[:, r % 4], raw[:, s, r % 2], ACT.Copy).then_inc(hi_done, 1)

            def copy_block(u_end, parity, dst, scale, func=ACT.Copy):
                act.wait_ge(used, u_end)
                for m in range(TT):
                    ins = act.activation(dst(m), ps[2 * parity + m][:], func, scale=scale(m))
                ins.then_inc(evac, 1)

            def turn_part(t, j, bank, gain, dst=a_hi):
                act.wait_ge(turned[t], j + 1)
                if gain is None:
                    ins = act.activation(dst[:, 2 * j:2 * j + 2, :], ps[bank][:].rearrange("p (a b) -> p a b", a=2), ACT.Copy)
                else:
                    for kk in range(2):
                        k = 2 * j + kk
                        ins = act.activation(dst[:, k, :], ps[bank][:, kk * TOK:(kk + 1) * TOK], ACT.Copy,
                                             scale=gains[:, gain, k:k + 1])
                ins.then_inc(turn_hi[t], 1)

            def split_high(t, j, src, gain, dst):
                for k in (2 * j, 2 * j + 1):
                    ins = act.activation(dst[:, k, :], src[:, k, :], ACT.Copy, scale=gains[:, gain, k:k + 1])
                ins.then_inc(turn_hi[t], 1)

            def split_x(j):
                if j % 2 == 0:
                    act.wait_ge(xT_in[j // 2], 16)
                split_high("x", j, xT, 0, a_hi)

            def turn_whole(t, j, bank, dst, gain):
                act.wait_ge(turned[t], j + 1)
                for kk in range(2):
                    ins = act.activation(dst(kk), ps[bank][:, kk * TOK:(kk + 1) * TOK], ACT.Copy, scale=gain(kk))
                ins.then_inc(turn_out[t], 1)

            def square(n, m, src, junk_):
                st_.run(act.activation(junk_, src[:, m], ACT.Square, accum_out=ss[:, 2 * n + m:2 * n + m + 1]))

            def root(n):
                act.activation(rs[:, 2 * n:2 * n + 2], ss[:, 2 * n:2 * n + 2], ACT.Sqrt, bias=eps[:, 0:1],
                               scale=1.0 / D).then_inc(sums, 1)

            act.wait_ge(consts, 4)
            act.activation(sm[:, 2, 14:15], eps[:], ACT.Copy)
            act.wait_ge(gain_in, 16)
            for u in range(LEAD):
                if u < 2:
                    split_x(u)
                hi(u)
            def copy_input(b):
                copy_block(U_IN + (b + 1) * BLK, b % 2, lambda m: z[:, m, b * NB:(b + 1) * NB], lambda m: rs[:, m:m + 1],
                           ACT.Gelu if b < 4 else ACT.Copy)

            for b in range(N_IN):
                for r in range(BLK):
                    hi(U_IN + b * BLK + r + LEAD)
                    if b == 0 and r % 2 == 0 and 2 <= r <= 12:
                        split_x(r // 2 + 1)
                    if b == 1 and r in (0, 2):
                        if r == 0:
                            act.wait_ge(x_in, 64)
                        square(0, r // 2, xh, z[:, 0, 0:D])
                    if b == 1 and r == 4:
                        root(0)
                    if b == 1 and r == 6:
                        act.wait_ge(rstds, 1)
                        copy_input(0)
                    if b == 1 and r == 8:
                        act.wait_ge(small_in, 16 * SMALLS)
                        act.wait_ge(toep_ps, 1)
                        act.activation(toep, ps[7][0:8, 0:SPITCH], ACT.Copy).then_inc(toep_sb, 1)
                    if b == 2 and r % 2:
                        if r == 1:
                            act.wait_ge(memT_in, 64)
                        split_high("mem", r // 2, memT, 1, m_hi)
                    if b == 4 and r in (2, 5):
                        act.wait_ge(mem_in, 64)
                        square(1, r // 4, memr, ar(MEM + 6144, D))
                    if b == 5 and r == 2:
                        root(1)
                    if b == 5 and r == 0:
                        act.wait_ge(grp_sq, 1)
                        act.activation(st[:, 0, 0:16], st[:, 0, 0:16], ACT.Sqrt, bias=eps[:, 0:1],
                                       scale=1.0 / SGU_D).then_inc(grp_root, 1)
                    if b in (7, 9) and r == 0:
                        n = (b - 7) // 2
                        act.wait_ge(grp_sq, 2 + n)
                        act.activation(stg[:, :, 16 * n:16 * n + 16], stg[:, :, 16 * n:16 * n + 16], ACT.Sqrt,
                                       bias=eps[:, 0:1], scale=1.0 / DIFF_D).then_inc(grp_root, 1)
                    if b == 6 and r == 2:
                        act.wait_ge(lam_sum, 2)
                        act.activation(lam[:, 2:4], lam[:, 0:2], ACT.Exp).then_inc(lam_exp, 1)
                if b:
                    copy_input(b)
            act_n0 = st_.n

            def head(i, odd):
                h = i * 2 + odd
                st_.n = i * 4 + (2 * odd + act_n0)
                for r in range(BLK):
                    hi_loop(i, 2 * BLK, U_CKV, odd * BLK + r + LEAD)
                    if r == 1:
                        act.wait_ge(qk_turned, h + 1)
                        for c in range(2):
                            rows = slice(64 * c, 64 * c + 64)
                            act.activation(qz[rows, c], ps[4][rows, 0:TOK], ACT.Copy, scale=qkg[rows, 0:1])
                        act.activation(kz, ps[4][:, TOK:2 * TOK], ACT.Copy, scale=qkg[:, 1:2]).then_inc(qk_ready, 1)
                    if r == 2:
                        act.activation(sm[:, 2, 15:16], eps[:], ACT.Exp)
                    if r == 4:
                        for qt in range(TT):
                            kn = P * (qt + 1)
                            act.wait_ge(logit_ready, i * 4 + (2 * odd + qt + 1))
                            for c in range(2):
                                ins = act.activation(logit[:, qt, c, 0:kn], logit[:, qt, c, 0:kn], ACT.Exp,
                                                     bias=sm[:, 0, 2 * qt + c:2 * qt + c + 1],
                                                     accum_out=sm[:, 1, 2 * qt + c:2 * qt + c + 1])
                            ins.then_inc(prob_ready, 1)
                    if r == 9:
                        act.wait_ge(aT_ps, h + 1)
                        act.activation(aT, ps[4][:, 0:3 * P].rearrange("p (a b) -> p a b", a=3), ACT.Copy).then_inc(aT_ready, 1)
                    if r == 11:
                        act.wait_ge(o_ps, h + 1)
                        for m in range(TT):
                            st_.run(act.activation(junk, ps[5][:, m * DIFF_V:(m + 1) * DIFF_V], ACT.Square,
                                                   accum_out=sm[:, 1, 8 + m:9 + m]))
                        act.activation(sm[:, 1, 8:10], sm[:, 1, 8:10], ACT.Sqrt, bias=eps[:, 0:1],
                                       scale=1.0 / DIFF_V).then_inc(o_rms, 1)
                    if r == 15:
                        act.wait_ge(turned["mix"], h + 1)
                        act.activation(mix_chunks(a_hi, h), ps[7][:].rearrange("p (a b) -> p a b", a=2),
                                       ACT.Copy).then_inc(turn_hi["mix"], 1)
                copy_block(i * (2 * BLK) + (U_CKV + (odd + 1) * BLK), odd, lambda m: kv[:, m, ds(h * NB, NB)],
                           lambda m: rs[:, 2 + m:3 + m])

            with act.Fori(0, DIFF_H // 2) as i:
                for odd in range(2):
                    head(i, odd)
            st_.n = act_n0 + 2 * DIFF_H

            def cross(h, r):
                if r == 1:
                    for g in range(2):
                        turn_whole("cq", 2 * h + g, 4 + g, lambda kk: qT[h % 2][:, 2 * g + kk],
                                   lambda kk: gains[:, 4, 2 * g + kk:2 * g + kk + 1])
                if r == 2:
                    for m in range(TT):
                        st_.run(act.activation(wk[:, 2048:2560], cq[:, m, h * CROSS_D:(h + 1) * CROSS_D], ACT.Square,
                                               accum_out=sm[:, 2, 2 * h + m:2 * h + m + 1]))
                    act.activation(sm[:, 2, 2 * h:2 * h + 2], sm[:, 2, 2 * h:2 * h + 2], ACT.Sqrt, bias=eps[:, 0:1],
                                   scale=1.0 / CROSS_D).then_inc(x_rms, 1)
                if r == 3:
                    act.activation(sm[:, 2, 15:16], eps[:], ACT.Exp)
                if r == 5:
                    act.wait_ge(x_max, h + 1)
                    for qt in range(TT):
                        n = 2 * h + qt
                        ins = act.activation(cp[:, h % 2, qt], ps[6][:, qt * TOK:(qt + 1) * TOK], ACT.Exp,
                                             bias=sm[:, 0, n:n + 1], scale=sm[:, 2, n:n + 1], accum_out=sm[:, 1, n:n + 1])
                    ins.then_inc(x_prob, 1)
                if r == 9:
                    act.wait_ge(x_pT, h + 1)
                    act.activation(cpT[:, h % 2], ps[7][:].rearrange("p (n q) -> p n q", q=P), ACT.Copy).then_inc(x_pT_out, 1)
                if r == 11:
                    for g in range(2):
                        turn_part("oc", 2 * h + g, 4 + g, None)

            for b in range(N_OUT):
                for r in range(BLK):
                    hi(U_OUT + b * BLK + r + LEAD)
                    if b and r in (3, 5):
                        turn_part("h1", 2 * (b - 1) + r // 4, 6 + r // 4, 2, m_hi)
                    if b == 1 and r == 0:
                        act.wait_ge(grp_sq, 4)
                        act.activation(st[:, 0, 0:8], st[:, 0, 0:8], ACT.Sqrt, bias=eps[:, 0:1],
                                       scale=1.0 / CROSS_D).then_inc(grp_root, 1)
                    if b == 2 and r % 2:
                        j = r // 2
                        turn_whole("ck", j, 4 + j % 2, lambda kk: kT[:, 2 * j + kk],
                                   lambda kk: gains[:, 4, 4 + (2 * j + kk) % CH:5 + (2 * j + kk) % CH])
            for b in range(N_CQ):
                for r in range(BLK):
                    hi(U_CQ + b * BLK + r + LEAD)
                    if b == 0:
                        if r in (3, 5):
                            turn_part("h1", 6 + r // 4, 6 + r // 4, 2, m_hi)
                        if r in (7, 9):
                            act.wait_ge(added, N_OUT)
                            square(2, (r - 7) // 2, xh, ar(QT, D))
                        if r == 11:
                            root(2)
                    else:
                        cross(b - 1, r)
                if b == 0:
                    act.wait_ge(rstds, 3)
                copy_block(U_CQ + (b + 1) * BLK, b % 2, lambda m: cq[:, m, b * NB:(b + 1) * NB], lambda m: rs[:, 4 + m:5 + m])
            for b in range(N_CO):
                for r in range(BLK):
                    hi(U_CO + b * BLK + r + LEAD)
                    if b == 0:
                        cross(CROSS_H - 1, r)
                    elif r in (3, 5):
                        turn_part("h2", 2 * (b - 1) + r // 4, 6 + r // 4, 3, m_hi)

            def peer_queries(b, r):
                if r == 4:
                    if b == 0:
                        act.wait_ge(rstds, 4)
                    for m in range(TT):
                        act.wait_ge(sc_ps, 2 * b + m + 1)
                        act.activation(sc[:, m, 4 * b:4 * b + 4], ps[4 + m][:].rearrange("p (a k) -> p a k", k=NK),
                                       ACT.Copy, scale=rs[:, 6 + m:7 + m]).then_inc(sc_out, 1)

            for b in range(N_PQ):
                for r in range(BLK):
                    hi(U_PQ + b * BLK + r + LEAD)
                    if b == 0:
                        if r in (3, 5):
                            turn_part("h2", 6 + r // 4, 6 + r // 4, 3, m_hi)
                        if r in (7, 9):
                            act.wait_ge(added, N_OUT + N_CO)
                            square(3, (r - 7) // 2, xh, ar(QT, D))
                        if r == 11:
                            root(3)
                    else:
                        peer_queries(b - 1, r)
                    if b == 1 and r % 2:
                        turn_part("h2n", r // 2, 6 + r // 2 % 2, 3)
                act.wait_ge(used, U_PQ + (b + 1) * BLK)
                for g in range(2):
                    c = 4 * b + 2 * g
                    ins = act.activation(pqT[:, c:c + 2], ps[2 * (b % 2) + g][:].rearrange("p (c t) -> p c t", c=2), ACT.Copy)
                ins.then_inc(evac, 1)

            def activations(i, half, it0, tokens, after=None):
                def gelu(jl):
                    act.wait_ge(used, i * 8 + (U_U[half] + 8 * it0 + 4 * (jl + 1)))
                    act.activation(arena[:, ds(i * (2 * TOK) + (G + (2 * it0 + jl) * TOK), TOK)], ps[jl][:, 0:TOK],
                                   ACT.Gelu).then_inc(gelu_done, 1)

                def gates(g):
                    act.wait_ge(gate_ps, i * TPI + (HOT + HOT * (g + 1)))
                    at_least(act, gates_saved[g // 2], i * 16)
                    src = ps[2 + g][:].rearrange("p (t j) -> p t j", j=NK)
                    act.activation(arena[:, ds(i * (TPI * HALF) + (W + HOT * g * HALF), HOT * HALF)]
                                   .rearrange("p (t j) -> p t j", j=HALF), src[:, :, 0:HALF], ACT.Copy)
                    act.activation(gate_st[:, g // 2, HOT * (g % 2):HOT * (g % 2 + 1), :], src[:, :, HALF:NK],
                                   ACT.Copy).then_inc(gate_out, 1)

                for r in range(8):
                    if isinstance(i, int):
                        hi(U_U[half] + 8 * (it0 + i) + r + LEAD)
                    else:
                        hi_loop(i, 8, U_U[half] + 8 * it0, r + LEAD)
                    if after:
                        after(r)
                    if r == 5:
                        gelu(0)
                    if tokens and r in (3, 5, 7):
                        gates(r // 2 - 1)
                gelu(1)
                if tokens:
                    gates(3)

            def coefficient_hi(half, j, parity):
                act.wait_ge(coef, half * HALF + j + 1)
                if half == 0 and j == 0:
                    for b in range(2):
                        act.wait_ge(gates_saved[b], 16 * TOK // TPI)
                act.wait_ge(used, U_V[half] + 4 * (j - 1) if j else U_U[half])
                act.activation(c_hi[:, parity], arena[:, ds(j * TOK + G, TOK)], ACT.Copy).then_inc(coef_hi, 1)

            def gate_exponentials(r):
                if r == 1:
                    for m in range(TT):
                        act.wait_ge(gate_in, m + 1)
                        act.activation(pk_gate(m), pk_gate(m), ACT.Exp).then_inc(gate_exp, 1)

            for half in range(2):
                if half == 0:
                    activations(0, 0, 0, 0, after=lambda r: peer_queries(N_PQ - 1, r))
                    with act.Fori(1, PLAIN - 1) as i:
                        activations(i, 0, 0, 0)
                    activations(PLAIN - 1, 0, 0, 0, after=gate_exponentials)
                    act.wait_ge(h_saved, 16)
                    activations(0, 0, PLAIN, TPI)
                    with act.Fori(1, TOK // TPI) as i:
                        activations(i, 0, PLAIN, TPI)
                else:
                    with act.Fori(0, ITS // 2) as i:
                        activations(i, 1, 0, 0)
                    act.wait_ge(stored, 128)
                    with act.Fori(ITS // 2, ITS - 1) as i:
                        activations(i, 1, 0, 0)
                activations(ITS - 1, half, 0, 0, after=lambda r: coefficient_hi(half, 0, 0) if r == 4 else None)
                with act.Fori(0, ITS - 1) as i:
                    for r in range(8):
                        hi_loop(i, 8, U_V[half], r + LEAD)
                        if r == 1:
                            act.wait_ge(coef, i * 2 + (half * HALF + 2))
                            act.wait_ge(used, i * 8 + U_V[half])
                            act.activation(c_hi[:, 1], arena[:, ds(i * (2 * TOK) + (G + TOK), TOK)], ACT.Copy).then_inc(coef_hi, 1)
                        if r == 5:
                            act.wait_ge(coef, i * 2 + (half * HALF + 3))
                            act.wait_ge(used, i * 8 + (U_V[half] + 4))
                            act.activation(c_hi[:, 0], arena[:, ds(i * (2 * TOK) + (G + 2 * TOK), TOK)], ACT.Copy).then_inc(coef_hi, 1)
                for r in range(8):
                    u = U_V[half] + 8 * (ITS - 1) + r + LEAD
                    if u < U_END:
                        hi(u)
                    if r == 1:
                        coefficient_hi(half, HALF - 1, 1)

        @block.vector
        def _(dve):
            st_ = Steps(dve, dve_step)
            TTT, TS, STT = dve.tensor_tensor, dve.tensor_scalar, dve.scalar_tensor_tensor

            def lo(u):
                if u < U_END:
                    dve.wait_ge(hi_done, u + 1)
                    TTT(w_lo[:, u % 4], raw[:, u % 8 // 2, u % 2], w_hi[:, u % 4].bitcast(F32), ALU.subtract).then_inc(lo_done, 1)

            def lo_loop(i, per, u0, r):
                dve.wait_ge(hi_done, i * per + (u0 + r + 1))
                TTT(w_lo[:, r % 4], raw[:, (r % 8) // 2, r % 2], w_hi[:, r % 4].bitcast(F32), ALU.subtract).then_inc(lo_done, 1)

            def turn_rest(t, j, bank, gain, dhi=a_hi, dlo=a_lo):
                dve.wait_ge(turn_hi[t], j + 1)
                src = ps[bank][:]
                if gain is None:
                    ins = TTT(dlo[:, 2 * j:2 * j + 2, :], src.rearrange("p (a b) -> p a b", a=2),
                              dhi[:, 2 * j:2 * j + 2, :].bitcast(F32), ALU.subtract)
                else:
                    for kk in range(2):
                        k = 2 * j + kk
                        ins = STT(dlo[:, k, :], src[:, kk * TOK:(kk + 1) * TOK], gains[:, gain, k:k + 1],
                                  dhi[:, k, :].bitcast(F32), ALU.mult, ALU.subtract)
                ins.then_inc(turn_out[t], 1)

            def split_low(t, j, src, gain, dhi, dlo):
                dve.wait_ge(turn_hi[t], j + 1)
                for k in (2 * j, 2 * j + 1):
                    ins = STT(dlo[:, k, :], src[:, k, :], gains[:, gain, k:k + 1], dhi[:, k, :].bitcast(F32), ALU.mult, ALU.subtract)
                ins.then_inc(turn_out[t], 1)

            def reciprocal_rms(n):
                dve.wait_ge(sums, n + 1)
                dve.reciprocal(rs[:, 2 * n:2 * n + 2], rs[:, 2 * n:2 * n + 2]).then_inc(rstds, 1)

            def spread(v, n):
                return v.unsqueeze(2).to_broadcast([P, v.shape[1], n])

            for u in range(LEAD):
                if u < 2:
                    split_low("x", u, xT, 0, a_hi, a_lo)
                lo(u)
            zv = z[:, :, ZV:ZV + 1024]

            def group_squares(n, src, out_, width):
                m = n % 2
                rows = sq[:, 1024 * m:1024 * (m + 1)]
                if n < 2:
                    st_.run(TTT(rows, src[:, m], src[:, m], ALU.mult))
                else:
                    ins = dve.tensor_reduce(out_[:, m], rows.rearrange("p (g c) -> p g c", c=width), AX.X, ALU.add)
                    if m == 0:
                        st_.run(ins)
                    else:
                        ins.then_inc(grp_sq, 1)

            for b in range(N_IN):
                for r in range(BLK):
                    lo(U_IN + b * BLK + r + LEAD)
                    if b == 0 and r % 2 == 0 and 2 <= r <= 12:
                        split_low("x", r // 2 + 1, xT, 0, a_hi, a_lo)
                    if b == 1 and r == 5:
                        reciprocal_rms(0)
                    if b == 2 and r % 2:
                        split_low("mem", r // 2, memT, 1, m_hi, m_lo)
                    if b == 5 and r == 4:
                        reciprocal_rms(1)
                    if b == 3 and r == 11:
                        for c in range(2):
                            dve.tensor_tensor_reduce(lamv[:, 2 * c], lamv[:, 2 * c], lamv[:, 2 * c + 1], 1.0, 0.0,
                                                     ALU.mult, ALU.add, lam[:, c:c + 1]).then_inc(lam_sum, 1)
                        st_.run(TS(subg[:], subg[:], 1.0 - LAM_INIT, None, ALU.mult))
                    if b == 4 and r in (2, 4, 6, 8):
                        if r == 2:
                            dve.wait_ge(evac, 4)
                            dve.wait_ge(toep_out, 16)
                        group_squares(r // 2 - 1, zv, st[:, 0, 0:16].rearrange("p (m g) -> p m g", m=TT), SGU_D)
                    if b == 5 and r == 3:
                        dve.wait_ge(grp_root, 1)
                        st_.run(dve.reciprocal(st[:, 0, 0:16], st[:, 0, 0:16]))
                    if b == 5 and r in (5, 9):
                        m = r // 8
                        v = zv[:, m].rearrange("p (g c) -> p g c", c=SGU_D)
                        st_.run(TTT(v, v, spread(st[:, 0, 8 * m:8 * m + 8], SGU_D), ALU.mult))
                    if b == 5 and r in (7, 11):
                        m = r // 8
                        dve.wait_ge(sgg_in, 16)
                        TTT(zv[:, m], zv[:, m], sgg, ALU.mult).then_inc(vn_ready, 1)
                    if b in (6, 8) and r in (2, 4, 6, 8):
                        n = (b - 6) // 2
                        if r == 2:
                            dve.wait_ge(evac, b)
                        group_squares(r // 2 - 1, z[:, :, ZQ + 1024 * n:ZQ + 1024 * (n + 1)], stg[:, :, 16 * n:16 * n + 16], DIFF_D)
                    if b in (7, 9) and r == 3:
                        n = (b - 7) // 2
                        dve.wait_ge(grp_root, 2 + n)
                        st_.run(dve.reciprocal(stg[:, :, 16 * n:16 * n + 16], stg[:, :, 16 * n:16 * n + 16]))
                    if b == 7 and 4 <= r < 12:
                        n = (r - 4) // 2
                        dve.wait_ge(sgu_ps, n + 1)
                        for hh in (0, 1) if r % 2 == 0 else (2, 3):
                            m, h = n // 2, 4 * (n % 2) + hh
                            u_ = z[:, m, ZU + h * SGU_D:ZU + (h + 1) * SGU_D]
                            ins = STT(u_, ps[4 + n][:, hh * P:(hh + 1) * P], sgb[:, h:h + 1], u_, ALU.add, ALU.mult)
                        if r == 11:
                            ins.then_inc(sgu_out, 1)
                    if b == 9 and r == 5:
                        dve.wait_ge(lam_exp, 1)
                        st_.run(TS(lam[:, 5:6], lam[:, 3:4], LAM_INIT, None, ALU.subtract))
                        st_.run(TTT(lam[:, 4:5], lam[:, 5:6], lam[:, 2:3], ALU.subtract))
            n0 = st_.n

            def head(i, odd):
                h = i * 2 + odd
                st_.n = i * 20 + (10 * odd + n0)
                for t in range(2):
                    src = z[:, :, ds(h * P + (ZQ + 1024 * t), P)].rearrange("p m (c d) -> p m c d", c=2)
                    ins = TTT(qk_st[:, 2 * t:2 * t + 2, :].rearrange("p m (c d) -> p m c d", c=2), src,
                              stg[:, :, ds(h * 2 + 16 * t, 2)].unsqueeze(3).to_broadcast([P, TT, 2, DIFF_D]), ALU.mult)
                ins.then_inc(qk_scaled, 1)
                for r in range(BLK):
                    lo_loop(i, 2 * BLK, U_CKV, odd * BLK + r + LEAD)
                    if r == 3:
                        for qt in range(TT):
                            kn = P * (qt + 1)
                            dve.wait_ge(score_ps, i * 4 + (2 * odd + qt + 1))
                            st_.run(STT(logit[:, qt, :, 0:kn], ps[5 + qt][:, 0:2 * kn].rearrange("p (c k) -> p c k", c=2),
                                        DIFF_D ** -0.5, bias[:, ds(h, 1), TOK - kn:TOK].to_broadcast([P, 2, kn]),
                                        ALU.mult, ALU.add))
                            dve.tensor_reduce(sm[:, 0, 2 * qt:2 * qt + 2], logit[:, qt, :, 0:kn], AX.X, ALU.max,
                                              negate=True).then_inc(logit_ready, 1)
                    if r == 6:
                        for qt in range(TT):
                            kn = P * (qt + 1)
                            s_ = sm[:, 1, 2 * qt:2 * qt + 2]
                            dve.wait_ge(prob_ready, i * 4 + (2 * odd + qt + 1))
                            st_.run(dve.reciprocal(s_, s_))
                            st_.done(TTT(s_[:, 1:2], s_[:, 1:2], lam[:, 4:5], ALU.mult))
                            st_.run(TS(logit[:, qt, 0, 0:kn], logit[:, qt, 0, 0:kn], s_[:, 0:1], None, ALU.mult))
                            STT(logit[:, qt, 0, 0:kn], logit[:, qt, 1, 0:kn], s_[:, 1:2], logit[:, qt, 0, 0:kn],
                                ALU.mult, ALU.add).then_inc(a_ready, 1)
                    if r == 12:
                        dve.wait_ge(o_rms, h + 1)
                        st_.run(dve.reciprocal(sm[:, 1, 8:10], sm[:, 1, 8:10]))
                        st_.run(TTT(o_st, ps[5][:, 0:TOK].rearrange("p (m d) -> p m d", m=TT), spread(sm[:, 1, 8:10], DIFF_V), ALU.mult))
                        TTT(o_st, o_st, subg[:].unsqueeze(1).to_broadcast([P, TT, DIFF_V]), ALU.mult).then_inc(o_ready, 1)
                    if r == 15:
                        dve.wait_ge(turn_hi["mix"], h + 1)
                        TTT(mix_chunks(a_lo, h), ps[7][:].rearrange("p (a b) -> p a b", a=2), mix_chunks(a_hi, h).bitcast(F32),
                            ALU.subtract).then_inc(turn_out["mix"], 1)

            dve.wait_ge(evac, N_IN - 2)
            dve.wait_ge(masked, 2)
            with dve.Fori(0, DIFF_H // 2) as i:
                for odd in range(2):
                    head(i, odd)
            st_.n = n0 + 10 * DIFF_H

            def add_block(u_end, b):
                dve.wait_ge(used, u_end)
                for m in range(TT):
                    v = xh[:, m, b * NB:(b + 1) * NB]
                    ins = TTT(v, ps[2 * (b % 2) + m][:], v, ALU.add)
                ins.then_inc(added, 1)

            def cross(h, r):
                n = slice(2 * h, 2 * h + 2)
                if r == 4:
                    dve.wait_ge(x_rms, h + 1)
                    st_.run(dve.reciprocal(sm[:, 2, n], sm[:, 2, n]))
                    st_.run(TS(sm[:, 2, n], sm[:, 2, n], CROSS_D ** -0.5, None, ALU.mult))
                    dve.wait_ge(x_score, h + 1)
                    st_.run(dve.tensor_reduce(sm[:, 0, n], ps[6][:].rearrange("p (t k) -> p t k", t=2), AX.X, ALU.max, negate=True))
                    TTT(sm[:, 0, n], sm[:, 0, n], sm[:, 2, n], ALU.mult).then_inc(x_max, 1)
                if r == 6:
                    dve.wait_ge(x_prob, h + 1)
                    st_.run(dve.reciprocal(sm[:, 1, n], sm[:, 1, n]))
                    for qt in range(TT):
                        ins = TS(cp[:, h % 2, qt], cp[:, h % 2, qt], sm[:, 1, 2 * h + qt:2 * h + qt + 1], None, ALU.mult)
                    ins.then_inc(x_norm, 1)
                if r == 11:
                    for g in range(2):
                        turn_rest("oc", 2 * h + g, 4 + g, None)

            for b in range(N_OUT):
                for r in range(BLK):
                    lo(U_OUT + b * BLK + r + LEAD)
                    if b and r in (3, 5):
                        turn_rest("h1", 2 * (b - 1) + r // 4, 6 + r // 4, 2, m_hi, m_lo)
                    if b == 0 and r == 1:
                        dve.wait_ge(evac, N_IN + N_CKV)
                    if b == 0 and r in (2, 8):
                        m = r // 8
                        st_.run(TTT(sq, kv[:, m, 0:D], kv[:, m, 0:D], ALU.mult))
                    if b == 0 and r in (5, 11):
                        m = r // 8
                        ins = dve.tensor_reduce(st[:, 0, 4 * m:4 * m + 4], sq.rearrange("p (h c) -> p h c", c=CROSS_D), AX.X, ALU.add)
                        if m == 0:
                            st_.run(ins)
                        else:
                            ins.then_inc(grp_sq, 1)
                    if b == 1 and r == 2:
                        dve.wait_ge(grp_root, 4)
                        st_.run(dve.reciprocal(st[:, 0, 0:8], st[:, 0, 0:8]))
                    if b == 1 and r in (8, 11):
                        m = (r - 8) // 3
                        v = kv[:, m, 0:D].rearrange("p (h c) -> p h c", c=CROSS_D)
                        TTT(v, v, spread(st[:, 0, 4 * m:4 * m + 4], CROSS_D), ALU.mult).then_inc(kc_ready, 1)
                add_block(U_OUT + (b + 1) * BLK, b)
            for b in range(N_CQ):
                for r in range(BLK):
                    lo(U_CQ + b * BLK + r + LEAD)
                    if b == 0:
                        if r in (3, 5):
                            turn_rest("h1", 6 + r // 4, 6 + r // 4, 2, m_hi, m_lo)
                        if r == 13:
                            reciprocal_rms(2)
                    else:
                        cross(b - 1, r)
            for b in range(N_CO):
                for r in range(BLK):
                    lo(U_CO + b * BLK + r + LEAD)
                    if b == 0:
                        cross(CROSS_H - 1, r)
                    elif r in (3, 5):
                        turn_rest("h2", 2 * (b - 1) + r // 4, 6 + r // 4, 3, m_hi, m_lo)
                add_block(U_CO + (b + 1) * BLK, b)

            def top8_two(n, sets, ready):
                part = slice(8 * n, 8 * n + 8)
                maxima, left = [], []
                for k, (vals, top, idx) in enumerate(sets):
                    if ready:
                        st_.upto(ready[k])
                    maxima.append(st_.done(dve.max(top[:, part], vals)))
                for k, (vals, top, idx) in enumerate(sets):
                    st_.upto(maxima[k])
                    left.append(st_.done(dve.max_index(idx[:, part], top[:, part], vals)))
                if n == 0:
                    for k, (vals, top, idx) in enumerate(sets):
                        st_.upto(left[k])
                        left[k] = st_.done(dve.match_replace(vals, top[:, part], vals, LOW))
                return left

            left = [None]

            def pick_keys(part):
                b, n = part // 8, part % 8
                m = n // 4
                if n % 4 == 0:
                    dve.wait_ge(sc_out, 2 * b + m + 1)
                hcs = [4 * b + 2 * (n // 2 % 2) + k for k in range(2)]
                left[0] = top8_two(n % 2, [(sc[:, m, hc], pk_top[:, m, hc], pk_idx[:, m, hc]) for hc in hcs],
                                   left[0] if n % 2 else None)

            for b in range(N_PQ):
                for r in range(BLK):
                    lo(U_PQ + b * BLK + r + LEAD)
                    if b == 0:
                        if r in (3, 5):
                            turn_rest("h2", 6 + r // 4, 6 + r // 4, 3, m_hi, m_lo)
                        if r == 13:
                            reciprocal_rms(3)
                            dve.wait_ge(rstds, 4)
                    if b == 0 and r >= 14 or b == 1 and r < 2:
                        c = slice(NB * ((r + 2) % BLK), NB * ((r + 2) % BLK + 1))
                        for m in range(TT):
                            ins = TS(xn[:, m, c], xh[:, m, c], rs[:, 6 + m:7 + m], None, ALU.mult)
                        ins.then_inc(xn_ready, 1)
                    if b == 1 and r % 2:
                        turn_rest("h2n", r // 2, 6 + r // 2 % 2, 3)
                    if b == 1 and r == 6:
                        dve.wait_ge(h_saved, 16)
                    if b == 1 and r in (6, 10, 14):
                        pick_keys(r // 4 - 1)
                    if b >= 2 and r % 2 == 0:
                        pick_keys(EARLY + 8 * (b - 2) + r // 2)

            last_plain = U_U[0] + 8 * (PLAIN - 1)
            nxt, debt = [U_U[0]], [0]

            def stream_to(u):
                while nxt[0] <= u:
                    lo(nxt[0] + LEAD)
                    nxt[0] += 1

            def beside(columns, instructions=1):
                debt[0] += columns + 80 * instructions
                while debt[0] >= FREE:
                    debt[0] -= FREE
                    if nxt[0] < last_plain:
                        stream_to(nxt[0])

            for part in range(EARLY + 16, 8 * N_PQ):
                pick_keys(part)
                beside((6 - 2 * (part % 2)) * NK, 6 - 2 * (part % 2))
            for m in range(TT):
                st_.settle()
                st_.run(dve.tensor_copy(pk_idxf[:, m], pk_idx[:, m]))
                tv = pk_top[:, m].rearrange("p (h c) k -> p h c k", c=2)
                fi = pk_idxf[:, m].rearrange("p (h c) k -> p h c k", c=2)
                shape = [P, PH, TOPK, TOPK]
                st_.run(TTT(cand, tv[:, :, 0].unsqueeze(3).to_broadcast(shape), tv[:, :, 1].unsqueeze(2).to_broadcast(shape), ALU.add))
                beside(2048)
                top, pos = pk(1536, m), pk(1792, m).bitcast(U32)
                for h in range(0, PH, 2):
                    sets = [(cand[:, hh].rearrange("p a b -> p (a b)"), top[:, hh * TOPK:(hh + 1) * TOPK],
                             pos[:, hh * TOPK:(hh + 1) * TOPK]) for hh in (h, h + 1)]
                    steps = top8_two(0, sets, None)
                    beside(6 * 256, 6)
                    top8_two(1, sets, steps)
                    beside(4 * 256, 4)
                st_.settle()
                st_.done(TS(pk(2048, m).bitcast(U32), pos, 4, None, ALU.logical_shift_right))
                st_.run(TS(pk(2304, m).bitcast(U32), pos, 15, None, ALU.bitwise_and))
                for c in range(2):
                    st_.run(dve.tensor_copy(pk(2560, m), pk(2048 + 256 * c, m).bitcast(U32)))
                    place = pk(2560, m).rearrange("p (h k) -> p h k", h=PH)
                    st_.run(TTT(eq, iota[:, 0:TOPK].unsqueeze(1).unsqueeze(1).to_broadcast(shape),
                                place.unsqueeze(3).to_broadcast(shape), ALU.is_equal))
                    beside(2048)
                    st_.run(TTT(eq, eq, fi[:, :, c].unsqueeze(2).to_broadcast(shape), ALU.mult))
                    beside(2048)
                    st_.run(dve.tensor_reduce(pk(2816 + 256 * c, m).rearrange("p (h k) -> p h k", h=PH), eq, AX.X, ALU.add))
                    beside(2048)
                top = pk(1536, m).rearrange("p (h k) -> p h k", h=PH)
                gate = pk_gate(m).rearrange("p (h k) -> p h k", h=PH)
                TTT(gate, top, top[:, :, 0:1].to_broadcast([P, PH, TOPK]), ALU.subtract).then_inc(gate_in, 1)
            stream_to(last_plain + 1)
            for m in range(TT):
                gate = pk_gate(m).rearrange("p (h k) -> p h k", h=PH)
                dve.wait_ge(gate_exp, m + 1)
                st_.run(dve.tensor_reduce(sm[:, m, 0:PH], gate, AX.X, ALU.add))
                st_.run(dve.reciprocal(sm[:, m, 0:PH], sm[:, m, 0:PH]))
                TTT(gate, gate, spread(sm[:, m, 0:PH], TOPK), ALU.mult).then_inc(picks_ready, 1)
            stream_to(last_plain + 7)
            dve.wait_ge(gate_ps, HOT)
            for n in range(3):
                st_.done(dve.tensor_copy(pickT[:, n], ps[4 + n][:, 0:TOK]))
            st_.settle()

            def hot_rows(i, tk):
                s = tk % HOT
                dve.wait_ge(gate_ps, i * TPI + (tk + 1))
                col = ds(i * TPI + tk, 1)
                TS(hot1[:, s], iota[:], pickT[:, 0, col], pickT[:, 2, col], ALU.is_equal, ALU.mult)
                TS(hot2[:, s], iota[:], pickT[:, 1, col], None, ALU.is_equal).then_inc(hot_ready, 1)

            gates_by_key = ar(W, TOK, HALF).rearrange("p t j -> p j t")
            acts = ar(G, HALF, TOK)

            def product(half, j):
                v = acts[:, ds(j, 1), :]
                TTT(v, v, gates_by_key[:, ds(j, 1), :], ALU.mult).then_inc(coef, 1)

            def remainder(half, j, parity):
                dve.wait_ge(coef_hi, j + (half * HALF + 1))
                TTT(c_lo[:, parity:parity + 1], acts[:, ds(j, 1), :], c_hi[:, parity:parity + 1].bitcast(F32),
                    ALU.subtract).then_inc(coef_ready, 1)

            def add_sums(half, n):
                s, m = n // 2, n % 2
                if n == 0:
                    dve.wait_ge(res_in, 16 * (half + 1))
                dve.wait_ge(used, U_V[half] + 4 * (HALF - 1) + s + 1)
                v = res[:, m, s * NB:(s + 1) * NB]
                TTT(v, ps[4 * m + s][:], v, ALU.add).then_inc(acc_out, 1)

            for half in range(2):
                if half:
                    for r in range(8):
                        lo(U_U[1] + r + LEAD)
                        if r < 5:
                            add_sums(0, r + 3)
                    with dve.Fori(1, ITS - 1) as i:
                        for r in range(8):
                            lo_loop(i, 8, U_U[1], r + LEAD)
                else:
                    with dve.Fori(0, TOK // TPI) as i:
                        for r in range(8):
                            hot_rows(i, 2 * r)
                            hot_rows(i, 2 * r + 1)
                            lo_loop(i, 8, U_U[0] + 8 * PLAIN, r + LEAD)
                for r in range(8):
                    lo(U_U[half] + 8 * (ITS - 1) + r + LEAD)
                    if r == 3:
                        if half:
                            dve.wait_ge(gates_back, 16 * TOK // TPI)
                        else:
                            dve.wait_ge(gate_out, TOK // HOT)
                        dve.wait_ge(gelu_done, half * HALF + 1)
                        product(half, 0)
                    if r == 5:
                        remainder(half, 0, 0)
                dve.wait_ge(gelu_done, (half + 1) * HALF)
                with dve.Fori(0, ITS - 1) as i:
                    for r in range(8):
                        lo_loop(i, 8, U_V[half], r + LEAD)
                        if r % 4 == 0:
                            product(half, i * 2 + (1 + r // 4))
                        if r % 4 == 2:
                            remainder(half, i * 2 + (1 + r // 4), 1 - r // 4)
                for r in range(8):
                    lo(U_V[half] + 8 * (ITS - 1) + r + LEAD)
                    if r == 0:
                        product(half, HALF - 1)
                    if r == 2:
                        remainder(half, HALF - 1, 1)
                    if half == 0 and r >= 5:
                        add_sums(0, r - 5)
            for n in range(8):
                add_sums(1, n)

        @block.tensor
        def _(pe):
            def turn(t, j, bank, src):
                for kk in range(2):
                    for m in range(TT):
                        ins = pe.transpose(ps[bank][:, kk * TOK + m * P:kk * TOK + (m + 1) * P], src(m, 2 * j + kk), ident[:])
                ins.then_inc(turned[t], 1)

            def columns_of(v):
                return lambda m, k: v[:, m, k * P:(k + 1) * P]

            def chunk(k, r, bank, ahi, alo):
                for m in range(TT):
                    o, sh, sl = ps[bank + m][:], ahi[:, k, m * P:(m + 1) * P], alo[:, k, m * P:(m + 1) * P]
                    pe.matmul(o, sh, w_hi[:, r % 4], start=(k == 0), stop=False)
                    pe.matmul(o, sh, w_lo[:, r % 4], start=False, stop=False)
                    ins = pe.matmul(o, sl, w_hi[:, r % 4], start=False, stop=(k == KC - 1))
                ins.then_inc(used, 1)
                return ins

            def project(i, u0, per, r, bank, ahi=a_hi, alo=a_lo):
                pe.wait_ge(lo_done, i * per + (u0 + r + 1))
                chunk(r % BLK, r, bank, ahi, alo)

            def bias_rows(r):
                if r == 0:
                    pe.wait_ge(onehot_in, 32)
                    pe.matmul(ps[7][0:8, 0:SPITCH], relb, onehot, start=True, stop=True).then_inc(toep_ps, 1)

            def spatial_gating(r):
                if r % 2 == 0 and r >= 8:
                    n = (r - 8) // 2
                    if n == 0:
                        pe.wait_ge(masked, 1)
                        pe.wait_ge(toep_sb, 1)
                    pe.wait_ge(vn_ready, n // 2 + 1)
                    for hh in range(4):
                        m, h = n // 2, 4 * (n % 2) + hh
                        ins = pe.matmul(ps[4 + n][:, hh * P:(hh + 1) * P], wst[:, h], z[:, m, ZV + h * SGU_D:ZV + (h + 1) * SGU_D],
                                        start=True, stop=True)
                    ins.then_inc(sgu_ps, 1)

            def block(u0, b, ahi=a_hi, alo=a_lo, before=None, after=None):
                for r in range(BLK):
                    if before:
                        before(r)
                    project(0, u0 + b * BLK, BLK, r, 2 * (b % 2), ahi, alo)
                    if after:
                        after(r)

            def parts_of(t):
                def before(r):
                    if r % 2 == 0:
                        pe.wait_ge(turn_out[t], r // 2 + 1)
                return before

            beside = {1: bias_rows, 6: spatial_gating}
            for b in range(N_IN):
                if b >= 2:
                    pe.wait_ge(evac, b - 1)
                block(U_IN, b, before=parts_of("x") if b == 0 else None, after=beside.get(b))
            def head(i, odd):
                h = i * 2 + odd
                pe.wait_ge(evac, h + (N_IN - 1))
                for r in range(BLK):
                    pe.wait_ge(lo_done, i * (2 * BLK) + (U_CKV + odd * BLK + r + 1))
                    chunk(r, r, 2 * odd, m_hi, m_lo)
                    if r == 0:
                        pe.wait_ge(qk_scaled, h + 1)
                        for n in range(4):
                            ins = pe.transpose(ps[4][:, n * P:(n + 1) * P], qk_st[:, n], ident[:])
                        ins.then_inc(qk_turned, 1)
                    if r == 2:
                        pe.wait_ge(qk_ready, h + 1)
                        for qt in range(TT):
                            kn = P * (qt + 1)
                            for c in range(2):
                                ins = pe.matmul(ps[5 + qt][:, c * kn:(c + 1) * kn], qz[:, c, qt * P:(qt + 1) * P], kz[:, 0:kn],
                                                start=True, stop=True)
                            ins.then_inc(score_ps, 1)
                    if r == 8:
                        for qt in range(TT):
                            pe.wait_ge(a_ready, i * 4 + (2 * odd + qt + 1))
                            for kt in range(qt + 1):
                                ins = pe.transpose(ps[4][:, (qt + kt) * P:(qt + kt + 1) * P], logit[:, qt, 0, kt * P:(kt + 1) * P], ident[:])
                        ins.then_inc(aT_ps, 1)
                    if r == 10:
                        pe.wait_ge(aT_ready, h + 1)
                        for qt in range(TT):
                            for kt in range(qt + 1):
                                ins = pe.matmul(ps[5][:, qt * DIFF_V:(qt + 1) * DIFF_V], aT[:, qt + kt],
                                                z[:, kt, ds(h * DIFF_V + ZVD, DIFF_V)], start=(kt == 0), stop=(kt == qt))
                        ins.then_inc(o_ps, 1)
                    if r == 14:
                        pe.wait_ge(u_staged, h + 1)
                        pe.wait_ge(o_ready, h + 1)
                        for n in range(4):
                            ins = pe.transpose(ps[7][:, n * P:(n + 1) * P], (u_st if n < 2 else o_st)[:, n % 2], ident[:])
                        ins.then_inc(turned["mix"], 1)

            pe.wait_ge(turn_out["mem"], 8)
            pe.wait_ge(sgu_out, 1)
            with pe.Fori(0, DIFF_H // 2) as i:
                for odd in range(2):
                    head(i, odd)

            def last_head(r):
                pe.wait_ge(turn_out["mix"], DIFF_H if r % 8 == 7 else DIFF_H - 1)

            def residual_turn(t, b):
                def after(r):
                    if r in (2, 4):
                        j = 2 * (b - 1) + r // 4
                        if r == 2:
                            pe.wait_ge(added, (N_OUT if t == "h2" else 0) + b)
                        turn(t, j, 6 + r // 4, columns_of(xh))
                return after

            def keys_turn(r):
                residual_turn("h1", 2)(r)
                if r % 2 == 0:
                    j = r // 2
                    if j == 0:
                        pe.wait_ge(kc_ready, 2)
                    at_least(pe, turn_out["ck"], j - 1)
                    turn("ck", j, 4 + j % 2, columns_of(kv))

            pe.wait_ge(evac, N_IN + N_CKV - 1)
            block(U_OUT, 0, before=last_head)
            pe.wait_ge(evac, N_IN + N_CKV)
            block(U_OUT, 1, after=residual_turn("h1", 1))
            pe.wait_ge(added, 1)
            block(U_OUT, 2, after=keys_turn)
            pe.wait_ge(added, 2)
            block(U_OUT, 3, after=residual_turn("h1", 3))

            def cross(h):
                def after(r):
                    if r == 0:
                        pe.wait_ge(evac, N_IN + N_CKV + h + 1)
                        for g in range(2):
                            turn("cq", 2 * h + g, 4 + g, columns_of(cq))
                    if r == 2:
                        pe.wait_ge(turn_out["cq"], 2 * h + 2)
                        pe.wait_ge(turn_out["ck"], 8)
                        for qt in range(TT):
                            for c in range(CH):
                                ins = pe.matmul(ps[6][:, qt * TOK:(qt + 1) * TOK], qT[h % 2][:, c, qt * P:(qt + 1) * P],
                                                kT[:, h * CH + c, :], start=(c == 0), stop=(c == CH - 1))
                        ins.then_inc(x_score, 1)
                    if r == 8:
                        pe.wait_ge(x_norm, h + 1)
                        for qt in range(TT):
                            for mt in range(TT):
                                n = 2 * mt + qt
                                ins = pe.transpose(ps[7][:, n * P:(n + 1) * P], cp[:, h % 2, qt, mt * P:(mt + 1) * P], ident[:])
                        ins.then_inc(x_pT, 1)
                    if r == 10:
                        pe.wait_ge(x_pT_out, h + 1)
                        for g in range(2):
                            for c in (2 * g, 2 * g + 1):
                                for mt in range(TT):
                                    v = kv[:, mt, D + h * CROSS_D + c * P:D + h * CROSS_D + (c + 1) * P]
                                    ins = pe.matmul(ps[4 + g][:, c % 2 * TOK:(c % 2 + 1) * TOK], v,
                                                    cpT[:, h % 2, 2 * mt:2 * mt + 2].rearrange("p n q -> p (n q)"),
                                                    start=(mt == 0), stop=(mt == 1))
                            ins.then_inc(turned["oc"], 1)
                return after

            pe.wait_ge(added, 3)
            block(U_CQ, 0, m_hi, m_lo, before=parts_of("h1"), after=residual_turn("h1", 4))
            for b in range(1, N_CQ):
                if b >= 2:
                    pe.wait_ge(evac, N_IN + N_CKV + b - 1)
                block(U_CQ, b, m_hi, m_lo, after=cross(b - 1))
            pe.wait_ge(evac, N_IN + N_CKV + 3)
            block(U_CO, 0, before=parts_of("oc"), after=cross(CROSS_H - 1))
            for b in range(1, N_CO):
                if b >= 2:
                    pe.wait_ge(added, N_OUT + b - 1)
                block(U_CO, b, after=residual_turn("h2", b))

            def query_block(b, before=None, after=None):
                for r in range(BLK):
                    if before:
                        before(r)
                    pe.wait_ge(lo_done, U_PQ + b * BLK + r + 1)
                    for c in range(4):
                        o = ps[2 * (b % 2) + c // 2][:, c % 2 * TOK:(c % 2 + 1) * TOK]
                        wh, wl = w_hi[:, r % 4, c * P:(c + 1) * P], w_lo[:, r % 4, c * P:(c + 1) * P]
                        pe.matmul(o, wh, m_hi[:, r], start=(r == 0 and c % 2 == 0), stop=False)
                        pe.matmul(o, wh, m_lo[:, r], start=False, stop=False)
                        ins = pe.matmul(o, wl, m_hi[:, r], start=False, stop=(r == KC - 1 and c % 2 == 1))
                    ins.then_inc(used, 1)
                    if after:
                        after(r)

            def peer_queries(b, r):
                if r == 2:
                    pe.wait_ge(evac, N_IN + N_CKV + N_CQ + b + 1)
                    pe.wait_ge(keys_in, 16)
                    for m in range(TT):
                        for a in range(4):
                            hc = 4 * b + a
                            ins = pe.matmul(ps[4 + m][:, a * NK:(a + 1) * NK], pqT[:, hc, m * P:(m + 1) * P], keysT[:, hc],
                                            start=True, stop=True)
                        ins.then_inc(sc_ps, 1)

            def queries_and_turn(r):
                peer_queries(0, r)
                if r % 2 == 0:
                    j = r // 2
                    pe.wait_ge(xn_ready, j // 2 + 1)
                    at_least(pe, turn_out["h2n"], j - 1)
                    turn("h2n", j, 6 + j % 2, columns_of(xn))

            pe.wait_ge(added, N_OUT + 3)
            query_block(0, before=parts_of("h2"), after=residual_turn("h2", 4))
            query_block(1, after=queries_and_turn)
            for b in (2, 3):
                pe.wait_ge(evac, N_IN + N_CKV + N_CQ + b - 1)
                query_block(b, after=lambda r: peer_queries(b - 1, r))
            pe.wait_ge(turn_out["h2n"], 8)
            pe.wait_ge(evac, N_IN + N_CKV + N_CQ + 3)

            def activations(i, half, it0, tokens, after=None):
                for r in range(8):
                    jl = r // 4
                    if r % 4 == 0:
                        at_least(pe, gelu_done, i * 2 + (half * HALF + 2 * it0 + jl - 1))
                    pe.wait_ge(lo_done, i * 8 + (U_U[half] + 8 * it0 + r + 1))
                    for dd in range(4):
                        k = 4 * (r % 4) + dd
                        o, uh, ul = ps[jl][:, 0:TOK], w_hi[:, r % 4, dd * P:(dd + 1) * P], w_lo[:, r % 4, dd * P:(dd + 1) * P]
                        pe.matmul(o, uh, a_hi[:, k], start=(k == 0), stop=False)
                        pe.matmul(o, uh, a_lo[:, k], start=False, stop=False)
                        ins = pe.matmul(o, ul, a_hi[:, k], start=False, stop=(k == KC - 1))
                    ins.then_inc(used, 1)
                    if after:
                        after(r)
                    for n in range(tokens // 8):
                        tk = r * (tokens // 8) + n
                        if tk % HOT == 0:
                            at_least(pe, gate_out, i * 4 + (tk // HOT - 3))
                        pe.wait_ge(hot_ready, i * TPI + (tk + 1))
                        pe.matmul(ps[2 + tk // HOT][:, (tk % HOT) * NK:(tk % HOT + 1) * NK], hot1[:, tk % HOT], hot2[:, tk % HOT],
                                  start=True, stop=True).then_inc(gate_ps, 1)

            def outputs(i, half, first, last):
                for r in range(8):
                    j, s = r // 4, r % 4
                    if s == 0:
                        pe.wait_ge(coef_ready, i * 2 + (half * HALF + j + 1))
                    pe.wait_ge(lo_done, i * 8 + (U_V[half] + r + 1))
                    if first and r < 2:
                        pe.wait_ge(gelu_done, (half + 1) * HALF - 1 + r)
                    for m in range(TT):
                        o, sh, sl = ps[4 * m + s][:], c_hi[:, j, m * P:(m + 1) * P], c_lo[:, j, m * P:(m + 1) * P]
                        pe.matmul(o, sh, w_hi[:, r % 4], start=first and j == 0, stop=False)
                        pe.matmul(o, sh, w_lo[:, r % 4], start=False, stop=False)
                        ins = pe.matmul(o, sl, w_hi[:, r % 4], start=False, stop=last and j == 1)
                    ins.then_inc(used, 1)

            def turn_picks(r):
                if r == 6:
                    pe.wait_ge(picks_ready, 2)
                    for n, col in enumerate((2816, 3072, 3328)):
                        for m in range(TT):
                            ins = pe.transpose(ps[4 + n][:, m * P:(m + 1) * P], pk(col, m), ident[:])
                    ins.then_inc(gate_ps, HOT)

            for half in range(2):
                if half == 0:
                    activations(0, 0, 0, 0, after=lambda r: peer_queries(N_PQ - 1, r))
                    with pe.Fori(1, PLAIN - 1) as i:
                        activations(i, 0, 0, 0)
                    activations(PLAIN - 1, 0, 0, 0, after=turn_picks)
                    activations(0, 0, PLAIN, TPI)
                    with pe.Fori(1, TOK // TPI) as i:
                        activations(i, 0, PLAIN, TPI)
                else:
                    pe.wait_ge(acc_out, 1)
                    activations(0, 1, 0, 0, after=lambda r: pe.wait_ge(acc_out, 3) if r == 3 else None)
                    with pe.Fori(1, ITS - 1) as i:
                        activations(i, 1, 0, 0)
                    pe.wait_ge(acc_out, 8)
                activations(ITS - 1, half, 0, 0)
                outputs(0, half, True, False)
                with pe.Fori(1, ITS - 1) as i:
                    outputs(i, half, False, False)
                outputs(ITS - 1, half, False, True)


def kernel(**inputs):
    import numpy as np
    import concourse.bacc as bacc
    from concourse import mybir as _mybir
    from concourse.bass_utils import run_bass_kernel_spmd

    a = {k: np.asarray(v) for k, v in inputs.items()}

    def projection(w):
        n = w.shape[1]
        return w.reshape(KC // 2, 2, P, n // NB, NB).transpose(3, 0, 2, 1, 4).reshape(-1, P, 2 * NB)

    def chunks(x):
        return x.T.reshape(KC, P, TOK).transpose(1, 0, 2)

    def columns(g):
        return g.reshape(-1, P).T

    dist = np.maximum(2 * P - 1 - np.arange(SPITCH), 0)
    exact = 16
    large = exact + (np.log(np.maximum(dist, 1).astype(np.float32) / exact) / np.float32(np.log(128 / exact)) * (32 - exact)).astype(np.int32)
    bucket = np.where(dist < exact, dist, np.minimum(large, 31))
    onehot = (np.arange(32)[:, None] == bucket[None, :]).astype(np.float32)

    arrays = {
        "x": a["x"][0], "mem": a["mem"][0], "x_cols": chunks(a["x"][0]), "mem_cols": chunks(a["mem"][0]),
        "w_in": projection(a["w_in"][0]), "w_ckv": projection(a["w_ckv"][0]), "w_out": projection(a["w_out"][0]),
        "w_cq": projection(a["w_cq"][0]), "w_co": projection(a["w_co"][0]), "peer_wq": projection(a["peer_wq"][0]),
        "peer_u": a["peer_u"][0].reshape(NK, NK, 2, 8, P).transpose(1, 2, 4, 3, 0).reshape(2 * NK, P, 8 * NK),
        "peer_v": a["peer_v"][0].reshape(NK, NK, 2, 1024).transpose(1, 2, 0, 3).reshape(2 * NK, NK, 1024),
        "peer_keys": a["peer_keys"][0].reshape(2 * PH, NK, P).transpose(2, 0, 1),
        "mix_g": columns(a["norm_mix_g"][0]), "mem_g": columns(a["norm_mem_g"][0]),
        "cross_g": columns(a["norm_cross_g"][0]), "ffn_g": columns(a["norm_ffn_g"][0]),
        "sgu_g": a["sgu_norm_g"][0].reshape(-1), "sgu_w": a["sgu_w"][0].transpose(2, 0, 1), "sgu_b": a["sgu_b"][0].T,
        "q_g": a["q_norm_g"][0][:, None], "k_g": a["k_norm_g"][0][:, None],
        "lambdas": np.stack([a[n][0] for n in ("lambda_q1", "lambda_k1", "lambda_q2", "lambda_k2")]),
        "subln_g": a["diff_subln_g"][0], "rel_bias": a["rel_bias"], "bucket_of": onehot,
        "cq_g": columns(a["cq_norm_g"][0]), "ck_g": columns(a["ck_norm_g"][0]),
    }
    arrays = {f"in_{k}": np.ascontiguousarray(v) for k, v in arrays.items()}
    nc = bacc.Bacc("TRN2", target_bir_lowering=False, num_devices=1)
    args = {k[3:]: nc.dram_tensor(k, v.shape, _mybir.dt.from_np(v.dtype), kind="ExternalInput").ap() for k, v in arrays.items()}
    out = nc.dram_tensor("out", (TOK, D), _mybir.dt.float32, kind="ExternalOutput").ap()
    hybrid_layer(nc, out=out, **args)
    r = run_bass_kernel_spmd(nc, [arrays], core_ids=[0])
    return r.results[0]["out"].reshape(1, TOK, D)
```
